# Optimizing a Trainium2 kernel written in Bass

```python
import math
import numpy as np
import jax, jax.numpy as jnp
from jax import lax

D_MODEL = 1024
BATCH = 1
SEQ = 256
DEPTH = 2

D_MIX = D_MODEL
RG_WIDTH = D_MIX // 2
RG_BLOCKS = 8
RG_BLOCK = RG_WIDTH // RG_BLOCKS
CONV_W = 4
RG_C = 8.0
A_MIN = 0.9
A_MAX = 0.999

NSA_WIDTH = D_MIX - RG_WIDTH
HEAD_DIM = 64
N_HEADS = NSA_WIDTH // HEAD_DIM
N_KV = 2
HPG = N_HEADS // N_KV
KV_WIDTH = N_KV * HEAD_DIM
ROPE_DIM = HEAD_DIM // 4
ROPE_THETA = 500000.0
CMP_LEN = 32
CMP_STRIDE = 16
CMP_HIDDEN = 2 * HEAD_DIM
SEL_LEN = 64
SEL_TOPN = 16
WINDOW = 512
N_BRANCH = 3
Q_BLOCK = 128
EPS = 1e-6
NEG = -1e30
BIG = 1e30
N_IN = 2 * RG_WIDTH + 2 * NSA_WIDTH + 6 * KV_WIDTH + N_BRANCH * N_HEADS


def rms_norm(x, g):
    xf = x.astype(jnp.float32)
    y = xf * lax.rsqrt(jnp.mean(xf * xf, axis=-1, keepdims=True) + EPS)
    return (y * g.astype(jnp.float32)).astype(x.dtype)

def rope_partial(x, pos):
    half = ROPE_DIM // 2
    inv = ROPE_THETA ** (-jnp.arange(half, dtype=jnp.float32) / half)
    ang = pos[:, None] * inv[None, :]
    cos, sin = jnp.cos(ang), jnp.sin(ang)
    xf = x.astype(jnp.float32)
    x1, x2, xp = xf[..., :half], xf[..., half:ROPE_DIM], xf[..., ROPE_DIM:]
    out = jnp.concatenate([x1 * cos - x2 * sin, x2 * cos + x1 * sin, xp], axis=-1)
    return out.astype(x.dtype)

def masked_softmax(s, mask):
    s = jnp.where(mask, s.astype(jnp.float32), NEG)
    return jax.nn.softmax(s, axis=-1) * mask

def causal_depthwise_conv(x, w, b):
    S = x.shape[1]
    xp = jnp.pad(x, ((0, 0), (CONV_W - 1, 0), (0, 0)))
    y = sum(xp[:, k:k + S] * w[k] for k in range(CONV_W))
    return y + b

def rg_lru(x, w_r, b_r, w_i, b_i, lam):
    B, S, C = x.shape
    xb = x.reshape(B, S, RG_BLOCKS, RG_BLOCK)
    r = jax.nn.sigmoid(jnp.einsum('bsnc,ncd->bsnd', xb, w_r).reshape(B, S, C) + b_r)
    i = jax.nn.sigmoid(jnp.einsum('bsnc,ncd->bsnd', xb, w_i).reshape(B, S, C) + b_i)
    log_a = (-RG_C * r.astype(jnp.float32)) * jax.nn.softplus(-lam.astype(jnp.float32))
    a = jnp.exp(log_a)
    u = jnp.sqrt(-jnp.expm1(2.0 * log_a)) * (i * x).astype(jnp.float32)

    def combine(left, right):
        a1, b1 = left
        a2, b2 = right
        return a1 * a2, a2 * b1 + b2

    _, h = lax.associative_scan(combine, (a, u), axis=1)
    return h.astype(x.dtype)

def compress_blocks(blocks, pe, w1, w2):
    z = (blocks + pe).reshape(blocks.shape[:-2] + (CMP_LEN * HEAD_DIM,))
    return jax.nn.silu(z @ w1) @ w2

def nsa(q, k_c, v_c, k_s, v_s, k_w, v_w, gates, q_g, k_g,
        pe_k, w1_k, w2_k, pe_v, w1_v, w2_v):
    B, S, _ = q.shape
    pos = jnp.arange(S, dtype=jnp.float32)
    scale = 1.0 / math.sqrt(HEAD_DIM)
    n_cmp = (S - CMP_LEN) // CMP_STRIDE + 1
    n_sel = S // SEL_LEN
    top_n = min(SEL_TOPN, n_sel)
    n_qb = S // Q_BLOCK

    def kv_heads(t):
        return t.reshape(B, S, N_KV, HEAD_DIM).transpose(0, 2, 1, 3)

    qh = q.reshape(B, S, N_KV, HPG, HEAD_DIM).transpose(0, 2, 3, 1, 4)
    qh = rope_partial(rms_norm(qh, q_g), pos)

    blk_idx = np.arange(n_cmp)[:, None] * CMP_STRIDE + np.arange(CMP_LEN)[None, :]
    kc = compress_blocks(kv_heads(k_c)[:, :, blk_idx], pe_k, w1_k, w2_k)
    vc = compress_blocks(kv_heads(v_c)[:, :, blk_idx], pe_v, w1_v, w2_v)
    cmp_end = jnp.arange(n_cmp) * CMP_STRIDE + (CMP_LEN - 1)
    kc = rope_partial(rms_norm(kc, k_g[0]), cmp_end.astype(jnp.float32))

    cs = np.arange(n_cmp)[:, None] * CMP_STRIDE
    ss = np.arange(n_sel)[None, :] * SEL_LEN
    ov = np.maximum(0, np.minimum(cs + CMP_LEN, ss + SEL_LEN) - np.maximum(cs, ss))
    overlap = jnp.asarray((ov / CMP_LEN).astype(np.float32))

    ks = rope_partial(rms_norm(kv_heads(k_s), k_g[1]), pos)
    ks_blk = ks.reshape(B, N_KV, n_sel, SEL_LEN * HEAD_DIM)
    vs_blk = kv_heads(v_s).reshape(B, N_KV, n_sel, SEL_LEN * HEAD_DIM)

    kw = rope_partial(rms_norm(kv_heads(k_w), k_g[2]), pos)
    kw_pad = jnp.pad(kw, ((0, 0), (0, 0), (WINDOW, 0), (0, 0)))
    vw_pad = jnp.pad(kv_heads(v_w), ((0, 0), (0, 0), (WINDOW, 0), (0, 0)))

    g = jax.nn.sigmoid(gates).reshape(B, S, N_KV, HPG, N_BRANCH).transpose(0, 2, 3, 1, 4)
    j_sel = jnp.arange(n_sel)

    def q_block(qi):
        q0 = qi * Q_BLOCK
        t = q0 + jnp.arange(Q_BLOCK)
        qb = lax.dynamic_slice_in_dim(qh, q0, Q_BLOCK, axis=3)
        gb = lax.dynamic_slice_in_dim(g, q0, Q_BLOCK, axis=3)
        s_c = jnp.einsum('bghqd,bgkd->bghqk', qb, kc) * scale
        p_c = masked_softmax(s_c, cmp_end[None, :] <= t[:, None])
        o_c = jnp.einsum('bghqk,bgkd->bghqd', p_c.astype(vc.dtype), vc)
        imp = jnp.einsum('bghqk,kj->bgqj', p_c, overlap)
        bt = (t // SEL_LEN)[:, None]
        force = (j_sel[None, :] == 0) | (j_sel[None, :] == bt) | (j_sel[None, :] == bt - 1)
        imp = jnp.where(force, BIG, jnp.where(j_sel[None, :] <= bt, imp, NEG))
        _, idx = lax.top_k(imp, top_n)
        flat = idx.reshape(B, N_KV, Q_BLOCK * top_n)[..., None]
        kg = jnp.take_along_axis(ks_blk, flat, axis=2).reshape(
            B, N_KV, Q_BLOCK, top_n * SEL_LEN, HEAD_DIM)
        vg = jnp.take_along_axis(vs_blk, flat, axis=2).reshape(
            B, N_KV, Q_BLOCK, top_n * SEL_LEN, HEAD_DIM)
        kpos = (idx[..., None] * SEL_LEN + jnp.arange(SEL_LEN)).reshape(
            B, N_KV, Q_BLOCK, top_n * SEL_LEN)
        m_s = (kpos <= t[None, None, :, None])[:, :, None]
        s_s = jnp.einsum('bghqd,bgqkd->bghqk', qb, kg) * scale
        p_s = masked_softmax(s_s, m_s)
        o_s = jnp.einsum('bghqk,bgqkd->bghqd', p_s.astype(vg.dtype), vg)
        kwb = lax.dynamic_slice_in_dim(kw_pad, q0, WINDOW + Q_BLOCK, axis=2)
        vwb = lax.dynamic_slice_in_dim(vw_pad, q0, WINDOW + Q_BLOCK, axis=2)
        kp = (q0 - WINDOW + jnp.arange(WINDOW + Q_BLOCK))[None, :]
        m_w = (kp <= t[:, None]) & (kp > t[:, None] - WINDOW) & (kp >= 0)
        s_w = jnp.einsum('bghqd,bgkd->bghqk', qb, kwb) * scale
        p_w = masked_softmax(s_w, m_w)
        o_w = jnp.einsum('bghqk,bgkd->bghqd', p_w.astype(vwb.dtype), vwb)
        return gb[..., 0:1] * o_c + gb[..., 1:2] * o_s + gb[..., 2:3] * o_w

    outs = lax.map(q_block, jnp.arange(n_qb))
    return outs.transpose(1, 0, 4, 2, 3, 5).reshape(B, S, NSA_WIDTH)

def hybrid_layer(x, norm_g, w_in, conv_w, conv_b, rg_wr, rg_br, rg_wi, rg_bi, rg_lam,
                 q_g, k_g, pe_k, w1_k, w2_k, pe_v, w1_v, w2_v, w_out):
    h = rms_norm(x, norm_g)
    z = h @ w_in
    sizes = [RG_WIDTH, RG_WIDTH, NSA_WIDTH] + [KV_WIDTH] * 6 + [NSA_WIDTH]
    cuts = list(np.cumsum(sizes))
    (rg_x, rg_gate, q, k_c, v_c, k_s, v_s, k_w, v_w, nsa_gate, br_gate) = jnp.split(
        z, cuts, axis=-1)
    y_a = rg_lru(causal_depthwise_conv(rg_x, conv_w, conv_b), rg_wr, rg_br, rg_wi, rg_bi, rg_lam)
    y_a = y_a * jax.nn.silu(rg_gate)
    y_b = nsa(q, k_c, v_c, k_s, v_s, k_w, v_w, br_gate, q_g, k_g,
              pe_k, w1_k, w2_k, pe_v, w1_v, w2_v)
    y_b = y_b * jax.nn.silu(nsa_gate)
    y = jnp.concatenate([y_a, y_b], axis=-1)
    return x + y @ w_out

def first_inputs(seed: int = 0) -> dict:
    key = jax.random.key(seed)
    ks = jax.random.split(key, 20)
    f32 = jnp.float32
    n = jax.random.normal
    a0 = jax.random.uniform(ks[10], (DEPTH, RG_WIDTH), f32, A_MIN, A_MAX)
    s0 = a0 ** (1.0 / RG_C)
    return {
        "x": n(ks[0], (BATCH, SEQ, D_MODEL), f32),
        "norm_g": 1.0 + 0.02 * n(ks[1], (DEPTH, D_MODEL), f32),
        "w_in": n(ks[2], (DEPTH, D_MODEL, N_IN), f32) * D_MODEL ** -0.5,
        "conv_w": n(ks[3], (DEPTH, CONV_W, RG_WIDTH), f32) * CONV_W ** -0.5,
        "conv_b": 0.01 * n(ks[4], (DEPTH, RG_WIDTH), f32),
        "rg_wr": n(ks[5], (DEPTH, RG_BLOCKS, RG_BLOCK, RG_BLOCK), f32) * RG_BLOCK ** -0.5,
        "rg_br": 0.01 * n(ks[6], (DEPTH, RG_WIDTH), f32),
        "rg_wi": n(ks[7], (DEPTH, RG_BLOCKS, RG_BLOCK, RG_BLOCK), f32) * RG_BLOCK ** -0.5,
        "rg_bi": 0.01 * n(ks[8], (DEPTH, RG_WIDTH), f32),
        "rg_lambda": jnp.log(s0) - jnp.log1p(-s0),
        "q_norm_g": 1.0 + 0.02 * n(ks[9], (DEPTH, HEAD_DIM), f32),
        "k_norm_g": 1.0 + 0.02 * n(ks[11], (DEPTH, N_BRANCH, HEAD_DIM), f32),
        "cmp_pe_k": 0.02 * n(ks[12], (DEPTH, CMP_LEN, HEAD_DIM), f32),
        "cmp_w1_k": n(ks[13], (DEPTH, CMP_LEN * HEAD_DIM, CMP_HIDDEN), f32) * (CMP_LEN * HEAD_DIM) ** -0.5,
        "cmp_w2_k": n(ks[14], (DEPTH, CMP_HIDDEN, HEAD_DIM), f32) * CMP_HIDDEN ** -0.5,
        "cmp_pe_v": 0.02 * n(ks[15], (DEPTH, CMP_LEN, HEAD_DIM), f32),
        "cmp_w1_v": n(ks[16], (DEPTH, CMP_LEN * HEAD_DIM, CMP_HIDDEN), f32) * (CMP_LEN * HEAD_DIM) ** -0.5,
        "cmp_w2_v": n(ks[17], (DEPTH, CMP_HIDDEN, HEAD_DIM), f32) * CMP_HIDDEN ** -0.5,
        "w_out": n(ks[18], (DEPTH, D_MIX, D_MODEL), f32) * D_MIX ** -0.5,
    }

def first_block(x, norm_g, w_in, conv_w, conv_b, rg_wr, rg_br, rg_wi, rg_bi, rg_lambda,
              q_norm_g, k_norm_g, cmp_pe_k, cmp_w1_k, cmp_w2_k, cmp_pe_v, cmp_w1_v,
              cmp_w2_v, w_out):
    for l in range(DEPTH):
        x = hybrid_layer(x, norm_g[l], w_in[l], conv_w[l], conv_b[l], rg_wr[l], rg_br[l],
                         rg_wi[l], rg_bi[l], rg_lambda[l], q_norm_g[l], k_norm_g[l],
                         cmp_pe_k[l], cmp_w1_k[l], cmp_w2_k[l], cmp_pe_v[l], cmp_w1_v[l],
                         cmp_w2_v[l], w_out[l])
    return x


DEPTH_2 = 1

HEAD = 64
RW_HEADS = 8
RW_DIM = RW_HEADS * HEAD
FOX_HEADS = 8
FOX_DIM = FOX_HEADS * HEAD
MIX_DIM = RW_DIM + FOX_DIM
DECAY_LORA = 64
AAA_LORA = 64
GATE_LORA = 128
RW_SPLITS = (RW_DIM, DECAY_LORA, RW_DIM, RW_DIM, AAA_LORA, GATE_LORA)
RW_COLS = sum(RW_SPLITS)
FOX_SPLITS = (FOX_DIM, FOX_DIM, FOX_DIM, FOX_HEADS)
FOX_COLS = sum(FOX_SPLITS)
IN_COLS = RW_COLS + FOX_COLS
N_GROUPS = 8
EXPERTS_PER_GROUP = 8
N_EXPERTS = N_GROUPS * EXPERTS_PER_GROUP
TOP_K = 2
D_EXPERT = D_MODEL // 2
ROW_BLOCK = 128
NORM_EPS = 1e-6
GN_EPS = 64e-5


def rms_norm_2(x, w, eps=NORM_EPS):
    xf = x.astype(jnp.float32)
    y = xf * lax.rsqrt(jnp.mean(xf * xf, axis=-1, keepdims=True) + eps)
    return (y * w.astype(jnp.float32)).astype(x.dtype)

def split_cols(p, sizes):
    idx = np.cumsum(sizes)[:-1].tolist()
    return jnp.split(p, idx, axis=-1)

def token_shift(p, mu):
    prev = jnp.pad(p, ((0, 0), (1, 0), (0, 0)))[:, :-1]
    return p + (prev - p) * mu

def rwkv7_scan(r, w, k, v, a, b):
    B_, T_, H_, N_ = r.shape

    def step(S, inp):
        r_t, w_t, k_t, v_t, a_t, b_t = inp
        sa = jnp.einsum('bhvk,bhk->bhv', S, a_t)
        S = S * w_t[:, :, None, :] + sa[..., None] * b_t[:, :, None, :] + v_t[..., None] * k_t[:, :, None, :]
        return S, jnp.einsum('bhvk,bhk->bhv', S, r_t)

    xs = tuple(jnp.moveaxis(z, 1, 0) for z in (r, w, k, v, a, b))
    S0 = jnp.zeros((B_, H_, N_, N_), jnp.float32)
    _, y = lax.scan(step, S0, xs)
    return jnp.moveaxis(y, 0, 1)

def rwkv7_mixer(p_rw, mu, w0, w2, a0, a2, g2, k_k, k_a, r_k, ln_w, ln_b):
    B_, T_, _ = p_rw.shape
    ps = token_shift(p_rw.astype(jnp.float32), mu.astype(jnp.float32))
    r, pw, k, v, pa, pg = split_cols(ps, RW_SPLITS)
    w = -jax.nn.softplus(-(w0 + jnp.tanh(pw) @ w2)) - 0.5
    decay = jnp.exp(-jnp.exp(w))
    a = jax.nn.sigmoid(a0 + pa @ a2)
    g = jax.nn.sigmoid(pg) @ g2
    heads = lambda z: z.reshape(B_, T_, RW_HEADS, HEAD)
    kk = heads(k * k_k)
    kk = kk / jnp.maximum(jnp.sqrt(jnp.sum(kk * kk, axis=-1, keepdims=True)), 1e-12)
    k = k * (1.0 + (a - 1.0) * k_a)
    r_h, k_h, v_h, a_h, w_h = heads(r), heads(k), heads(v), heads(a), heads(decay)
    y = rwkv7_scan(r_h, w_h, k_h, v_h, -kk, kk * a_h)
    mean = jnp.mean(y, axis=-1, keepdims=True)
    var = jnp.mean(jnp.square(y - mean), axis=-1, keepdims=True)
    y = ((y - mean) * lax.rsqrt(var + GN_EPS)).reshape(B_, T_, RW_DIM) * ln_w + ln_b
    bonus = jnp.sum(r_h * k_h * r_k, axis=-1, keepdims=True) * v_h
    return (y + bonus.reshape(B_, T_, RW_DIM)) * g

def fox_attention(q, k, v, log_f):
    T_ = q.shape[1]
    c = jnp.cumsum(log_f, axis=1).transpose(0, 2, 1)
    scale = HEAD ** -0.5
    outs = []
    for blk in range(T_ // Q_BLOCK):
        q0, q1 = blk * Q_BLOCK, (blk + 1) * Q_BLOCK
        s = jnp.einsum('bqhd,bkhd->bhqk', q[:, q0:q1], k[:, :q1]).astype(jnp.float32) * scale
        s = s + c[:, :, q0:q1, None] - c[:, :, None, :q1]
        causal = jnp.arange(q1)[None, :] <= jnp.arange(q0, q1)[:, None]
        s = jnp.where(causal, s, -jnp.inf)
        p = jax.nn.softmax(s, axis=-1)
        outs.append(jnp.einsum('bhqk,bkhd->bqhd', p.astype(v.dtype), v[:, :q1]))
    return jnp.concatenate(outs, axis=1)

def fox_mixer(p_fox, b_f, qn_w, kn_w):
    B_, T_, _ = p_fox.shape
    q, k, v, f = split_cols(p_fox, FOX_SPLITS)
    heads = lambda z: z.reshape(B_, T_, FOX_HEADS, HEAD)
    q = rms_norm_2(heads(q), qn_w)
    k = rms_norm_2(heads(k), kn_w)
    log_f = jax.nn.log_sigmoid((f + b_f).astype(jnp.float32))
    return fox_attention(q, k, heads(v), log_f).reshape(B_, T_, FOX_DIM)

def hierarchical_moe(h, rg_w, rg_b, re_w, re_b, w_gate, w_up, w_down):
    B_, T_, D_ = h.shape
    xt = h.reshape(-1, D_)
    M = xt.shape[0]
    g_logits = (xt @ rg_w + rg_b).astype(jnp.float32)
    g_prob = jax.nn.softmax(g_logits, axis=-1)
    g_sel = jnp.argmax(g_logits, axis=-1)
    g_gate = jnp.take_along_axis(g_prob, g_sel[:, None], axis=-1)
    e_logits = (xt @ re_w + re_b).astype(jnp.float32).reshape(M, N_GROUPS, EXPERTS_PER_GROUP)
    e_logits = jnp.take_along_axis(e_logits, g_sel[:, None, None], axis=1)[:, 0]
    top_p, top_i = lax.top_k(jax.nn.softmax(e_logits, axis=-1), TOP_K)
    gates = g_gate * top_p / jnp.sum(top_p, axis=-1, keepdims=True)
    expert_id = (g_sel[:, None] * EXPERTS_PER_GROUP + top_i).astype(jnp.int32)
    A = M * TOP_K
    flat_id = expert_id.reshape(A)
    flat_tok = jnp.repeat(jnp.arange(M, dtype=jnp.int32), TOP_K)
    order = jnp.argsort(flat_id)
    sid = flat_id[order]
    counts = jnp.bincount(flat_id, length=N_EXPERTS)
    start = jnp.cumsum(counts) - counts
    padded = (counts + ROW_BLOCK - 1) // ROW_BLOCK * ROW_BLOCK
    pad_end = jnp.cumsum(padded)
    pad_start = pad_end - padded
    dest_sorted = (pad_start[sid] + jnp.arange(A, dtype=jnp.int32) - start[sid]).astype(jnp.int32)
    n_blocks = (A + N_EXPERTS * (ROW_BLOCK - 1) + ROW_BLOCK - 1) // ROW_BLOCK
    buf_tok = jnp.zeros((n_blocks * ROW_BLOCK,), jnp.int32).at[dest_sorted].set(flat_tok[order])
    block_expert = jnp.minimum(
        jnp.searchsorted(pad_end, jnp.arange(n_blocks, dtype=jnp.int32) * ROW_BLOCK, side='right'),
        N_EXPERTS - 1)
    xb = xt[buf_tok].reshape(n_blocks, ROW_BLOCK, D_)

    def expert_block(args):
        xblk, e = args
        hid = jax.nn.silu(xblk @ w_gate[e]) * (xblk @ w_up[e])
        return hid @ w_down[e]

    yb = lax.map(expert_block, (xb, block_expert)).reshape(-1, D_)
    dest = jnp.zeros((A,), jnp.int32).at[order].set(dest_sorted)
    y = jnp.sum(yb[dest].reshape(M, TOP_K, D_) * gates[..., None].astype(yb.dtype), axis=1)
    return y.reshape(B_, T_, D_)

def second_inputs(seed: int = 0) -> dict:
    key = jax.random.key(seed)
    ks = jax.random.split(key, 32)
    n = lambda i, shape, s: jax.random.normal(ks[i], shape, jnp.float32) * s
    L = DEPTH_2
    return {
        "x": n(0, (BATCH, SEQ, D_MODEL), 1.0),
        "norm_mix_w": 1.0 + n(1, (L, D_MODEL), 0.05),
        "w_in": n(2, (L, D_MODEL, IN_COLS), D_MODEL ** -0.5),
        "mu_shift": jax.random.uniform(ks[3], (L, RW_COLS), jnp.float32),
        "rw_w0": jax.random.uniform(ks[4], (L, RW_DIM), jnp.float32, minval=-4.0, maxval=1.0),
        "rw_w2": n(5, (L, DECAY_LORA, RW_DIM), 0.1 * DECAY_LORA ** -0.5),
        "rw_a0": n(6, (L, RW_DIM), 0.1),
        "rw_a2": n(7, (L, AAA_LORA, RW_DIM), AAA_LORA ** -0.5),
        "rw_g2": n(8, (L, GATE_LORA, RW_DIM), GATE_LORA ** -0.5),
        "rw_k_k": 0.85 + n(9, (L, RW_DIM), 0.05),
        "rw_k_a": 1.0 + n(10, (L, RW_DIM), 0.05),
        "rw_r_k": n(11, (L, RW_HEADS, HEAD), 0.1),
        "rw_ln_w": 1.0 + n(12, (L, RW_DIM), 0.05),
        "rw_ln_b": n(13, (L, RW_DIM), 0.02),
        "fox_b_f": jax.random.uniform(ks[14], (L, FOX_HEADS), jnp.float32, minval=1.0, maxval=4.0),
        "fox_q_norm_w": 1.0 + n(15, (L, HEAD), 0.05),
        "fox_k_norm_w": 1.0 + n(16, (L, HEAD), 0.05),
        "w_out": n(17, (L, MIX_DIM, D_MODEL), MIX_DIM ** -0.5),
        "norm_ffn_w": 1.0 + n(18, (L, D_MODEL), 0.05),
        "router_group_w": n(19, (L, D_MODEL, N_GROUPS), D_MODEL ** -0.5),
        "router_group_b": n(20, (L, N_GROUPS), 0.01),
        "router_expert_w": n(21, (L, D_MODEL, N_EXPERTS), D_MODEL ** -0.5),
        "router_expert_b": n(22, (L, N_EXPERTS), 0.01),
        "exp_w_gate": n(23, (L, N_EXPERTS, D_MODEL, D_EXPERT), D_MODEL ** -0.5),
        "exp_w_up": n(24, (L, N_EXPERTS, D_MODEL, D_EXPERT), D_MODEL ** -0.5),
        "exp_w_down": n(25, (L, N_EXPERTS, D_EXPERT, D_MODEL), D_EXPERT ** -0.5),
    }

def second_block(x, norm_mix_w, w_in, mu_shift, rw_w0, rw_w2, rw_a0, rw_a2, rw_g2, rw_k_k, rw_k_a,
              rw_r_k, rw_ln_w, rw_ln_b, fox_b_f, fox_q_norm_w, fox_k_norm_w, w_out, norm_ffn_w,
              router_group_w, router_group_b, router_expert_w, router_expert_b,
              exp_w_gate, exp_w_up, exp_w_down):
    for l in range(DEPTH_2):
        h = rms_norm_2(x, norm_mix_w[l])
        p = h @ w_in[l]
        y_rw = rwkv7_mixer(p[..., :RW_COLS], mu_shift[l], rw_w0[l], rw_w2[l], rw_a0[l], rw_a2[l],
                           rw_g2[l], rw_k_k[l], rw_k_a[l], rw_r_k[l], rw_ln_w[l], rw_ln_b[l])
        y_fox = fox_mixer(p[..., RW_COLS:], fox_b_f[l], fox_q_norm_w[l], fox_k_norm_w[l])
        y_mix = jnp.concatenate([y_rw.astype(x.dtype), y_fox.astype(x.dtype)], axis=-1)
        x = x + y_mix @ w_out[l]
        h = rms_norm_2(x, norm_ffn_w[l])
        x = x + hierarchical_moe(h, router_group_w[l], router_group_b[l], router_expert_w[l],
                                 router_expert_b[l], exp_w_gate[l], exp_w_up[l], exp_w_down[l]).astype(x.dtype)
    return x


def setup_inputs(seed=0):
    out = dict(first_inputs(seed))
    for name, value in second_inputs(seed + 1).items():
        if name != "x":
            out[name + "_2"] = value
    return out


def reference(
    x, norm_g, w_in, conv_w, conv_b, rg_wr, rg_br, rg_wi, rg_bi, rg_lambda, q_norm_g, k_norm_g,
    cmp_pe_k, cmp_w1_k, cmp_w2_k, cmp_pe_v, cmp_w1_v, cmp_w2_v, w_out, norm_mix_w_2, w_in_2,
    mu_shift_2, rw_w0_2, rw_w2_2, rw_a0_2, rw_a2_2, rw_g2_2, rw_k_k_2, rw_k_a_2, rw_r_k_2,
    rw_ln_w_2, rw_ln_b_2, fox_b_f_2, fox_q_norm_w_2, fox_k_norm_w_2, w_out_2, norm_ffn_w_2,
    router_group_w_2, router_group_b_2, router_expert_w_2, router_expert_b_2, exp_w_gate_2,
    exp_w_up_2, exp_w_down_2,
):
    x = first_block(
        x, norm_g, w_in, conv_w, conv_b, rg_wr, rg_br, rg_wi, rg_bi, rg_lambda, q_norm_g,
        k_norm_g, cmp_pe_k, cmp_w1_k, cmp_w2_k, cmp_pe_v, cmp_w1_v, cmp_w2_v, w_out,
    )
    return second_block(
        x, norm_mix_w_2, w_in_2, mu_shift_2, rw_w0_2, rw_w2_2, rw_a0_2, rw_a2_2, rw_g2_2,
        rw_k_k_2, rw_k_a_2, rw_r_k_2, rw_ln_w_2, rw_ln_b_2, fox_b_f_2, fox_q_norm_w_2,
        fox_k_norm_w_2, w_out_2, norm_ffn_w_2, router_group_w_2, router_group_b_2,
        router_expert_w_2, router_expert_b_2, exp_w_gate_2, exp_w_up_2, exp_w_down_2,
    )


_drawn_inputs = setup_inputs


def setup_inputs(seed=0):
    import zlib

    import numpy as np

    out = dict(_drawn_inputs(seed))
    spreads = {}
    factors = {'norm_g': 2.908,
     'rg_br': 8.0,
     'rg_bi': 8.0,
     'q_norm_g': 6.112,
     'k_norm_g': 7.866,
     'cmp_pe_k': 8.0,
     'cmp_pe_v': 4.095,
     'rw_w2_2': 64.0,
     'rw_a0_2': 22.24,
     'rw_k_k_2': 200.0,
     'rw_ln_b_2': 172.104,
     'fox_q_norm_w_2': 19.888,
     'fox_k_norm_w_2': 51.471,
     'router_group_b_2': 64.0,
     'router_expert_b_2': 38.632,
     'norm_mix_w_2': 2.886,
     'rw_a2_2': 3.139,
     'rw_k_a_2': 8.0,
     'rw_r_k_2': 4.238,
     'rw_ln_w_2': 59.311,
     'norm_ffn_w_2': 8.0,
     'router_group_w_2': 2.784,
     'router_expert_w_2': 3.023,
     'exp_w_gate_2': 2.804,
     'fox_b_f_2': 3.748}
    for name, (base, spread) in spreads.items():
        noise = np.random.default_rng([zlib.crc32(name.encode()), seed]).standard_normal(out[name].shape)
        drawn = base * np.exp(spread * noise) if base else spread * noise
        out[name] = __import__('jax').numpy.asarray(drawn.astype(out[name].dtype))
    for name, factor in factors.items():
        out[name] = (out[name] * factor).astype(out[name].dtype)
    return out
```

```python
from contextlib import ExitStack

import numpy as np

import concourse.bass as bass
from concourse import mybir

F32 = mybir.dt.float32
I32 = mybir.dt.int32
U32 = mybir.dt.uint32
ALU = mybir.AluOpType
ACT = mybir.ActivationFunctionType
AX = mybir.AxisListType

P = 128
T = 256
MT = T // P
D = 1024
KC = D // P
DEPTH = 2
HD = 64
EPS = 1e-6
NEG = -1e30
LOWEST = -3e38
SCALE = HD ** -0.5

RG = 512
CT = RG // P
CONV_W = 4
NH = 8
NG = 2
HPG = NH // NG
ROPE = 16
CMP_LEN, CMP_STRIDE = 32, 16
NB = (T - CMP_LEN) // CMP_STRIDE + 1
HID = 128
LP = CMP_LEN // 2
CHUNK = 32
SLOT = 4096
NSLOT = 6
NE = 64
NGROUP, EPG = 8, 8
DE = 512
BLK = 32
NRING = 6

COL_RGX, COL_RGG, COL_Q = 0, RG, 2 * RG
COL_KC = 3 * RG
COL_KW = COL_KC + 4 * NG * HD
COL_NG = COL_KW + 2 * NG * HD
COL_BR = COL_NG + NH * HD
N_IN = COL_BR + 3 * NH
NKW = 2 * NG * HD + 3 * NH

REGION = 20800
N_SMALL2 = 20

ROW_CONV, ROW_CB, ROW_BR, ROW_BI, ROW_LAM, ROW_PEK, ROW_PEV = 0, 16, 20, 24, 28, 32, 48
NROWS = 64


def constants():
    cols, at = [], {}

    def add(name, a):
        a = np.asarray(a, np.float32).reshape(P, -1)
        at[name] = (sum(c.shape[1] for c in cols), a.shape[1])
        cols.append(a)

    p = np.arange(P)[:, None]
    f = np.arange(P)[None, :]
    add("ident", p == f)
    add("causal", np.concatenate([np.zeros((P, P)), np.where(f <= p, 0.0, NEG)], 1))
    end = np.arange(NB) * CMP_STRIDE + CMP_LEN - 1
    seen = np.stack([end[None, :] <= (m * P + p) for m in range(MT)], 1)
    add("cmp_neg", np.where(seen, 0.0, NEG))
    add("cmp_one", seen)
    inv = (np.float32(500000.0) ** (-np.arange(ROPE // 2, dtype=np.float32) / (ROPE // 2))).astype(np.float32)

    def rope(name, pos):
        ang = (pos.astype(np.float32)[..., None] * inv).astype(np.float32)
        c, s = np.cos(ang), np.sin(ang)
        add(name + "_cos", np.concatenate([c, c], -1))
        add(name + "_sin", np.concatenate([-s, s], -1))

    rope("pos", np.arange(MT)[None, :] * P + p)
    rope("end", np.concatenate([end, np.zeros(P - NB)])[:, None])
    add("minus_half", np.full((P, 32), -0.5))
    first = sum(c.shape[1] for c in cols)
    same = lambda n: p // n == f // n
    add("upto", np.concatenate([p <= f, np.ones((P, P))], 1))
    add("restart", np.tile((np.arange(T) % CHUNK != 0)[None], (P, 1)))
    add("below_half_t", (p < f) & same(CHUNK // 2))
    add("below_half", (f < p) & same(CHUNK // 2))
    add("across", (f < p) & same(CHUNK) & ~same(CHUNK // 2))
    add("below_t", (p < f) & same(CHUNK))
    add("upto_t", (p <= f) & same(CHUNK))
    add("head_ones", same(HD))
    add("head_pick", p // HD == np.arange(2)[None, :])
    second = sum(c.shape[1] for c in cols)
    add("before", p < f)
    add("ones", np.ones((P, P)))
    add("iota", np.tile(np.arange(P)[None], (P, 1)))
    add("slot_of", np.tile((np.arange(P) % BLK)[None], (P, 1)))
    add("blocks", np.tile((np.arange(T // BLK) * BLK)[None], (P, 1)))
    return np.concatenate(cols, 1).astype(np.float32), at, (first, second)


def shape(ap, *dims):
    return ap.to_broadcast(list(dims))


def semaphores(nc, ctx, names, suffix=""):
    sems = {n: ctx.enter_context(nc.semaphore(n + suffix)) for n in names}
    nums = sorted(s.num for s in sems.values())
    assert nums == list(range(nums[0], nums[0] + len(nums)))
    return sems, range(nums[0], nums[-1] + 1)


class Chain:

    def __init__(self, eng, sem):
        self.eng, self.sem, self.n = eng, sem, 0

    def __call__(self, ins):
        self.n += 1
        ins.then_inc(self.sem, 1)
        self.eng.wait_ge(self.sem, self.n)
        return ins


def view(ap, *dims):
    names = "abcd"[:len(dims)]
    return ap.rearrange(f"p ({' '.join(names)}) -> p {' '.join(names)}", **dict(zip(names, dims)))


def carve(region):
    at = [0]

    def room(*dims):
        n = int(np.prod(dims))
        ap = region[:, at[0]:at[0] + n]
        at[0] += n
        assert at[0] <= region.shape[1], (at[0], region.shape)
        return view(ap, *dims)

    room.at = at
    return room


def layers_part(nc, ctx, a, mem, psum, const):
    slot, loaded = mem["slots"], mem["loaded"]
    X, XN, HT = mem["x"], mem["xn"], mem["ht"]
    arrived, release = mem["arrived"], mem["release"]
    ident, B = const("ident"), psum
    room = carve(mem["region"])

    rows, params_both, params = room(P), room(DEPTH, NROWS), room(NROWS)
    norm_g = room(DEPTH, KC)
    gain, gain12, gain_c = room(3, HD), room(12, HD), room(HD)
    ss, rstd = room(MT), room(MT)
    ssq, rsq = room(MT * 12), room(MT * 12)
    ssk, rsk = room(NG), room(NG)
    wri = room(2, CT, P)
    w2 = room(2, HD)
    qk_flat = room(MT * 12 * HD)
    qk = view(qk_flat, MT, 12, HD)
    qt = room(MT, HPG, P)
    kt = room(2, T)
    vsw = room(MT, 2, NG, HD)
    tbr, coef, rden = room(MT, 3 * NH), room(MT, 3, NH), room(NH)
    tc, hc = room(2 * NG * NB), room(2 * NG * NB)
    kc, ka, kb = room(NG, HD), room(NG, HD), room(NG, ROPE)
    kct = room(16)
    xc = room(CT, T + CONV_W - 1)
    cv, tr, ti, aa, sgr = room(CT, T), room(CT, T), room(CT, T), room(CT, T), room(CT, T)
    lam, half_b = room(12, CT), room(2, CT)
    sgn_flat = room(MT * NH * HD)
    sgn = view(sgn_flat, MT, NH * HD)
    rot_a, rot_b = [view(sgn_flat[:, i * MT * 12 * ROPE:(i + 1) * MT * 12 * ROPE], MT, 12, ROPE) for i in range(2)]
    cs, cmax = room(MT, NH, NB), room(NH)
    pc, pct = room(MT, NG, HPG * 32), room(MT, NG, P)
    rowmax, negmax, den = room(2, NH), room(2, NH), room(MT, 3, NH)
    yb, tmp = room(MT, NH, HD), room(NH, HD)
    prob = [view(XN[:, :], NH, T), view(HT[:, :], NH, T)]
    ring = room(NRING * 4 * P)
    pt = view(ring, NRING, 4, P)
    vbd = room(NG, HPG * HD)
    ybt = view(qk_flat[:, 0:4 * T], 4, T)
    ht = view(HT[:, :], KC, T)
    junk = ring[:, 0:MT * D]
    sqk = view(ring[:, 0:MT * 12 * HD], MT * 12, HD)
    z = view(ring[:, MT * 12 * HD:MT * 12 * HD + 2 * LP * NG * NB], 2, LP, NG * NB)

    names = """params_ready ss_ready rstd_ready xn_ready params_transposed h_transposed ht_ready
        q_done kcvc_done ksvs_done kwvw_done rgx_done qk_copied qk_ss qk_rstd qk_ready qk_transposed qkt_ready
        z_ready comp1_done comp1_tanh hid_ready comp2_done kc_ss kc_rstd kc_ready kc_transposed kct_ready vbd_ready
        xc_ready cv_ready half_ready lam_in lam_exp c_ready lru_gates_done tr_ready ti_ready rgg_done rgg_tanh sgr_ready
        nsag_done nsag_tanh sgn_ready cmp_scores cmp_out cmp_shifted cmp_exp pc_ready pc_transposed pct_ready
        th_ready aa_ready uq_in uq_ready ya_ready scores masked exp_done p_transposed pt_ready weighed o_taken
        yb_ready yb_transposed ybt_ready out_done x_added dve_step pool_step""".split()
    S, layer_sems = semaphores(nc, ctx, names)

    Q_S, KV_S, KW_S, RGX_S, W1_S, RGG_S, NSAG_S, WO_S = 0, 1, 2, 3, 4, 5, 1, (2, 3)

    def chunk(s, width):
        return slot[:, s, 0:KC * width].rearrange("p (c n) -> p c n", c=KC)

    w_out_c = [chunk(s, 512) for s in WO_S]
    w1_c = slot[:, W1_S, :].rearrange("p (v l h) -> p v l h", v=2, l=LP)
    STEPS = [(0, 0), (1, 0), (0, 1), (1, 1)]
    GROUPS = [2 * (m + 1) for _, m in STEPS]

    def pairs(n, g):
        nk = STEPS[n][1] + 1
        return [((4 * g + b) // nk, (4 * g + b) % nk) for b in range(4)]

    def score_out(n, h):
        (br, m), (g, j) = STEPS[n], divmod(h, HPG)
        if m == 0:
            return B[4 + 2 * br + g][:, j * P:(j + 1) * P]
        return B[4 + 2 * g + j // 2][:, j % 2 * T:(j % 2 + 1) * T]

    def arrive(eng, name):
        eng.drain().then_inc(arrived, 1)
        eng.wait_ge(release[name], 1)
        eng.sem_clear(release[name])

    with nc.Block() as block:

        @block.sync
        def _(sp):
            win, wout = a["w_in"], a["w_out"]

            def load(s, src, width=512):
                sp.dma_start(chunk(s, width), src.rearrange("(p c) n -> p c n", c=KC)).then_inc(loaded[s], 16)

            def load_kw(l):
                kw = chunk(KW_S, NKW)
                sp.dma_start(kw[:, :, 0:256], win[l, :, COL_KW:COL_NG].rearrange("(p c) n -> p c n", c=KC))\
                    .then_inc(loaded[KW_S], 16)
                sp.dma_start(kw[:, :, 256:NKW], win[l, :, COL_BR:N_IN].rearrange("(p c) n -> p c n", c=KC))\
                    .then_inc(mem["br_loaded"], 16)

            def load_w1(l):
                for v, name in enumerate(("cmp_w1_k", "cmp_w1_v")):
                    sp.dma_start(w1_c[:, v], a[name][l].rearrange("(l p) h -> p l h", p=P)).then_inc(mem["w1_loaded"][v], 16)

            def load_small(l):
                sp.dma_start(gain[:, 0], shape(a["q_norm_g"][l:l + 1], P, HD)).then_inc(mem["small_in"], 16)
                sp.dma_start(gain[:, 1:3], shape(a["k_norm_g"][l:l + 1, 1:3], P, 2, HD)).then_inc(mem["small_in"], 16)
                sp.dma_start(gain_c, shape(a["k_norm_g"][l:l + 1, 0], P, HD)).then_inc(mem["small_in"], 16)
                for v, n in enumerate(("cmp_w2_k", "cmp_w2_v")):
                    sp.dma_start(w2[:, v], a[n][l]).then_inc(mem["small_in"], 16)
                for v, n in enumerate(("rg_wr", "rg_wi")):
                    for u in range(2):
                        r = slice(64 * u, 64 * u + 64)
                        sp.dma_start(wri[r, v, :, r], a[n][l].rearrange("(i u) c d -> u c i d", u=2)[u]).then_inc(mem["small_in"], 16)

            sp.dma_start(X[:, :].rearrange("p (m n) -> p m n", m=MT),
                         a["x"].rearrange("b (m p) n -> p (b m) n", p=P)).then_inc(mem["x_in"], 16)
            sp.wait_ge(mem["zeroed"], 4)
            sp.dma_start(mem["const"][:, :], a["constants"][:, 0:mem["const"].shape[1]]).then_inc(mem["const_in"], 16)
            for l in range(DEPTH):
                at = l * NROWS
                sp.dma_start(rows[at + ROW_CONV:at + ROW_CB], a["conv_w"][l].rearrange("k (i p) -> (k i) p", p=P)).then_inc(mem["rows_in"], 16)
                for r, n in ((ROW_CB, "conv_b"), (ROW_BR, "rg_br"), (ROW_BI, "rg_bi"), (ROW_LAM, "rg_lambda")):
                    sp.dma_start(rows[at + r:at + r + 4], a[n][l].rearrange("(i p) -> i p", p=P)).then_inc(mem["rows_in"], 16)
                for r, n in ((ROW_PEK, "cmp_pe_k"), (ROW_PEV, "cmp_pe_v")):
                    sp.dma_start(rows[at + r:at + r + LP], a[n][l].rearrange("(l t) d -> l (t d)", t=2)).then_inc(mem["rows_in"], 16)
            sp.dma_start(norm_g, a["norm_g"].rearrange("l (p c) -> p l c", c=KC)).then_inc(mem["norm_in"], 16)
            load_small(0)
            load(Q_S, win[0, :, COL_Q:COL_KC])
            load(KV_S, win[0, :, COL_KC:COL_KW])
            load_kw(0)
            load(RGX_S, win[0, :, COL_RGX:COL_RGG])
            load_w1(0)
            load(RGG_S, win[0, :, COL_RGG:COL_Q])
            for l in range(DEPTH):
                sp.wait_ge(S["ksvs_done"], MT)
                load(NSAG_S, win[l, :, COL_NG:COL_BR])
                for h, done, n in ((0, S["kwvw_done"], MT), (1, S["rgx_done"], 2)):
                    sp.wait_ge(done, n)
                    sp.dma_start(w_out_c[h], wout[l, :, h * 512:(h + 1) * 512].rearrange("(k p) n -> p k n", p=P))\
                        .then_inc(loaded[WO_S[h]], 16)
                if l + 1 < DEPTH:
                    sp.wait_ge(S["q_done"], MT)
                    load(Q_S, win[l + 1, :, COL_Q:COL_KC])
                    sp.wait_ge(S["comp1_done"], 1)
                    load_w1(l + 1)
                    sp.wait_ge(S["rgg_done"], 2)
                    load(RGG_S, win[l + 1, :, COL_RGG:COL_Q])
                    sp.wait_ge(S["nsag_done"], MT)
                    load(KV_S, win[l + 1, :, COL_KC:COL_KW])
                    sp.wait_ge(S["out_done"], 2 * MT)
                    load_small(l + 1)
                    load_kw(l + 1)
                    load(RGX_S, win[l + 1, :, COL_RGX:COL_RGG])
                else:
                    for done, n, names in ((S["q_done"], MT, ("fq",)), (S["comp1_done"], 1, ("fk",)), (S["rgg_done"], 2, ("fv",)),
                                           (S["nsag_done"], MT, ("lora",)), (S["out_done"], 2 * MT, ("r", "k"))):
                        sp.wait_ge(done, n)
                        for name in names:
                            load_mixer_weights(sp, a, slot, loaded, name)
                arrive(sp, "sp")

        @block.gpsimd
        def _(pool):
            nc.gpsimd.memset(wri, 0.0).then_inc(mem["zeroed"], 1)
            nc.gpsimd.memset(vbd, 0.0).then_inc(mem["zeroed"], 1)
            nc.gpsimd.memset(xc[:, :, 0:CONV_W - 1], 0.0).then_inc(mem["zeroed"], 1)
            nc.gpsimd.memset(pc, 0.0).then_inc(mem["zeroed"], 1)
            pool.wait_ge(mem["zeroed"], 4)
            pool.wait_ge(mem["const_in"], 16)
            with pool.Fori(0, DEPTH):
                steps = [0]

                def inv_root(out, src, scale, ready, n, done):
                    pool.wait_ge(ready, n)
                    nc.gpsimd.tensor_scalar(out, src, scale, EPS, ALU.mult, ALU.add).then_inc(S["pool_step"], 1)
                    steps[0] += 1
                    pool.wait_ge(S["pool_step"], steps[0])
                    nc.gpsimd.tensor_tensor(out, out, const("minus_half")[0:out.shape[0], 0:out.shape[1]], ALU.pow)\
                        .then_inc(done, 1)

                inv_root(rstd, ss, 1.0 / D, S["ss_ready"], MT, S["rstd_ready"])
                inv_root(rsq, ssq, 1.0 / HD, S["qk_ss"], 1, S["qk_rstd"])
                inv_root(rsk[0:NB], ssk[0:NB], 1.0 / HD, S["kc_ss"], 1, S["kc_rstd"])
                arrive(pool, "pool")

        @block.scalar
        def _(act):
            act.wait_ge(mem["rows_transposed"], 1)
            nc.scalar.copy(params_both.rearrange("p l r -> p (l r)"), B[7][:, 0:P]).then_inc(mem["both_ready"], 1)
            act.wait_ge(mem["both_ready"], 1)
            act.wait_ge(mem["x_in"], 16)
            with act.Fori(0, DEPTH) as l:
                for m in range(MT):
                    nc.scalar.activation(junk[:, m * D:(m + 1) * D], X[:, m * D:(m + 1) * D], ACT.Square,
                                         accum_out=ss[:, m:m + 1]).then_inc(S["ss_ready"], 1)
                nc.scalar.copy(params.unsqueeze(1), params_both[:, bass.ds(l, 1)]).then_inc(S["params_ready"], 1)
                act.wait_ge(S["params_ready"], 1)
                nc.scalar.mul(half_b.rearrange("p a b -> p (a b)"), params[:, ROW_BR:ROW_LAM], 0.5).then_inc(S["half_ready"], 1)
                act.wait_ge(S["lam_in"], 1)
                nc.scalar.activation(lam[:, 1], lam[:, 0], ACT.Exp, scale=-1.0).then_inc(S["lam_exp"], 1)
                for m in range(MT):
                    act.wait_ge(S["q_done"], m + 1)
                    nc.scalar.copy(qk[:, m, 0:NH].rearrange("p (j g) d -> p g j d", g=NG),
                                   B[4 + m][:, :].rearrange("p (g j d) -> p g j d", g=NG, d=HD)).then_inc(S["qk_copied"], 1)
                act.wait_ge(S["ksvs_done"], MT)
                for m in range(MT):
                    v = B[7][:, m * 256:(m + 1) * 256].rearrange("p (k d) -> p k d", d=HD)
                    nc.scalar.copy(qk[:, m, 8:10], v[:, 0:2]).then_inc(S["qk_copied"], 1)
                    nc.scalar.copy(vsw[:, m, 0], v[:, 2:4]).then_inc(S["qk_copied"], 1)
                for m in range(MT):
                    act.wait_ge(S["kwvw_done"], m + 1)
                    v = B[m][:, 0:256].rearrange("p (k d) -> p k d", d=HD)
                    nc.scalar.copy(qk[:, m, 10:12], v[:, 0:2]).then_inc(S["qk_copied"], 1)
                    nc.scalar.copy(vsw[:, m, 1], v[:, 2:4]).then_inc(S["qk_copied"], 1)
                    nc.scalar.activation(tbr[:, m], B[m][:, 256:NKW], ACT.Tanh, scale=0.5).then_inc(S["qk_copied"], 1)
                for b in range(2):
                    act.wait_ge(S["rgx_done"], b + 1)
                    nc.scalar.copy(xc[:, 2 * b:2 * b + 2, CONV_W - 1:], B[2 + b][:, :].rearrange("p (i t) -> p i t", i=2))\
                        .then_inc(S["xc_ready"], 1)
                act.wait_ge(S["comp1_done"], 1)
                nc.scalar.activation(tc, B[6][:, 0:2 * NG * NB], ACT.Tanh, scale=0.5).then_inc(S["comp1_tanh"], 1)
                for m in range(MT):
                    act.wait_ge(S["qk_transposed"], m + 1)
                    b0, b1 = (B[4], B[5]) if m == 0 else (B[7], B[0])
                    nc.scalar.copy(qt[:, m], b0[:, :].rearrange("p (j t) -> p j t", j=HPG)).then_inc(S["qkt_ready"], 1)
                    nc.scalar.copy(kt[:, :, m * P:(m + 1) * P], b1[:, 0:256].rearrange("p (v t) -> p v t", v=2))\
                        .then_inc(S["qkt_ready"], 1)
                for b in range(2):
                    act.wait_ge(S["rgg_done"], b + 1)
                    nc.scalar.activation(sgr[:, 2 * b:2 * b + 2], B[2 + b][:, :].rearrange("p (i t) -> p i t", i=2),
                                         ACT.Tanh, scale=0.5).then_inc(S["rgg_tanh"], 1)
                act.wait_ge(S["half_ready"], 1)
                for g, (out, sem) in enumerate(((tr, S["tr_ready"]), (ti, S["ti_ready"]))):
                    for i in range(CT):
                        if i % 2 == 0:
                            act.wait_ge(S["lru_gates_done"], 2 * g + i // 2 + 1)
                        nc.scalar.activation(out[:, i], B[4 + 2 * g + i // 2][:, i % 2 * T:(i % 2 + 1) * T], ACT.Tanh,
                                             bias=half_b[:, g, i:i + 1], scale=0.5).then_inc(sem, 1)
                act.wait_ge(S["kc_transposed"], 1)
                nc.scalar.copy(kct[:, 0:NB], B[1][:, 256:256 + NB]).then_inc(S["kct_ready"], 1)
                for m in range(MT):
                    act.wait_ge(S["nsag_done"], m + 1)
                    nc.scalar.activation(sgn[:, m], B[2 * m][:, :], ACT.Tanh, scale=0.5).then_inc(S["nsag_tanh"], 1)
                for m in range(MT):
                    act.wait_ge(S["cmp_shifted"], m + 1)
                    nc.scalar.activation(cs[:, m], cs[:, m], ACT.Exp, scale=SCALE).then_inc(S["cmp_exp"], 1)

                def exps(n):
                    br, m = STEPS[n]
                    act.wait_ge(S["masked"], n + 1)
                    for h in range(NH):
                        p = prob[n % 2][:, h, 0:(m + 1) * P]
                        nc.scalar.activation(p, p, ACT.Exp, bias=negmax[:, n % 2, h:h + 1], scale=SCALE,
                                             accum_out=den[:, m, 1 + br, h:h + 1]).then_inc(S["exp_done"], 1)

                def evacuate(n):
                    for g in range(GROUPS[n]):
                        k = sum(GROUPS[:n]) + g
                        if k >= NRING:
                            act.wait_ge(S["weighed"], k - NRING + 1)
                        act.wait_ge(S["p_transposed"], k + 1)
                        nc.scalar.copy(pt[:, k % NRING], B[k % 2][:, :].rearrange("p (b t) -> p b t", b=4)).then_inc(S["pt_ready"], 1)

                exps(0)
                for m in range(MT):
                    act.wait_ge(S["pc_transposed"], m + 1)
                    nc.scalar.copy(pct[:, m], B[m][:, 0:256].rearrange("p (g t) -> p g t", g=NG)).then_inc(S["pct_ready"], 1)
                exps(1)
                evacuate(0)
                exps(2)
                act.wait_ge(S["c_ready"], 2)
                act.wait_ge(S["tr_ready"], CT)
                for i in range(CT):
                    nc.scalar.activation(aa[:, i], tr[:, i], ACT.Exp, bias=lam[:, 11, i:i + 1], scale=lam[:, 11, i:i + 1])\
                        .then_inc(S["aa_ready"], 1)
                act.wait_ge(S["aa_ready"], CT)
                for i in range(CT):
                    nc.scalar.activation(tr[:, i], tr[:, i], ACT.Tanh, bias=lam[:, 10, i:i + 1], scale=lam[:, 10, i:i + 1])\
                        .then_inc(S["th_ready"], 1)
                evacuate(1)
                exps(3)
                act.wait_ge(S["uq_in"], 1)
                nc.scalar.activation(tr, tr, ACT.Sqrt, scale=0.5).then_inc(S["uq_ready"], 1)
                evacuate(2)
                evacuate(3)
                for m in range(MT):
                    act.wait_ge(S["yb_transposed"], m + 1)
                    nc.scalar.copy(ybt[:, :, m * P:(m + 1) * P], B[m][:, :].rearrange("p (k t) -> p k t", k=4)).then_inc(S["ybt_ready"], 1)
                arrive(act, "act")

        @block.tensor
        def _(pe):
            pe.wait_ge(mem["const_in"], 16)
            pe.wait_ge(mem["rows_in"], 16 * 7 * DEPTH)
            nc.tensor.transpose(B[7][:, 0:P], rows, ident).then_inc(mem["rows_transposed"], 1)
            with pe.Fori(0, DEPTH) as l:
                weights = (l + 1) * 16
                second = (l + 1) * 32
                first_of_two = l * 32 + 16

                for m in range(MT):
                    pe.wait_ge(S["xn_ready"], m + 1)
                    xn = XN[:, m * D:(m + 1) * D].rearrange("p (k c) -> p k c", c=KC)
                    for c in range(KC):
                        t = nc.tensor.transpose(B[2 * m + c // 4][:, c % 4 * P:(c % 4 + 1) * P], xn[:, :, c], ident)
                        if c % 4 == 3:
                            t.then_inc(S["h_transposed"], 1)

                def tokens(m, out, w, cols):
                    for c in range(KC):
                        mm = nc.tensor.matmul(out, ht[:, c, m * P:(m + 1) * P], w[:, c, cols], start=c == 0, stop=c == KC - 1)
                    return mm

                def features(out, w, cols):
                    for c in range(KC):
                        mm = nc.tensor.matmul(out, w[:, c, cols], ht[:, c, :], start=c == 0, stop=c == KC - 1)
                    return mm

                pe.wait_ge(loaded[Q_S], weights)
                for m in range(MT):
                    pe.wait_ge(S["ht_ready"], 2 * (m + 1))
                    tokens(m, B[4 + m][:, :], chunk(Q_S, 512), slice(0, 512)).then_inc(S["q_done"], 1)
                pe.wait_ge(loaded[KV_S], first_of_two)
                kv = chunk(KV_S, 512)
                for v in range(2):
                    features(B[6][:, v * T:(v + 1) * T], kv, slice(v * P, (v + 1) * P)).then_inc(S["kcvc_done"], 1)
                pe.wait_ge(S["params_ready"], 1)
                for m in range(MT):
                    tokens(m, B[7][:, m * 256:(m + 1) * 256], kv, slice(256, 512)).then_inc(S["ksvs_done"], 1)
                pe.wait_ge(loaded[KW_S], first_of_two)
                pe.wait_ge(mem["br_loaded"], weights)
                for m in range(MT):
                    tokens(m, B[m][:, 0:NKW], chunk(KW_S, NKW), slice(0, NKW)).then_inc(S["kwvw_done"], 1)
                pe.wait_ge(loaded[RGX_S], first_of_two)
                for i in range(CT):
                    mm = features(B[2 + i // 2][:, i % 2 * T:(i % 2 + 1) * T], chunk(RGX_S, 512), slice(i * P, (i + 1) * P))
                    if i % 2:
                        mm.then_inc(S["rgx_done"], 1)
                pe.wait_ge(S["z_ready"], 1)
                for v in range(2):
                    pe.wait_ge(mem["w1_loaded"][v], weights)
                    for i in range(LP):
                        mm = nc.tensor.matmul(B[6][:, v * NG * NB:(v + 1) * NG * NB], w1_c[:, v, i], z[:, v, i],
                                              start=i == 0, stop=i == LP - 1)
                mm.then_inc(S["comp1_done"], 1)
                pe.wait_ge(loaded[RGG_S], weights)
                pe.wait_ge(S["xc_ready"], 2)
                for i in range(CT):
                    mm = features(B[2 + i // 2][:, i % 2 * T:(i % 2 + 1) * T], chunk(RGG_S, 512), slice(i * P, (i + 1) * P))
                    if i % 2:
                        mm.then_inc(S["rgg_done"], 1)
                pe.wait_ge(S["qk_ready"], 1)
                for m in range(MT):
                    b0, b1 = (B[4], B[5]) if m == 0 else (B[7], B[0])
                    for j in range(HPG):
                        nc.tensor.transpose(b0[:, j * P:(j + 1) * P], qk[:, m, 2 * j:2 * j + 2].rearrange("p g d -> p (g d)"), ident)
                    for v in range(2):
                        t = nc.tensor.transpose(b1[:, v * P:(v + 1) * P], qk[:, m, 8 + 2 * v:10 + 2 * v].rearrange("p g d -> p (g d)"), ident)
                    t.then_inc(S["qk_transposed"], 1)
                pe.wait_ge(S["hid_ready"], 1)
                pe.wait_ge(mem["small_in"], weights * 9)
                for v in range(2):
                    for g in range(NG):
                        at = (v * NG + g) * NB
                        mm = nc.tensor.matmul(B[1][0:NB, (v * NG + g) * HD:(v * NG + g + 1) * HD], hc[:, at:at + NB], w2[:, v],
                                              start=True, stop=True)
                mm.then_inc(S["comp2_done"], 1)
                for g in range(2):
                    pe.wait_ge(S["qkt_ready"], 2 * (g + 1))
                    for i in range(CT):
                        pe.wait_ge(S["cv_ready"], i + 1)
                        mm = nc.tensor.matmul(B[4 + 2 * g + i // 2][:, i % 2 * T:(i % 2 + 1) * T], wri[:, g, i], cv[:, i],
                                              start=True, stop=True)
                        if i % 2:
                            mm.then_inc(S["lru_gates_done"], 1)
                pe.wait_ge(S["kc_ready"], 1)
                pe.wait_ge(S["vbd_ready"], 1)
                nc.tensor.transpose(B[1][:, 256:256 + NB], kc[0:NB].rearrange("p g d -> p (g d)"), ident[0:NB, 0:NB])\
                    .then_inc(S["kc_transposed"], 1)
                pe.wait_ge(loaded[NSAG_S], second)
                for m in range(MT):
                    if m:
                        pe.wait_ge(S["sgr_ready"], 1)
                    tokens(m, B[2 * m][:, :], chunk(NSAG_S, 512), slice(0, 512)).then_inc(S["nsag_done"], 1)
                pe.wait_ge(S["kct_ready"], 1)
                pe.wait_ge(S["sgr_ready"], 2)
                for m in range(MT):
                    for g in range(NG):
                        r = slice(64 * g, 64 * g + 64)
                        for j in range(HPG):
                            at = (m * HPG + j) * 16
                            mm = nc.tensor.matmul(B[(3, 1)[g]][:, at:at + NB], qt[r, m, j], kct[r, 0:NB], start=True, stop=True)
                        mm.then_inc(S["cmp_scores"], 1)

                def score(n):
                    br, m = STEPS[n]
                    for j in range(HPG):
                        for g in range(NG):
                            r = slice(64 * g, 64 * g + 64)
                            mm = nc.tensor.matmul(score_out(n, g * HPG + j), qt[r, m, j], kt[r, br, 0:(m + 1) * P],
                                                  start=True, stop=True)
                    mm.then_inc(S["scores"], 1)

                def transpose_group(n, g):
                    k = sum(GROUPS[:n]) + g
                    if k >= 2:
                        pe.wait_ge(S["pt_ready"], k - 1)
                    else:
                        pe.wait_ge(S["pct_ready"], k + 1)
                    for b, (h, key) in enumerate(pairs(n, g)):
                        t = nc.tensor.transpose(B[k % 2][:, b * P:(b + 1) * P], prob[n % 2][:, h, key * P:(key + 1) * P], ident)
                    t.then_inc(S["p_transposed"], 1)

                def weigh_group(n, g):
                    br, m = STEPS[n]
                    k = sum(GROUPS[:n]) + g
                    pe.wait_ge(S["pt_ready"], k + 1)
                    for b, (h, key) in enumerate(pairs(n, g)):
                        mm = nc.tensor.matmul(B[2 + n % 2][:, h * HD:(h + 1) * HD], pt[:, k % NRING, b], vsw[:, key, br, h // HPG],
                                              start=key == 0, stop=key == m)
                    mm.then_inc(S["weighed"], 1)

                def attend(n):
                    pe.wait_ge(S["exp_done"], NH * (n + 1))
                    pe.wait_ge(S["o_taken"], n + 1)
                    for g in range(GROUPS[n]):
                        transpose_group(n, g)
                        if g:
                            weigh_group(n, g - 1)
                    weigh_group(n, GROUPS[n] - 1)

                pe.wait_ge(S["tr_ready"], CT)
                score(0)
                pe.wait_ge(S["ti_ready"], CT)
                score(1)
                for m in range(MT):
                    pe.wait_ge(S["pc_ready"], m + 1)
                    if m == 0:
                        pe.wait_ge(S["sgn_ready"], 1)
                    for g in range(NG):
                        t = nc.tensor.transpose(B[m][:, g * P:(g + 1) * P], pc[:, m, g], ident)
                    t.then_inc(S["pc_transposed"], 1)
                pe.wait_ge(S["vbd_ready"], 1)
                for m in range(MT):
                    pe.wait_ge(S["pct_ready"], m + 1)
                    pe.wait_ge(S["sgn_ready"] if m == 0 else S["cmp_shifted"], 2)
                    for g in range(NG):
                        mm = nc.tensor.matmul(B[2 + m][:, g * 256:(g + 1) * 256], pct[:, m, g], vbd[:, g], start=True, stop=True)
                    mm.then_inc(S["cmp_out"], 1)
                attend(0)
                pe.wait_ge(S["masked"], 2)
                score(2)
                attend(1)
                pe.wait_ge(S["masked"], 3)
                score(3)
                attend(2)
                attend(3)
                for m in range(MT):
                    pe.wait_ge(S["yb_ready"], m + 1)
                    pe.wait_ge(S["pt_ready"], sum(GROUPS))
                    for k in range(4):
                        t = nc.tensor.transpose(B[m][:, k * P:(k + 1) * P],
                                                yb[:, m, 2 * k:2 * k + 2].rearrange("p h d -> p (h d)"), ident)
                    t.then_inc(S["yb_transposed"], 1)
                pe.wait_ge(S["masked"], 4)
                pe.wait_ge(S["ya_ready"], CT)
                for h in range(2):
                    pe.wait_ge(loaded[WO_S[h]], second)
                for m in range(MT):
                    pe.wait_ge(S["ybt_ready"], m + 1)
                    for h in range(2):
                        for k in range(KC):
                            y = cv[:, k, m * P:(m + 1) * P] if k < CT else ybt[:, k - CT, m * P:(m + 1) * P]
                            mm = nc.tensor.matmul(B[4 + 2 * m + h][:, :], y, w_out_c[h][:, k, :], start=k == 0, stop=k == KC - 1)
                        mm.then_inc(S["out_done"], 1)
                arrive(pe, "pe")

        @block.vector
        def _(dve):
            dve.wait_ge(mem["zeroed"], 4)
            dve.wait_ge(mem["x_in"], 16)
            with dve.Fori(0, DEPTH) as l:
                after = Chain(dve, S["dve_step"])
                V = nc.vector
                dve.wait_ge(S["rstd_ready"], 1)
                for m in range(MT):
                    V.tensor_scalar(XN[:, m * D:(m + 1) * D], X[:, m * D:(m + 1) * D], rstd[:, m:m + 1], None, ALU.mult)\
                        .then_inc(S["xn_ready"], 1)
                dve.wait_ge(mem["norm_in"], 16)
                for m in range(MT):
                    for b in range(2):
                        dve.wait_ge(S["h_transposed"], 2 * m + b + 1)
                        V.tensor_tensor(ht[:, 4 * b:4 * b + 4, m * P:(m + 1) * P], B[2 * m + b][:, :].rearrange("p (c t) -> p c t", c=4),
                                        shape(norm_g[:, bass.ds(l, 1), 4 * b:4 * b + 4].rearrange("p l c -> p c l"), P, 4, P), ALU.mult)\
                            .then_inc(S["ht_ready"], 1)
                dve.wait_ge(mem["small_in"], (l + 1) * 16 * 9)
                V.tensor_copy(gain12[:, 0:8], shape(gain[:, 0:1], P, 8, HD))
                after(V.tensor_copy(gain12[:, 8:12].rearrange("p (v g) d -> p v g d", v=2),
                                    shape(gain[:, 1:3].unsqueeze(2), P, 2, NG, HD)))
                dve.wait_ge(S["params_ready"], 1)
                pl = params[:, ROW_LAM:ROW_LAM + 4]
                after(V.tensor_scalar(lam[:, 7], pl, -1.0, 0.0, ALU.mult, ALU.max))
                V.scalar_tensor_tensor(lam[:, 0], lam[:, 7], 2.0, pl, ALU.mult, ALU.add).then_inc(S["lam_in"], 1)
                dve.wait_ge(S["lam_exp"], 1)
                log1p_of(V, after, lam)
                after(V.scalar_tensor_tensor(lam[:, 9], lam[:, 8], 2.0, lam[:, 7], ALU.mult, ALU.add))
                V.tensor_scalar(lam[:, 10], lam[:, 9], 4.0, None, ALU.mult).then_inc(S["c_ready"], 1)
                V.tensor_scalar(lam[:, 11], lam[:, 9], -4.0, None, ALU.mult).then_inc(S["c_ready"], 1)
                dve.wait_ge(S["kcvc_done"], 2)
                for v in range(2):
                    for g in range(NG):
                        src = B[6][64 * g:64 * g + 64, v * T:(v + 1) * T]
                        for t in range(2):
                            rws = slice(64 * t, 64 * t + 64)
                            tok = src.rearrange("p (b i t) -> p t i b", t=2, i=LP // 2)[:, t]
                            row = (ROW_PEK, ROW_PEV)[v]
                            for half in range(2):
                                i = slice(half * LP // 2, (half + 1) * LP // 2)
                                pe = shape(params[rws, row + i.start:row + i.stop].unsqueeze(2), 64, LP // 2, NB)
                                ins = V.tensor_tensor(z[rws, v, i, g * NB:(g + 1) * NB], tok[:, :, half:half + NB], pe, ALU.add)
                ins.then_inc(S["z_ready"], 1)
                dve.wait_ge(S["qk_copied"], 12)
                flat = qk.rearrange("p m k d -> p (m k) d")
                after(V.tensor_tensor(sqk, flat, flat, ALU.mult))
                V.tensor_reduce(ssq, sqk, AX.X, ALU.add).then_inc(S["qk_ss"], 1)
                for i in range(CT):
                    if i % 2 == 0:
                        dve.wait_ge(S["xc_ready"], i // 2 + 1)
                    w = lambda k: params[:, ROW_CONV + 4 * k + i:ROW_CONV + 4 * k + i + 1]
                    after(V.tensor_scalar(cv[:, i], xc[:, i, 0:T], w(0), params[:, ROW_CB + i:ROW_CB + i + 1], ALU.mult, ALU.add))
                    for k in range(1, CONV_W):
                        ins = V.scalar_tensor_tensor(cv[:, i], xc[:, i, k:k + T], w(k), cv[:, i], ALU.mult, ALU.add)
                        if k < CONV_W - 1:
                            after(ins)
                    ins.then_inc(S["cv_ready"], 1)
                dve.wait_ge(S["qk_rstd"], 1)
                after(V.tensor_tensor(flat, flat, shape(rsq.unsqueeze(2), P, MT * 12, HD), ALU.mult))
                after(V.tensor_tensor(qk, qk, shape(gain12.unsqueeze(1), P, MT, 12, HD), ALU.mult))
                cos, sin = [const("pos_" + n).rearrange("p (m r) -> p m r", m=MT) for n in ("cos", "sin")]
                wide = lambda t, lo, hi: shape(t[:, :, lo:hi].unsqueeze(2), P, MT, 12, hi - lo)
                V.tensor_tensor(rot_a, qk[:, :, :, 0:ROPE], wide(cos, 0, ROPE), ALU.mult)
                V.tensor_tensor(rot_b[:, :, :, 0:8], qk[:, :, :, 8:16], wide(sin, 0, 8), ALU.mult)
                after(V.tensor_tensor(rot_b[:, :, :, 8:16], qk[:, :, :, 0:8], wide(sin, 8, 16), ALU.mult))
                V.tensor_tensor(qk[:, :, :, 0:ROPE], rot_a, rot_b, ALU.add).then_inc(S["qk_ready"], 1)
                dve.wait_ge(S["comp1_tanh"], 1)
                V.scalar_tensor_tensor(hc, tc, 1.0, B[6][:, 0:2 * NG * NB], ALU.add, ALU.mult).then_inc(S["hid_ready"], 1)
                dve.wait_ge(S["comp2_done"], 1)
                kn, kan, kbn = kc[0:NB], ka[0:NB], kb[0:NB]
                after(V.tensor_scalar(kn, B[1][0:NB, 0:NG * HD].rearrange("p (g d) -> p g d", g=NG), 0.5, None, ALU.mult))
                after(V.tensor_tensor(kan, kn, kn, ALU.mult))
                V.tensor_reduce(ssk[0:NB], kan, AX.X, ALU.add).then_inc(S["kc_ss"], 1)
                for g in range(NG):
                    for j in range(HPG):
                        ins = V.tensor_scalar(vbd[32 * j:32 * j + NB, g, j * HD:(j + 1) * HD],
                                              B[1][0:NB, (NG + g) * HD:(NG + g + 1) * HD], 0.5, None, ALU.mult)
                ins.then_inc(S["vbd_ready"], 1)
                dve.wait_ge(S["kc_rstd"], 1)
                after(V.tensor_tensor(kn, kn, shape(rsk[0:NB].unsqueeze(2), NB, NG, HD), ALU.mult))
                after(V.tensor_tensor(kn, kn, shape(gain_c[0:NB].unsqueeze(1), NB, NG, HD), ALU.mult))
                ec, es = [shape(const("end_" + n)[0:NB].unsqueeze(1), NB, NG, ROPE) for n in ("cos", "sin")]
                V.tensor_tensor(kan[:, :, 0:ROPE], kn[:, :, 0:ROPE], ec, ALU.mult)
                V.tensor_tensor(kbn[:, :, 0:8], kn[:, :, 8:16], es[:, :, 0:8], ALU.mult)
                after(V.tensor_tensor(kbn[:, :, 8:16], kn[:, :, 0:8], es[:, :, 8:16], ALU.mult))
                V.tensor_tensor(kn[:, :, 0:ROPE], kan[:, :, 0:ROPE], kbn, ALU.add).then_inc(S["kc_ready"], 1)
                for b in range(2):
                    dve.wait_ge(S["rgg_tanh"], b + 1)
                    g2 = sgr[:, 2 * b:2 * b + 2]
                    V.scalar_tensor_tensor(g2, g2, 1.0, B[2 + b][:, :].rearrange("p (i t) -> p i t", i=2), ALU.add, ALU.mult)\
                        .then_inc(S["sgr_ready"], 1)
                for m in range(MT):
                    dve.wait_ge(S["nsag_tanh"], m + 1)
                    V.scalar_tensor_tensor(sgn[:, m], sgn[:, m], 1.0, B[2 * m][:, :], ALU.add, ALU.mult).then_inc(S["sgn_ready"], 1)
                dve.wait_ge(S["cmp_scores"], MT * NG)
                for m in range(MT):
                    neg = const("cmp_neg")[:, m * NB:(m + 1) * NB]
                    for g in range(NG):
                        sc = view(B[(3, 1)[g]][:, m * 64:(m + 1) * 64], HPG, 16)[:, :, 0:NB]
                        ins = V.tensor_tensor(cs[:, m, g * HPG:(g + 1) * HPG], sc, shape(neg.unsqueeze(1), P, HPG, NB), ALU.add)
                    after(ins)
                    after(V.tensor_reduce(cmax, cs[:, m], AX.X, ALU.max))
                    V.tensor_tensor(cs[:, m], cs[:, m], shape(cmax.unsqueeze(2), P, NH, NB), ALU.subtract).then_inc(S["cmp_shifted"], 1)
                    if m == 0:
                        dve.wait_ge(S["cmp_shifted"], 1)

                def mask(n):
                    br, m = STEPS[n]
                    dve.wait_ge(S["scores"], n + 1)
                    if n >= 2:
                        dve.wait_ge(S["p_transposed"], sum(GROUPS[:n - 1]))
                    for h in range(NH):
                        ins = V.tensor_tensor_reduce(out=prob[n % 2][:, h, 0:(m + 1) * P], in0=score_out(n, h),
                                                     in1=const("causal")[:, (1 - m) * P:], scale=1.0, scalar=LOWEST,
                                                     op0=ALU.add, op1=ALU.max, accum_out=rowmax[:, n % 2, h:h + 1])
                    after(ins)
                    if n >= 2:
                        dve.wait_ge(S["exp_done"], NH * (n - 1))
                    V.tensor_scalar(negmax[:, n % 2], rowmax[:, n % 2], -SCALE, None, ALU.mult).then_inc(S["masked"], 1)

                def take(n, br, m, bank, first):
                    after(V.reciprocal(rden, den[:, m, br]))
                    after(V.scalar_tensor_tensor(coef[:, m, br], tbr[:, m].rearrange("p (h b) -> p b h", b=3)[:, br], 1.0, rden,
                                                 ALU.add, ALU.mult))
                    o = bank[:, :].rearrange("p (h d) -> p h d", h=NH)
                    by = shape(coef[:, m, br].unsqueeze(2), P, NH, HD)
                    if first:
                        V.tensor_tensor(yb[:, m], o, by, ALU.mult).then_inc(S["o_taken"], 1)
                        dve.wait_ge(S["o_taken"], n)
                    else:
                        V.tensor_tensor(tmp, o, by, ALU.mult).then_inc(S["o_taken"], 1)
                        dve.wait_ge(S["o_taken"], n)
                        after(V.tensor_tensor(yb[:, m], yb[:, m], tmp, ALU.add))

                def finish(m):
                    yf = yb[:, m].rearrange("p h d -> p (h d)")
                    V.scalar_tensor_tensor(yf, yf, 0.25, sgn[:, m], ALU.mult, ALU.mult).then_inc(S["yb_ready"], 1)

                mask(0)
                for m in range(MT):
                    dve.wait_ge(S["cmp_exp"], m + 1)
                    V.tensor_reduce(den[:, m, 0], cs[:, m], AX.X, ALU.add)
                    one = const("cmp_one")[:, m * NB:(m + 1) * NB]
                    V.tensor_tensor(pc[:, m].rearrange("p g (j k) -> p (g j) k", k=32)[:, :, 0:NB], cs[:, m],
                                    shape(one.unsqueeze(1), P, NH, NB), ALU.mult).then_inc(S["pc_ready"], 1)
                dve.wait_ge(S["pc_ready"], 2)
                mask(1)
                for m in range(MT):
                    dve.wait_ge(S["cmp_out"], m + 1)
                    take(m + 1, 0, m, B[2 + m], True)
                mask(2)
                dve.wait_ge(S["weighed"], sum(GROUPS[:1]))
                take(3, 1, 0, B[2], False)
                mask(3)
                dve.wait_ge(S["weighed"], sum(GROUPS[:2]))
                take(4, 2, 0, B[3], False)
                finish(0)
                dve.wait_ge(S["th_ready"], CT)
                xt = xc[:, :, CONV_W - 1:]
                after(V.tensor_scalar(xt, tr, 1.0, None, ALU.add))
                after(V.reciprocal(xt, xt))
                V.tensor_tensor(tr, tr, xt, ALU.mult).then_inc(S["uq_in"], 1)
                dve.wait_ge(S["ti_ready"], CT)
                dve.wait_ge(S["lru_gates_done"], 4)
                after(V.scalar_tensor_tensor(cv, ti, 1.0, cv, ALU.add, ALU.mult))
                dve.wait_ge(S["uq_ready"], 1)
                after(V.tensor_tensor(cv, cv, tr, ALU.mult))
                for i in range(CT):
                    ins = V.tensor_tensor_scan(ti[:, i], aa[:, i], cv[:, i], 0.0, ALU.mult, ALU.add)
                after(ins)
                for i in range(CT):
                    V.scalar_tensor_tensor(cv[:, i], ti[:, i], 0.5, sgr[:, i], ALU.mult, ALU.mult).then_inc(S["ya_ready"], 1)
                dve.wait_ge(S["weighed"], sum(GROUPS[:3]))
                take(5, 1, 1, B[2], False)
                dve.wait_ge(S["weighed"], sum(GROUPS[:4]))
                take(6, 2, 1, B[3], False)
                finish(1)
                for m in range(MT):
                    for h in range(2):
                        dve.wait_ge(S["out_done"], 2 * m + h + 1)
                        x = X[:, m * D + h * 512:m * D + (h + 1) * 512]
                        V.tensor_tensor(x, x, B[4 + 2 * m + h][:, :], ALU.add).then_inc(S["x_added"], 1)
                dve.wait_ge(S["x_added"], 2 * MT)
                dve.drain()
                dve.wait_ge(arrived, 4)
                dve.sem_clear(layer_sems)
                dve.sem_clear(arrived)
                for r in release.values():
                    dve.sem_inc(r, 1)


def log1p_of(V, after, w):
    after(V.tensor_scalar(w[:, 2], w[:, 1], 2.0, None, ALU.add))
    after(V.reciprocal(w[:, 3], w[:, 2]))
    after(V.tensor_tensor(w[:, 4], w[:, 1], w[:, 3], ALU.mult))
    after(V.tensor_tensor(w[:, 5], w[:, 4], w[:, 4], ALU.mult))
    after(V.tensor_scalar(w[:, 6], w[:, 5], 1.0 / 17, None, ALU.mult))
    for k in range(15, 1, -2):
        after(V.scalar_tensor_tensor(w[:, 6], w[:, 6], 1.0 / k, w[:, 5], ALU.add, ALU.mult))
    after(V.scalar_tensor_tensor(w[:, 8], w[:, 6], 1.0, w[:, 4], ALU.add, ALU.mult))


ROW_MU, ROW_W0, ROW_A0, ROW_KK, ROW_KA, ROW_RK, NROWS2 = 0, 14, 18, 22, 26, 30, 34
LORA = 64
RW = 512
COL2_R, COL2_PW, COL2_K, COL2_V, COL2_PA = 0, RW, RW + LORA, 2 * RW + LORA, 3 * RW + LORA
COL2_FQ = COL2_PA + LORA + P
COL2_FK, COL2_FV, COL2_F = COL2_FQ + 512, COL2_FQ + 1024, COL2_FQ + 1536
N_IN2 = COL2_F + NH
LORA_W = 2 * LORA + P + NH
FQ_S, FK_S, FV_S, LORA_S, R_S, K_S, V_S, WO2_S = 0, 4, 5, 1, 2, 3, 0, (2, 3)
DECAY = float(np.exp(np.float32(-0.5)))
NTILE = 14


def load_mixer_weights(sp, a, slot, loaded, name):
    win = a["w_in_2"]

    def load(s, at, cols, width):
        dst = slot[:, s, 0:KC * width].rearrange("p (c n) -> p c n", c=KC)[:, :, at:at + cols[1] - cols[0]]
        sp.dma_start(dst, win[0, :, cols[0]:cols[1]].rearrange("(p c) n -> p c n", c=KC)).then_inc(loaded[s], 16)

    wide = {"fq": (FQ_S, COL2_FQ), "fk": (FK_S, COL2_FK), "fv": (FV_S, COL2_FV), "r": (R_S, COL2_R), "k": (K_S, COL2_K), "v": (V_S, COL2_V)}
    if name == "lora":
        load(LORA_S, 0, (COL2_PW, COL2_PW + LORA), LORA_W)
        load(LORA_S, LORA, (COL2_PA, COL2_FQ), LORA_W)
        load(LORA_S, 2 * LORA + P, (COL2_F, N_IN2), LORA_W)
    else:
        s, c = wide[name]
        load(s, 0, (c, c + 512), 512)


def mixer_part(nc, ctx, a, mem, psum, layout, first, second):
    slot, loaded = mem["slots"], mem["loaded"]
    X, XN, HT = mem["x"], mem["xn"], mem["ht"]
    B = psum
    room = carve(mem["region"])
    const2 = room(second - first)

    def const(name):
        at, w = layout[name]
        return const2[:, at - first:at - first + w] if at >= first else mem["const"][:, at:at + w]

    ident = const("ident")
    rows, params = room(P), room(NROWS2)
    norm_g = room(KC)
    gain, b_f = room(2, HD), room(NH)
    lora_w, g2 = room(RW), room(RW)
    ln_w, ln_b = room(RW), room(RW)
    ss, rstd = room(MT), room(MT)
    ssq, rsq = room(MT * 2 * NH), room(MT * 2 * NH)
    half_b = room(2, CT)
    f8, wk = room(MT * NH), room(9, MT * NH)
    rowmax, negmax, den = room(2, NH), room(2, NH), room(2, NH)
    rden = room(NH)
    bonus = room(MT, NH)
    last = room(CT, T // CHUNK)
    mean, var, rvar = room(MT * NH), room(MT * NH), room(MT * NH)
    raw_flat = room(NTILE * (T + 1))
    raw = view(raw_flat, NTILE, T + 1)
    ps = room(NTILE, T)
    r_, k_, v_ = ps[:, 0:4], ps[:, 4:8], ps[:, 8:12]
    aa, gt, ld, kk = room(CT, T), room(CT, T), room(CT, T), room(CT, T)
    qk_flat, v2 = room(MT * 2 * NH * HD), room(MT, NH * HD)
    qk = view(qk_flat, MT, 2 * NH, HD)
    yft = room(4, T)
    ht = view(HT[:, :], KC, T)
    lc, ex, ei = [view(raw_flat[:, i * CT * T:(i + 1) * CT * T], CT, T) for i in range(3)]
    room45 = carve(slot[:, 4:6].rearrange("p s n -> p (s n)"))
    qt, kt = room45(4, T), room45(4, T)
    pt = room45(4, 4, P)
    sqk = room45(MT * 2 * NH, HD)
    yf = view(pt.rearrange("p a b t -> p (a b t)")[:, 0:MT * RW], MT, RW)
    prob = [view(qk_flat[:, 0:NH * P], NH, P), view(XN[:, :], NH, T)]
    room45 = carve(slot[:, 4:6].rearrange("p s n -> p (s n)"))
    am, wu = room45(MT, NH, P), room45(MT, NH, P)
    rbt, rkt = room45(MT, NH, P), room45(MT, NH, P)
    room01 = carve(slot[:, 0:2].rearrange("p s n -> p (s n)"))
    btok, ktok, vtok = room01(MT, RW), room01(MT, RW), room01(MT, RW)
    wt = room01(MT, CT, P)
    rk = room01(CT, T)
    state = room01(T // CHUNK + 1, CT, HD)
    chunks = [view(XN[:, :], 4, 2, CT, HD), view(HT[:, :], 4, 2, CT, HD)]
    flats = [qk_flat, v2.rearrange("p m n -> p (m n)")] + [t.rearrange("p i t -> p (i t)") for t in (lc, kk, ex, ei)]
    units = [view(f[:, i:i + 512], 4, P) for f in flats for i in range(0, f.shape[1], 512)]
    W = []
    for u in range(2):
        w = dict(zip(("NT", "N", "NO", "F", "AKT", "P2", "P2T"), units[7 * u:7 * u + 7]))
        w.update(P4=w["NT"], P4T=w["N"], P8=w["P2"], XD=w["P2T"], Q=w["AKT"])
        W.append(w)
    yr, yrt = view(ex.rearrange("p i t -> p (i t)"), MT * NH, HD), ei
    ysq = lc.rearrange("p i t -> p (i t)")

    names = """small_in const2_in ss_ready rstd_ready xn_ready params_transposed params_ready h_transposed ht_ready
        fq_done fk_done fv_done f_done lora_done rkv_done raw_ready qkv_copied f_ready f_abs f_exp qk_ss qk_rstd qk_ready
        qk_transposed qkt_ready scores masked exp_done p_transposed pt_ready weighed yf_ready yf_transposed yft_ready
        shifted lora_in lora_mul lora_tanh gates_ready kk_sq kk_sum kk_root kk_ready lc_ready decays_ready
        scaled tok_transposed tok_ready bonus_done bonus_ready unit_made unit_taken chunk_made chunk_taken
        state_made state_ready sa_made sa_ready y_made y_taken y_var y_rstd y_ready y_transposed yrt_ready
        out_done x_added dve_step pool_step act_step""".split()
    S, mixer_sems = semaphores(nc, ctx, names, "_2")
    GROUPS = [2, 4]
    NCH = T // CHUNK
    STAGES = "NT N AKT RBT RKT P2 P2T MV P4 P4T F2 P8 F3 F4 XD Q F5 WU WT".split()

    def order(m, u, stage):
        return (m * len(STAGES) + STAGES.index(stage)) * 2 + u

    def score_out(m, h):
        i, u = divmod(h, 2)
        return B[2 + u][:, i * P:(i + 1) * P] if m == 0 else B[4 + 2 * u + i // 2][:, i % 2 * T:(i % 2 + 1) * T]

    def pairs(m, g):
        return [((4 * g + b) // (m + 1), (4 * g + b) % (m + 1)) for b in range(4)]

    n_small = 0
    with nc.Block() as block:

        @block.sync
        def _(sp):
            sp.wait_ge(S["fq_done"], MT)
            load_mixer_weights(sp, a, slot, loaded, "v")
            wout = a["w_out_2"]
            for h in range(2):
                sp.wait_ge(S["rkv_done"], 2 * (h + 1))
                dst = slot[:, WO2_S[h], :].rearrange("p (k n) -> p k n", k=KC)
                sp.dma_start(dst, wout[0, :, h * 512:(h + 1) * 512].rearrange("(k p) n -> p k n", p=P)).then_inc(loaded[WO2_S[h]], 16)
            sp.wait_ge(S["y_ready"], 1)
            load_first_experts(sp, a, mem, False)

        @block.gpsimd
        def _(pool):
            pool.wait_ge(S["ss_ready"], MT)
            nc.gpsimd.memset(raw[:, :, 0:1], 0.0).then_inc(S["pool_step"], 1)
            steps = [1]

            def inv_root(out, src, scale, eps, ready, n, done):
                pool.wait_ge(ready, n)
                nc.gpsimd.tensor_scalar(out, src, scale, eps, ALU.mult, ALU.add).then_inc(S["pool_step"], 1)
                steps[0] += 1
                pool.wait_ge(S["pool_step"], steps[0])
                nc.gpsimd.tensor_tensor(out, out, const("minus_half")[0:out.shape[0], 0:out.shape[1]], ALU.pow).then_inc(done, 1)

            inv_root(rstd, ss, 1.0 / D, EPS, S["ss_ready"], MT, S["rstd_ready"])
            inv_root(rsq, ssq, 1.0 / HD, EPS, S["qk_ss"], 1, S["qk_rstd"])
            inv_root(rvar, var, 1.0 / HD, 64e-5, S["y_var"], 1, S["y_rstd"])

        @block.scalar
        def _(act):
            n = [0]

            def small(dst, src):
                act.dma_start(dst, src).then_inc(S["small_in"], 16)
                n[0] += 1

            act.dma_start(const2, a["constants"][:, first:first + const2.shape[1]]).then_inc(S["const2_in"], 16)
            mu = a["mu_shift_2"]
            for t, c in ((0, COL2_R), (4, COL2_K), (8, COL2_V)):
                small(rows[t:t + 4], mu[0, c:c + RW].rearrange("(i p) -> i p", p=P))
            small(rows[12:13, 0:LORA], mu[0:1, COL2_PW:COL2_PW + LORA])
            small(rows[12:13, LORA:P], mu[0:1, COL2_PA:COL2_PA + LORA])
            small(rows[13:14], mu[0:1, COL2_PA + LORA:COL2_FQ])
            for r, name in ((ROW_W0, "rw_w0_2"), (ROW_A0, "rw_a0_2"), (ROW_KK, "rw_k_k_2"), (ROW_KA, "rw_k_a_2")):
                small(rows[r:r + 4], a[name][0].rearrange("(i p) -> i p", p=P))
            small(rows[ROW_RK:ROW_RK + 4], a["rw_r_k_2"][0].rearrange("(i u) d -> i (u d)", u=2))
            small(norm_g, a["norm_mix_w_2"][0].rearrange("(p c) -> p c", c=KC))
            small(gain[:, 0], shape(a["fox_q_norm_w_2"], P, HD))
            small(gain[:, 1], shape(a["fox_k_norm_w_2"], P, HD))
            small(b_f, shape(a["fox_b_f_2"], P, NH))
            small(lora_w[0:LORA], a["rw_w2_2"][0])
            small(lora_w[LORA:P], a["rw_a2_2"][0])
            small(g2, a["rw_g2_2"][0])
            small(ln_w, shape(a["rw_ln_w_2"], P, RW))
            small(ln_b, shape(a["rw_ln_b_2"], P, RW))
            assert n[0] == N_SMALL2
            for m in range(MT):
                nc.scalar.activation(raw_flat[:, m * D:(m + 1) * D], X[:, m * D:(m + 1) * D], ACT.Square,
                                     accum_out=ss[:, m:m + 1]).then_inc(S["ss_ready"], 1)
            act.wait_ge(S["params_transposed"], 1)
            nc.scalar.copy(params, B[7][:, 0:NROWS2]).then_inc(S["params_ready"], 1)
            act.wait_ge(S["params_ready"], 1)
            nc.scalar.mul(half_b.rearrange("p a b -> p (a b)"), params[:, ROW_W0:ROW_KK], 0.5).then_inc(S["params_ready"], 1)
            for m in range(MT):
                act.wait_ge(S["fq_done"], m + 1)
                nc.scalar.copy(qk[:, m, 0:NH], view(B[4 + m][:, :], NH, HD)).then_inc(S["qkv_copied"], 1)
            for m in range(MT):
                act.wait_ge(S["fk_done"], m + 1)
                nc.scalar.copy(qk[:, m, NH:], view(B[6 + m][:, :], NH, HD)).then_inc(S["qkv_copied"], 1)
            for m in range(MT):
                act.wait_ge(S["fv_done"], m + 1)
                nc.scalar.copy(v2[:, m], B[m][:, :]).then_inc(S["qkv_copied"], 1)
            act.wait_ge(S["f_abs"], 1)
            nc.scalar.activation(wk[:, 1], wk[:, 0], ACT.Exp, scale=-1.0).then_inc(S["f_exp"], 1)
            act.wait_ge(S["pool_step"], 1)
            act.wait_ge(S["lora_done"], 1)
            nc.scalar.copy(raw[:, 12:14, 1:], view(B[3][:, :], 2, T)).then_inc(S["raw_ready"], 1)
            for b in range(4):
                act.wait_ge(S["rkv_done"], b + 1)
                nc.scalar.copy(raw[:, 2 * b:2 * b + 2, 1:], view(B[b][:, :], 2, T)).then_inc(S["raw_ready"], 1)
            for m in range(MT):
                act.wait_ge(S["qk_transposed"], m + 1)
                nc.scalar.copy(qt[:, :, m * P:(m + 1) * P], view(B[4 + 2 * m][:, :], 4, P)).then_inc(S["qkt_ready"], 1)
                nc.scalar.copy(kt[:, :, m * P:(m + 1) * P], view(B[5 + 2 * m][:, :], 4, P)).then_inc(S["qkt_ready"], 1)
            for b in range(2):
                act.wait_ge(S["rkv_done"], 5 + b)
                nc.scalar.copy(raw[:, 8 + 2 * b:10 + 2 * b, 1:], view(B[b][:, :], 2, T)).then_inc(S["raw_ready"], 1)
            for m in range(MT):
                act.wait_ge(S["masked"], m + 1)
                for h in range(NH):
                    p = prob[m][:, h]
                    nc.scalar.activation(p, p, ACT.Exp, bias=negmax[:, m, h:h + 1], scale=SCALE,
                                         accum_out=den[:, m, h:h + 1]).then_inc(S["exp_done"], 1)
                for g in range(GROUPS[m]):
                    k = sum(GROUPS[:m]) + g
                    if k >= 4:
                        act.wait_ge(S["weighed"], k - 3)
                    act.wait_ge(S["p_transposed"], k + 1)
                    nc.scalar.copy(pt[:, k % 4], view(B[k % 2][:, :], 4, P)).then_inc(S["pt_ready"], 1)
            act.wait_ge(S["shifted"], NTILE)
            nc.scalar.activation(ps[0:LORA, 12], ps[0:LORA, 12], ACT.Tanh).then_inc(S["lora_in"], 1)
            nc.scalar.activation(ps[:, 13], ps[:, 13], ACT.Tanh, scale=0.5).then_inc(S["lora_in"], 1)
            for m in range(MT):
                act.wait_ge(S["yf_transposed"], m + 1)
                nc.scalar.copy(yft[:, :, m * P:(m + 1) * P], view(B[4 + m][:, :], 4, P)).then_inc(S["yft_ready"], 1)
            act.wait_ge(S["params_ready"], 2)
            for g, out in enumerate((ld, aa)):
                for i in range(CT):
                    if i % 2 == 0:
                        act.wait_ge(S["lora_mul"], 2 * g + i // 2 + 1)
                    bank = B[(6, 7, 0, 1)[2 * g + i // 2]]
                    nc.scalar.activation(out[:, i], bank[:, i % 2 * T:(i % 2 + 1) * T], ACT.Tanh, bias=half_b[:, g, i:i + 1],
                                         scale=0.5).then_inc(S["lora_tanh"], 1)
            for b in range(2):
                act.wait_ge(S["lora_mul"], 5 + b)
                nc.scalar.copy(gt[:, 2 * b:2 * b + 2], view(B[2 + b][:, :], 2, T)).then_inc(S["gates_ready"], 1)
            for b in range(2):
                act.wait_ge(S["kk_sum"], b + 1)
                nc.scalar.activation(lc[:, 2 * b:2 * b + 2], view(B[4 + b][:, :], 2, T), ACT.Sqrt).then_inc(S["kk_root"], 1)
            act.wait_ge(S["lc_ready"], 1)
            nc.scalar.activation(ex, lc, ACT.Exp).then_inc(S["decays_ready"], 1)
            nc.scalar.activation(ei, lc, ACT.Exp, scale=-1.0).then_inc(S["decays_ready"], 1)
            act.wait_ge(S["lc_ready"], 2)
            nc.scalar.activation(ld, ld, ACT.Exp).then_inc(S["decays_ready"], 1)
            for m in range(MT):
                act.wait_ge(S["tok_transposed"], m + 1)
                nc.scalar.copy(vtok[:, m], B[m][:, :]).then_inc(S["tok_ready"], 1)
            for m in range(MT):
                act.wait_ge(S["tok_transposed"], 2 + m + 1)
                nc.scalar.copy(am[:, m, :, 0:HD], view(B[2 + m][:, :], NH, HD)).then_inc(S["tok_ready"], 1)
            for j, dst in enumerate((btok, ktok)):
                for m in range(MT):
                    act.wait_ge(S["tok_transposed"], 4 + 2 * j + m + 1)
                    nc.scalar.copy(dst[:, m], B[4 + 2 * j + m][:, :]).then_inc(S["tok_ready"], 1)
            act.wait_ge(S["bonus_done"], 1)
            nc.scalar.copy(bonus.rearrange("p m h -> p (m h)"), B[0][:, 0:MT * NH]).then_inc(S["bonus_ready"], 1)
            for q in range(NCH):
                m, c = divmod(q, 4)
                act.wait_ge(S["chunk_made"], q + 1)
                nc.scalar.copy(chunks[m][:, c].rearrange("p x i k -> p (x i k)"), B[q % 8][:, :]).then_inc(S["chunk_taken"], 1)

        @block.tensor
        def _(pe):
            pe.wait_ge(S["small_in"], 16 * N_SMALL2)
            pe.wait_ge(S["const2_in"], 16)
            nc.tensor.transpose(B[7][:, 0:NROWS2], rows[0:NROWS2], ident[0:NROWS2, 0:NROWS2]).then_inc(S["params_transposed"], 1)
            for m in range(MT):
                pe.wait_ge(S["xn_ready"], m + 1)
                xn = XN[:, m * D:(m + 1) * D].rearrange("p (k c) -> p k c", c=KC)
                for c in range(KC):
                    t = nc.tensor.transpose(B[2 * m + c // 4][:, c % 4 * P:(c % 4 + 1) * P], xn[:, :, c], ident)
                    if c % 4 == 3:
                        t.then_inc(S["h_transposed"], 1)

            def chunk(s, width=512):
                return slot[:, s, 0:KC * width].rearrange("p (c n) -> p c n", c=KC)

            def tokens(m, out, w, cols):
                for c in range(KC):
                    mm = nc.tensor.matmul(out, ht[:, c, m * P:(m + 1) * P], w[:, c, cols], start=c == 0, stop=c == KC - 1)
                return mm

            def features(out, w, cols):
                for c in range(KC):
                    mm = nc.tensor.matmul(out, w[:, c, cols], ht[:, c, :], start=c == 0, stop=c == KC - 1)
                return mm

            for s, uses, bank, done in ((FQ_S, 1, 4, S["fq_done"]), (FK_S, 0, 6, S["fk_done"]), (FV_S, 1, 0, S["fv_done"])):
                pe.wait_ge(loaded[s], 16 * (DEPTH * uses + 1))
                for m in range(MT):
                    pe.wait_ge(S["ht_ready"], 2 * (m + 1) if s != FV_S else 4)
                    if bank + m == 7:
                        pe.wait_ge(S["params_ready"], 1)
                    tokens(m, B[bank + m][:, :], chunk(s), slice(0, 512)).then_inc(done, 1)
            pe.wait_ge(loaded[LORA_S], 16 * (DEPTH * 2 + 3))
            w = chunk(LORA_S, LORA_W)
            for m in range(MT):
                mm = tokens(m, B[2][:, m * NH:(m + 1) * NH], w, slice(2 * LORA + P, LORA_W))
            mm.then_inc(S["f_done"], 1)
            features(B[3][:, 0:T], w, slice(0, P))
            features(B[3][:, T:], w, slice(P, 2 * P)).then_inc(S["lora_done"], 1)
            pe.wait_ge(S["qkv_copied"], 6)
            for b in range(4):
                if b == 0:
                    pe.wait_ge(loaded[R_S], 16 * (DEPTH * 2 + 1))
                if b == 2:
                    pe.wait_ge(loaded[K_S], 16 * (DEPTH * 2 + 1))
                    pe.wait_ge(S["f_ready"], 1)
                    pe.wait_ge(S["raw_ready"], 1)
                for i in range(2):
                    mm = features(B[b][:, i * T:(i + 1) * T], chunk((R_S, K_S)[b // 2]), slice((2 * b % 4 + i) * P, (2 * b % 4 + i + 1) * P))
                mm.then_inc(S["rkv_done"], 1)
            pe.wait_ge(S["qk_ready"], 1)
            for m in range(MT):
                for j in range(2):
                    for i in range(4):
                        at = j * NH + 2 * i
                        t = nc.tensor.transpose(B[4 + 2 * m + j][:, i * P:(i + 1) * P], qk[:, m, at:at + 2].rearrange("p u d -> p (u d)"), ident)
                t.then_inc(S["qk_transposed"], 1)
            pe.wait_ge(loaded[V_S], 16 * (DEPTH + 2))
            pe.wait_ge(S["raw_ready"], 3)
            for b in range(2):
                for i in range(2):
                    mm = features(B[b][:, i * T:(i + 1) * T], chunk(V_S), slice((2 * b + i) * P, (2 * b + i + 1) * P))
                mm.then_inc(S["rkv_done"], 1)
            pe.wait_ge(S["raw_ready"], 5)
            pe.wait_ge(S["f_ready"], 2)
            upto = const("upto")
            for m in range(MT):
                pe.wait_ge(S["qkt_ready"], 2 if m == 0 else 4)
                for i in range(4):
                    for u in range(2):
                        h = 2 * i + u
                        out = score_out(m, h)
                        lf = lambda s: shape(f8[:, s * NH + h:s * NH + h + 1], P, P)
                        nc.tensor.matmul(out, lf(0), upto[:, 0:(m + 1) * P], start=True, stop=False)
                        if m:
                            nc.tensor.matmul(out[:, P:T], lf(1), upto[:, 0:P], start=False, stop=False)
                        r = slice(64 * u, 64 * u + 64)
                        mm = nc.tensor.matmul(out, qt[r, i, m * P:(m + 1) * P], kt[r, i, 0:(m + 1) * P], start=False, stop=True)
                mm.then_inc(S["scores"], 1)
            for m in range(MT):
                pe.wait_ge(S["exp_done"], NH * (m + 1))
                if m == 0:
                    pe.wait_ge(S["raw_ready"], 7)
                    pe.wait_ge(S["masked"], 1)
                base = sum(GROUPS[:m])

                def weigh(g):
                    pe.wait_ge(S["pt_ready"], base + g + 1)
                    for b, (h, key) in enumerate(pairs(m, g)):
                        mm = nc.tensor.matmul(B[2 + m][:, h * HD:(h + 1) * HD], pt[:, (base + g) % 4, b], v2[:, key, h * HD:(h + 1) * HD],
                                              start=key == 0, stop=key == m)
                    mm.then_inc(S["weighed"], 1)

                for g in range(GROUPS[m]):
                    if base + g >= 2:
                        pe.wait_ge(S["pt_ready"], base + g - 1)
                    for b, (h, key) in enumerate(pairs(m, g)):
                        t = nc.tensor.transpose(B[(base + g) % 2][:, b * P:(b + 1) * P], prob[m][:, h, key * P:(key + 1) * P], ident)
                    t.then_inc(S["p_transposed"], 1)
                    if g:
                        weigh(g - 1)
                weigh(GROUPS[m] - 1)
            pe.wait_ge(S["masked"], 2)
            for m in range(MT):
                pe.wait_ge(S["yf_ready"], m + 1)
                for k in range(4):
                    t = nc.tensor.transpose(B[4 + m][:, k * P:(k + 1) * P], yf[:, m, k * P:(k + 1) * P], ident)
                t.then_inc(S["yf_transposed"], 1)
            pe.wait_ge(S["lora_in"], 3)
            for g in range(3):
                r = (slice(0, LORA), slice(LORA, P), slice(0, P))[g]
                w = (lora_w, lora_w, g2)[g]
                for i in range(CT):
                    bank = B[(6, 7, 0, 1, 2, 3)[2 * g + i // 2]]
                    mm = nc.tensor.matmul(bank[:, i % 2 * T:(i % 2 + 1) * T], w[r, i * P:(i + 1) * P], ps[r, 12 + (g == 2)], start=True, stop=True)
                    if i % 2:
                        mm.then_inc(S["lora_mul"], 1)
            pe.wait_ge(S["kk_sq"], 1)
            pe.wait_ge(S["yft_ready"], 2)
            for i in range(CT):
                mm = nc.tensor.matmul(B[4 + i // 2][:, i % 2 * T:(i % 2 + 1) * T], const("head_ones"), lc[:, i], start=True, stop=True)
                if i % 2:
                    mm.then_inc(S["kk_sum"], 1)
            for j, (src, n) in enumerate(((v_, 0), (ld, 1), (ex, 3), (ei, 4))):
                for m in range(MT):
                    if j == 0:
                        pe.wait_ge(S["lora_tanh"], 8)
                    if j == 1:
                        pe.wait_ge(S["gates_ready"], 2)
                    if j == 2:
                        pe.wait_ge(S["kk_root"], 2)
                    if n:
                        pe.wait_ge(S["scaled"], n)
                    for i in range(CT):
                        t = nc.tensor.transpose(B[2 * j + m][:, i * P:(i + 1) * P], src[:, i, m * P:(m + 1) * P], ident)
                    t.then_inc(S["tok_transposed"], 1)
            pe.wait_ge(S["tok_ready"], 1)
            for m in range(MT):
                for i in range(CT):
                    at = m * NH + 2 * i
                    mm = nc.tensor.matmul(B[0][:, at:at + 2], rk[:, i, m * P:(m + 1) * P], const("head_pick"), start=True, stop=True)
            mm.then_inc(S["bonus_done"], 1)
            pe.wait_ge(S["tok_ready"], 8)
            pe.wait_ge(S["bonus_ready"], 1)

            def unit(m, u, stage, operands, width=P, rows_out=slice(0, P), transpose=False):
                k = order(m, u, stage)
                if k >= 8:
                    pe.wait_ge(S["unit_taken"], k - 7)
                for i in range(CT):
                    left, right = operands(i)
                    out = B[k % 8][rows_out, i * width:(i + 1) * width]
                    mm = nc.tensor.transpose(out, left, ident) if transpose else nc.tensor.matmul(out, left, right, start=True, stop=True)
                mm.then_inc(S["unit_made"], 1)

            for m in range(MT):
                tile = slice(m * P, (m + 1) * P)
                row = [slice(64 * u, 64 * u + 64) for u in range(2)]
                for u in range(2):
                    unit(m, u, "NT", lambda i: (aa[row[u], i, tile], ld[row[u], i, tile]))
                for u in range(2):
                    unit(m, u, "N", lambda i: (ld[row[u], i, tile], aa[row[u], i, tile]))
                for u in range(2):
                    unit(m, u, "AKT", lambda i: (k_[row[u], i, tile], ld[row[u], i, tile]))
                for u in range(2):
                    unit(m, u, "RBT", lambda i: (aa[row[u], i, tile], r_[row[u], i, tile]))
                for u in range(2):
                    unit(m, u, "RKT", lambda i: (k_[row[u], i, tile], r_[row[u], i, tile]))

                def step(stage, needs, operands, **kw):
                    for u in range(2):
                        pe.wait_ge(S["unit_taken"], max(order(m, u, n) for n in needs) + 1)
                        unit(m, u, stage, lambda i: operands(W[u], u, i), **kw)

                step("P2", ("NT", "N"), lambda w, u, i: (w["NT"][:, i], w["N"][:, i]))
                step("P2T", ("NT", "N"), lambda w, u, i: (w["N"][:, i], w["NT"][:, i]))
                step("MV", ("AKT",), lambda w, u, i: (w["AKT"][:, i], vtok[:, m, (2 * i + u) * HD:(2 * i + u + 1) * HD]), width=HD)
                step("P4", ("P2", "P2T"), lambda w, u, i: (w["P2T"][:, i], w["P2"][:, i]))
                step("P4T", ("P2", "P2T"), lambda w, u, i: (w["P2"][:, i], w["P2T"][:, i]))
                step("F2", ("P2", "NT"), lambda w, u, i: (w["P2"][:, i], w["F"][:, i]))
                step("P8", ("P4", "P4T"), lambda w, u, i: (w["P4T"][:, i], w["P4"][:, i]))
                step("F3", ("P4", "F2"), lambda w, u, i: (w["P4"][:, i], w["F"][:, i]))
                step("F4", ("P8", "F3"), lambda w, u, i: (w["P8"][:, i], w["F"][:, i]))
                step("XD", ("F4",), lambda w, u, i: (w["F"][:, i], None), transpose=True)
                step("Q", ("F4", "N"), lambda w, u, i: (w["NO"][:, i], w["F"][:, i]))
                step("F5", ("XD", "Q"), lambda w, u, i: (w["XD"][:, i], w["Q"][:, i]))
                step("WU", ("F5", "MV"), lambda w, u, i: (w["F"][:, i], am[:, m, 2 * i + u]))
                for u in range(2):
                    unit(m, u, "WT", lambda i: (am[:, m, 2 * i + u, 0:HD], W[u]["F"][:, i]), rows_out=row[u])
            for q in range(NCH):
                m, c = divmod(q, 4)
                if q == 0:
                    pe.wait_ge(S["unit_taken"], order(MT - 1, 1, "WT") + 1)
                s = slice(CHUNK * c, CHUNK * (c + 1))
                for i in range(CT):
                    for u in range(2):
                        h = 2 * i + u
                        cols = slice(h * HD, (h + 1) * HD)
                        out = B[q % 8][64 * u:64 * u + 64, :]
                        g_out, h_out = out[:, i * HD:(i + 1) * HD], out[:, 256 + i * HD:256 + (i + 1) * HD]
                        nc.tensor.matmul(g_out, wu[s, m, h, 0:HD], btok[s, m, cols], start=True, stop=True)
                        nc.tensor.matmul(h_out, btok[s, m, cols], wu[s, m, h, HD:P], start=True, stop=False)
                        mm = nc.tensor.matmul(h_out, ktok[s, m, cols], vtok[s, m, cols], start=False, stop=True)
                mm.then_inc(S["chunk_made"], 1)
            for q in range(NCH):
                m, c = divmod(q, 4)
                pe.wait_ge(S["chunk_taken"], NCH)
                pe.wait_ge(S["state_ready"], 2 * q + 1)
                for u in range(2):
                    r = slice(64 * u, 64 * u + 64)
                    for i in range(CT):
                        mm = nc.tensor.matmul(B[u][r, i * HD:(i + 1) * HD], chunks[m][r, c, 0, i], state[r, q, i], start=True, stop=True)
                mm.then_inc(S["state_made"], 1)
            pe.wait_ge(S["state_ready"], 2 * NCH - 1)
            for m in range(MT):
                for u in range(2):
                    r = slice(64 * u, 64 * u + 64)
                    for i in range(CT):
                        for c in range(4):
                            mm = nc.tensor.matmul(B[2 + 2 * m + u][CHUNK * c:CHUNK * (c + 1), i * HD:(i + 1) * HD],
                                                  wt[r, m, i, CHUNK * c:CHUNK * (c + 1)], state[r, 4 * m + c, i], start=True, stop=True)
                    mm.then_inc(S["sa_made"], 1)
            for m in range(MT):
                for u in range(2):
                    bank = B[(6, 7, 0, 1)[2 * m + u]]
                    pe.wait_ge(S["sa_ready"], 2 * m + u + 1)
                    pe.wait_ge(S["state_ready"], 2 * NCH)
                    r = slice(64 * u, 64 * u + 64)
                    for i in range(CT):
                        h = 2 * i + u
                        out = bank[:, i * HD:(i + 1) * HD]
                        nc.tensor.matmul(out, rkt[:, m, h], vtok[:, m, h * HD:(h + 1) * HD], start=i == 0, stop=False, skip_group_check=True)
                        nc.tensor.matmul(out, rbt[:, m, h], wu[:, m, h, HD:P], start=False, stop=False, skip_group_check=True)
                    for i in range(CT):
                        for c in range(4):
                            t = slice(m * P + CHUNK * c, m * P + CHUNK * (c + 1))
                            mm = nc.tensor.matmul(bank[CHUNK * c:CHUNK * (c + 1), i * HD:(i + 1) * HD], r_[r, i, t], state[r, 4 * m + c, i],
                                                  start=False, stop=True, skip_group_check=True)
                    mm.then_inc(S["y_made"], 1)
            pe.wait_ge(S["y_ready"], 1)
            pe.wait_ge(S["sa_ready"], 4)
            for m in range(MT):
                for k in range(4):
                    at = m * NH + 2 * k
                    t = nc.tensor.transpose(B[2 + m][:, k * P:(k + 1) * P], yr[:, at:at + 2].rearrange("p h d -> p (h d)"), ident)
                t.then_inc(S["y_transposed"], 1)
            pe.wait_ge(S["yrt_ready"], 2)
            for h in range(2):
                pe.wait_ge(loaded[WO2_S[h]], 16 * (DEPTH * 2 + 2))
            for m in range(MT):
                for h in range(2):
                    w = slot[:, WO2_S[h], :].rearrange("p (k n) -> p k n", k=KC)
                    for k in range(KC):
                        y = (yrt if k < 4 else yft)[:, k % 4, m * P:(m + 1) * P]
                        mm = nc.tensor.matmul(B[4 + 2 * m + h][:, :], y, w[:, k, :], start=k == 0, stop=k == KC - 1)
                    mm.then_inc(S["out_done"], 1)

        @block.vector
        def _(dve):
            V = nc.vector
            after = Chain(dve, S["dve_step"])
            dve.wait_ge(S["rstd_ready"], 1)
            for m in range(MT):
                V.tensor_scalar(XN[:, m * D:(m + 1) * D], X[:, m * D:(m + 1) * D], rstd[:, m:m + 1], None, ALU.mult).then_inc(S["xn_ready"], 1)
            dve.wait_ge(S["small_in"], 16 * N_SMALL2)
            dve.wait_ge(S["const2_in"], 16)
            for m in range(MT):
                for b in range(2):
                    dve.wait_ge(S["h_transposed"], 2 * m + b + 1)
                    V.tensor_tensor(ht[:, 4 * b:4 * b + 4, m * P:(m + 1) * P], view(B[2 * m + b][:, :], 4, P),
                                    shape(norm_g[:, 4 * b:4 * b + 4].unsqueeze(2), P, 4, P), ALU.mult).then_inc(S["ht_ready"], 1)
            dve.wait_ge(S["qkv_copied"], 4)
            flat = qk.rearrange("p m k d -> p (m k) d")
            dve.wait_ge(S["fv_done"], MT)
            dve.wait_ge(S["fk_done"], MT)
            after(V.tensor_tensor(sqk, flat, flat, ALU.mult))
            V.tensor_reduce(ssq, sqk, AX.X, ALU.add).then_inc(S["qk_ss"], 1)
            dve.wait_ge(S["f_done"], 1)
            V.tensor_tensor(view(wk[:, 2], MT, NH), view(B[2][:, 0:MT * NH], MT, NH), shape(b_f.unsqueeze(1), P, MT, NH), ALU.add)\
                .then_inc(S["f_ready"], 1)
            dve.wait_ge(S["f_ready"], 1)
            after(V.tensor_scalar(wk[:, 7], wk[:, 2], -1.0, 0.0, ALU.mult, ALU.max))
            V.scalar_tensor_tensor(wk[:, 0], wk[:, 7], 2.0, wk[:, 2], ALU.mult, ALU.add).then_inc(S["f_abs"], 1)
            dve.wait_ge(S["f_exp"], 1)
            log1p_of(V, after, wk)
            after(V.scalar_tensor_tensor(wk[:, 6], wk[:, 8], 2.0, wk[:, 7], ALU.mult, ALU.add))
            V.tensor_scalar(f8, wk[:, 6], 8.0, None, ALU.mult).then_inc(S["f_ready"], 1)
            dve.wait_ge(S["qk_rstd"], 1)
            after(V.tensor_tensor(flat, flat, shape(rsq.unsqueeze(2), P, MT * 2 * NH, HD), ALU.mult))
            for m in range(MT):
                g4 = view(qk_flat[:, m * 1024:(m + 1) * 1024], 2, NH, HD)
                ins = V.tensor_tensor(g4, g4, shape(gain.unsqueeze(2), P, 2, NH, HD), ALU.mult)
            ins.then_inc(S["qk_ready"], 1)

            def mask(m):
                dve.wait_ge(S["scores"], m + 1)
                for h in range(NH):
                    ins = V.tensor_tensor_reduce(out=prob[m][:, h], in0=score_out(m, h), in1=const("causal")[:, (1 - m) * P:], scale=1.0,
                                                 scalar=LOWEST, op0=ALU.add, op1=ALU.max, accum_out=rowmax[:, m, h:h + 1])
                after(ins)
                V.tensor_scalar(negmax[:, m], rowmax[:, m], -SCALE, None, ALU.mult).then_inc(S["masked"], 1)

            def shift(tiles, ready):
                dve.wait_ge(S["raw_ready"], ready)
                dve.wait_ge(S["params_ready"], 1)
                after(V.tensor_tensor(ps[:, tiles], raw[:, tiles, 0:T], raw[:, tiles, 1:], ALU.subtract))
                for i in range(tiles.start, tiles.stop):
                    V.scalar_tensor_tensor(ps[:, i], ps[:, i], params[:, ROW_MU + i:ROW_MU + i + 1], raw[:, i, 1:], ALU.mult, ALU.add)\
                        .then_inc(S["shifted"], 1)

            dve.wait_ge(S["qk_transposed"], 2)
            mask(0)
            mask(1)
            shift(slice(12, 14), 1)
            shift(slice(0, 8), 5)
            shift(slice(8, 12), 7)
            dve.wait_ge(S["lora_in"], 2)
            V.tensor_scalar(ps[:, 13], ps[:, 13], 0.5, 0.5, ALU.mult, ALU.add).then_inc(S["lora_in"], 1)
            for m in range(MT):
                dve.wait_ge(S["weighed"], sum(GROUPS[:m + 1]))
                if m == 0:
                    dve.wait_ge(S["weighed"], sum(GROUPS))
                after(V.reciprocal(rden, den[:, m]))
                V.tensor_tensor(view(yf[:, m], NH, HD), view(B[2 + m][:, :], NH, HD), shape(rden.unsqueeze(2), P, NH, HD), ALU.mult)\
                    .then_inc(S["yf_ready"], 1)
                dve.wait_ge(S["yf_ready"], m + 1)
            prm = lambda row, i: params[:, row + i:row + i + 1]
            dve.wait_ge(S["shifted"], NTILE)
            for i in range(CT):
                ins = V.tensor_scalar(kk[:, i], k_[:, i], prm(ROW_KK, i), None, ALU.mult)
            after(ins)
            V.tensor_tensor(lc, kk, kk, ALU.mult).then_inc(S["kk_sq"], 1)
            dve.wait_ge(S["lora_tanh"], 8)
            after(V.tensor_scalar(ld, ld, 1.0, -DECAY / 2, ALU.add, ALU.mult))
            after(V.tensor_scalar(aa, aa, 0.5, 0.5, ALU.mult, ALU.add))
            dve.wait_ge(S["kk_root"], 2)
            after(V.tensor_scalar(lc, lc, 1e-12, None, ALU.max))
            after(V.reciprocal(lc, lc))
            after(V.tensor_tensor(kk, kk, lc, ALU.mult))
            for i in range(CT):
                ins = V.tensor_tensor_scan(lc[:, i], const("restart"), ld[:, i], 0.0, ALU.mult, ALU.add)
            ins.then_inc(S["lc_ready"], 1)
            dve.wait_ge(S["lc_ready"], 1)
            V.tensor_tensor(ld, lc, ld, ALU.subtract).then_inc(S["lc_ready"], 1)
            for i in range(CT):
                ins = V.tensor_scalar(rk[:, i], aa[:, i], 1.0, prm(ROW_KA, i), ALU.subtract, ALU.mult)
            after(ins)
            after(V.scalar_tensor_tensor(k_, rk, 1.0, k_, ALU.add, ALU.mult))
            for i in range(CT):
                ins = V.scalar_tensor_tensor(rk[:, i], r_[:, i], prm(ROW_RK, i), k_[:, i], ALU.mult, ALU.mult)
            after(ins)
            dve.wait_ge(S["decays_ready"], 3)
            V.scalar_tensor_tensor(ld, kk, -1.0, ld, ALU.mult, ALU.mult).then_inc(S["scaled"], 1)
            ends = lambda t: t.rearrange("p i (q s) -> p (i q) s", s=CHUNK)
            V.tensor_copy(last.rearrange("p i q -> p (i q)"), ends(ex)[:, :, CHUNK - 1])
            V.tensor_tensor(aa, aa, kk, ALU.mult)
            V.tensor_tensor(r_, r_, ex, ALU.mult).then_inc(S["scaled"], 1)
            dve.wait_ge(S["scaled"], 2)
            after(V.tensor_tensor(aa, aa, ei, ALU.mult))
            by = shape(last.rearrange("p i q -> p (i q)").unsqueeze(2), P, CT * NCH, CHUNK)
            V.tensor_tensor(ends(ex), ends(aa), by, ALU.mult).then_inc(S["scaled"], 1)
            after(V.tensor_tensor(k_, k_, ei, ALU.mult))
            V.tensor_tensor(ends(ei), ends(k_), by, ALU.mult).then_inc(S["scaled"], 1)

            def take(m, u, stage):
                dve.wait_ge(S["unit_made"], order(m, u, stage) + 1)
                return view(B[order(m, u, stage) % 8][:, :], CT, P)

            def masked_copy(out, bank, name):
                return V.tensor_tensor(out, bank, shape(const(name).unsqueeze(1), P, CT, P), ALU.mult)

            taken = [0]

            def end(ins):
                ins.then_inc(S["unit_taken"], 1)
                taken[0] += 1

            def settle():
                dve.wait_ge(S["unit_taken"], taken[0])

            for m in range(MT):
                for u in range(2):
                    bank = take(m, u, "NT")
                    end(masked_copy(W[u]["NT"], bank, "below_half_t"))
                settle()
                for u in range(2):
                    after(V.tensor_tensor(W[u]["F"], W[u]["NT"], shape(ident.unsqueeze(1), P, CT, P), ALU.add))
                for u in range(2):
                    bank = take(m, u, "N")
                    masked_copy(W[u]["NO"], bank, "across")
                    end(masked_copy(W[u]["N"], bank, "below_half"))
                for u in range(2):
                    end(masked_copy(W[u]["AKT"], take(m, u, "AKT"), "below_t"))
                heads = lambda t, u: t[:, m].rearrange("p (i u) t -> p u i t", u=2)[:, u]
                for name, out in (("RBT", rbt), ("RKT", rkt)):
                    for u in range(2):
                        end(masked_copy(heads(out, u), take(m, u, name), "upto_t"))
                for name in ("P2", "P2T"):
                    for u in range(2):
                        end(V.tensor_copy(W[u][name], take(m, u, name)))
                for u in range(2):
                    bank = B[order(m, u, "MV") % 8]
                    dve.wait_ge(S["unit_made"], order(m, u, "MV") + 1)
                    end(V.tensor_copy(heads(am, u)[:, :, HD:P], view(bank[:, 0:CT * HD], CT, HD)))
                for name in ("P4", "P4T"):
                    for u in range(2):
                        end(V.tensor_copy(W[u][name], take(m, u, name)))

                def add_f(stage):
                    for u in range(2):
                        settle()
                        end(V.tensor_tensor(W[u]["F"], W[u]["F"], take(m, u, stage), ALU.add))

                add_f("F2")
                for u in range(2):
                    end(V.tensor_copy(W[u]["P8"], take(m, u, "P8")))
                add_f("F3")
                add_f("F4")
                for u in range(2):
                    end(V.tensor_copy(W[u]["XD"], take(m, u, "XD")))
                for u in range(2):
                    end(V.tensor_copy(W[u]["Q"], take(m, u, "Q")))
                add_f("F5")
                for u in range(2):
                    end(V.tensor_copy(heads(wu, u), take(m, u, "WU")))
                for u in range(2):
                    r = slice(64 * u, 64 * u + 64)
                    end(V.tensor_copy(wt[r, m], take(m, u, "WT")[r]))
            settle()
            V.memset(state[:, 0], 0.0).then_inc(S["state_ready"], 1)
            dve.wait_ge(S["chunk_taken"], NCH)
            dve.wait_ge(S["state_ready"], 1)
            for q in range(NCH):
                m, c = divmod(q, 4)
                nxt = state[:, q + 1]
                pcq = shape(last[:, :, q:q + 1], P, CT, HD)
                after(V.tensor_tensor(nxt, state[:, q], pcq, ALU.mult))
                after(V.tensor_tensor(nxt, nxt, chunks[m][:, c, 1], ALU.add))
                dve.wait_ge(S["state_made"], q + 1)
                for u in range(2):
                    r = slice(64 * u, 64 * u + 64)
                    V.tensor_tensor(nxt[r], nxt[r], view(B[u][r, 0:CT * HD], CT, HD), ALU.add).then_inc(S["state_ready"], 1)
                dve.wait_ge(S["state_ready"], 2 * q + 3)
            for m in range(MT):
                for u in range(2):
                    dve.wait_ge(S["sa_made"], 2 * m + u + 1)
                    su = wu[:, m].rearrange("p (i u) t -> p u i t", u=2)[:, u, :, HD:P]
                    V.tensor_tensor(su, su, view(B[2 + 2 * m + u][:, 0:CT * HD], CT, HD), ALU.add).then_inc(S["sa_ready"], 1)
            for m in range(MT):
                for u in range(2):
                    dve.wait_ge(S["y_made"], 2 * m + u + 1)
                    V.tensor_copy(yr[:, m * NH:(m + 1) * NH].rearrange("p (i u) d -> p u i d", u=2)[:, u],
                                  view(B[(6, 7, 0, 1)[2 * m + u]][:, 0:CT * HD], CT, HD)).then_inc(S["y_taken"], 1)
            dve.wait_ge(S["y_taken"], 4)
            wide = lambda t: shape(t.unsqueeze(2), P, MT * NH, HD)
            sq = view(ysq, MT * NH, HD)
            after(V.tensor_reduce(mean, yr, AX.X, ALU.add))
            after(V.tensor_scalar(mean, mean, 1.0 / HD, None, ALU.mult))
            after(V.tensor_tensor(yr, yr, wide(mean), ALU.subtract))
            after(V.tensor_tensor(sq, yr, yr, ALU.mult))
            V.tensor_reduce(var, sq, AX.X, ALU.add).then_inc(S["y_var"], 1)
            dve.wait_ge(S["bonus_ready"], 1)
            dve.wait_ge(S["y_var"], 1)
            after(V.tensor_tensor(sq, view(vtok.rearrange("p m n -> p (m n)"), MT * NH, HD), wide(bonus.rearrange("p m h -> p (m h)")), ALU.mult))
            dve.wait_ge(S["y_rstd"], 1)
            after(V.tensor_tensor(yr, yr, wide(rvar), ALU.mult))
            flat_y = yr.rearrange("p (m h) d -> p m (h d)", m=MT)
            after(V.tensor_tensor(flat_y, flat_y, shape(ln_w.unsqueeze(1), P, MT, RW), ALU.mult))
            after(V.tensor_tensor(flat_y, flat_y, shape(ln_b.unsqueeze(1), P, MT, RW), ALU.add))
            V.tensor_tensor(yr, yr, sq, ALU.add).then_inc(S["y_ready"], 1)
            for m in range(MT):
                dve.wait_ge(S["y_transposed"], m + 1)
                V.tensor_tensor(yrt[:, :, m * P:(m + 1) * P], view(B[2 + m][:, :], 4, P), gt[:, :, m * P:(m + 1) * P], ALU.mult)\
                    .then_inc(S["yrt_ready"], 1)
            for m in range(MT):
                for h in range(2):
                    dve.wait_ge(S["out_done"], 2 * m + h + 1)
                    x = X[:, m * D + h * 512:m * D + (h + 1) * 512]
                    V.tensor_tensor(x, x, B[4 + 2 * m + h][:, :], ALU.add).then_inc(S["x_added"], 1)

    nc.all_engine_barrier(sems_to_clear=mixer_sems)


def expert_slots(slot):
    wide = [slot[:, s, :].rearrange("p (c n) -> p c n", c=KC) for s in (0, 5, 1, 2)]
    return wide[0:2], wide[2:4], [slot[:, s, :].rearrange("p (j n) -> p j n", j=DE // P) for s in (4, 3)]


def load_first_experts(sp, a, mem, last_two):
    w_gate, w_up, w_down = expert_slots(mem["slots"])

    def load(w, name, e, done):
        if name == "exp_w_down_2":
            src = a[name][0, e].rearrange("(j p) n -> p j n", p=P)
        else:
            src = a[name][0, e].rearrange("(p c) n -> p c n", c=KC)
        sp.dma_start(w, src).then_inc(done, 16)

    if last_two:
        load(w_up[1], "exp_w_up_2", 1, mem["up_in"][1])
        load(w_down[1], "exp_w_down_2", 1, mem["down_in"][1])
    else:
        load(w_gate[0], "exp_w_gate_2", 0, mem["gate_in"][0])
        load(w_up[0], "exp_w_up_2", 0, mem["up_in"][0])
        load(w_down[0], "exp_w_down_2", 0, mem["down_in"][0])
        load(w_gate[1], "exp_w_gate_2", 1, mem["gate_in"][1])


def experts_part(nc, ctx, a, mem, psum, layout, second):
    X, XN, HT = mem["x"], mem["xn"], mem["ht"]
    arrived, release = mem["arrived"], mem["release"]
    slot, B = mem["slots"], psum
    room = carve(mem["region"])
    const3 = room(sum(w for _, w in layout.values()) - second)

    def const(name):
        at, w = layout[name]
        return const3[:, at - second:at - second + w] if at >= second else mem["const"][:, at:at + w]

    ident = const("ident")
    gain = room(D)
    w_route, b_route = room(KC, NGROUP + NE), room(NGROUP + NE)
    ss, rstd = room(MT), room(MT)
    logit = room(MT, NGROUP + NE)
    top, top_f = room(MT, 8), room(MT, 8)
    best, best_f = room(MT, 8), room(MT, 8)
    neg_top, group_sum, group_gate, eq_group = room(MT), room(MT), room(MT), room(MT, NGROUP)
    exp_junk, of_group, chosen = room(MT, NGROUP), room(MT, EPG, NGROUP), room(MT, EPG)
    gap, first_gate, second_gate = room(MT), room(MT), room(MT)
    ids = room(MT, 2)
    pick, member, gate_of, place = room(MT, 2, NE), room(MT, NE), room(MT, NE), room(MT, NE)
    fullest, over = room(1), room(T // BLK)
    sel, sel_gate = [room(MT, BLK) for _ in range(2)], room(MT, P)
    xt = [room(KC, BLK) for _ in range(2)]
    sgt = [room(MT, P) for _ in range(2)]
    th, hid, hidt = room(P), room(P), room(P)
    y = room(4, 256)
    ht = view(HT[:, :], KC, T)
    xn = view(XN[:, :], MT, P, KC)
    index = ctx.enter_context(nc.sbuf_tensor("router_index", [P, 2 * MT * 8], U32))
    passes = ctx.enter_context(nc.sbuf_tensor("pass_count", [1, 2], I32))

    S, _ = semaphores(nc, ctx, """params_in ss_ready pool_step rstd_ready xn_ready h_transposed ht_ready routed gap_ready group_ready
        gates_exp member_ready ranked passes_ready acc_ready dve_step scored stored""".split(), "_3")
    Q, pass_sems = semaphores(nc, ctx, """sel_ready gathered xt_ready
        sgt_ready gate_done gate_tanh up_done hid_half hid_ready hid_transposed hidt_ready down_done y_ready combined
        pass_step""".split(), "_e")
    gate_in, up_in, down_in = mem["gate_in"], mem["up_in"], mem["down_in"]
    w_gate, w_up, w_down = expert_slots(slot)

    def arrive(eng, name):
        eng.drain().then_inc(arrived, 1)
        eng.wait_ge(release[name], 1)
        eng.sem_clear(release[name])

    with nc.Block() as block:

        @block.sync
        def _(sp):
            def rest_of_pass():
                with sp.Fori(0, NE // 2 - 1) as k:
                    for u in range(2):
                        e = bass.ds(k * 2 + 2 + u, 1)
                        sp.wait_ge(Q["gate_done"], k * 2 + 1 + u)
                        sp.dma_start(w_gate[u], a["exp_w_gate_2"][0, e].rearrange("a (p c) n -> p (a c) n", c=KC)).then_inc(gate_in[u], 16)
                        sp.wait_ge(Q["up_done"], k * 2 + 1 + u)
                        sp.dma_start(w_up[u], a["exp_w_up_2"][0, e].rearrange("a (p c) n -> p (a c) n", c=KC)).then_inc(up_in[u], 16)
                        sp.wait_ge(Q["down_done"], k * 2 + 1 + u)
                        sp.dma_start(w_down[u], a["exp_w_down_2"][0, e].rearrange("a (j p) n -> p (a j) n", p=P)).then_inc(down_in[u], 16)
                arrive(sp, "sp")

            sp.wait_ge(S["params_in"], 16 * 6)
            load_first_experts(sp, a, mem, True)
            rest_of_pass()
            sp.wait_ge(S["passes_ready"], 1)
            n = sp.value_load(passes[0:1, 0:1], min_val=1, max_val=T // BLK)
            with sp.If(n > 1):
                with sp.Fori(1, n):
                    load_first_experts(sp, a, mem, False)
                    load_first_experts(sp, a, mem, True)
                    rest_of_pass()
            for m in range(MT):
                sp.wait_ge(S["routed"], m + 1)
                sp.dma_start(a["out"][0, m * P:(m + 1) * P], X[:, m * D:(m + 1) * D]).then_inc(S["stored"], 16)
            sp.wait_ge(S["stored"], 16 * MT)

        @block.gpsimd
        def _(pool):
            pool.wait_ge(S["ss_ready"], MT)
            nc.gpsimd.tensor_scalar(rstd, ss, 1.0 / D, EPS, ALU.mult, ALU.add).then_inc(S["pool_step"], 1)
            pool.wait_ge(S["pool_step"], 1)
            nc.gpsimd.tensor_tensor(rstd, rstd, const("minus_half")[:, 0:MT], ALU.pow).then_inc(S["rstd_ready"], 1)

        @block.scalar
        def _(act):
            act.dma_start(const3, a["constants"][:, second:second + const3.shape[1]]).then_inc(S["params_in"], 16)
            act.dma_start(gain, shape(a["norm_ffn_w_2"], P, D)).then_inc(S["params_in"], 16)
            act.dma_start(w_route[:, :, 0:NGROUP], a["router_group_w_2"][0].rearrange("(p c) n -> p c n", c=KC)).then_inc(S["params_in"], 16)
            act.dma_start(w_route[:, :, NGROUP:], a["router_expert_w_2"][0].rearrange("(p c) n -> p c n", c=KC)).then_inc(S["params_in"], 16)
            act.dma_start(b_route[:, 0:NGROUP], shape(a["router_group_b_2"], P, NGROUP)).then_inc(S["params_in"], 16)
            act.dma_start(b_route[:, NGROUP:], shape(a["router_expert_b_2"], P, NE)).then_inc(S["params_in"], 16)
            for m in range(MT):
                nc.scalar.activation(HT[:, m * D:(m + 1) * D], X[:, m * D:(m + 1) * D], ACT.Square, accum_out=ss[:, m:m + 1]).then_inc(S["ss_ready"], 1)
            for m in range(MT):
                for b in range(2):
                    act.wait_ge(S["h_transposed"], 2 * m + b + 1)
                    nc.scalar.copy(ht[:, 4 * b:4 * b + 4, m * P:(m + 1) * P], view(B[2 * m + b][:, :], 4, P)).then_inc(S["ht_ready"], 1)
            act.wait_ge(S["gap_ready"], 1)
            for m in range(MT):
                nc.scalar.activation(exp_junk[:, m], logit[:, m, 0:NGROUP], ACT.Exp, bias=neg_top[:, m:m + 1],
                                     accum_out=group_sum[:, m:m + 1]).then_inc(S["group_ready"], 1)
            act.wait_ge(S["gap_ready"], 2)
            nc.scalar.activation(second_gate, gap, ACT.Exp).then_inc(S["gates_exp"], 1)

            def copies(e, u, tail, follow):
                if tail:
                    act.wait_ge(Q["hid_transposed"], e)
                    nc.scalar.copy(hidt, B[7][:, 256:256 + P]).then_inc(Q["hidt_ready"], 1)
                    act.wait_ge(Q["down_done"], e)
                    for j in range(4):
                        r = slice(BLK * j, BLK * (j + 1))
                        nc.scalar.copy(y[r, j], B[7][r, 0:256]).then_inc(Q["y_ready"], 1)
                if follow:
                    act.wait_ge(Q["gathered"], e + 2)
                    nc.scalar.copy(xt[1 - u].rearrange("p c s -> p (c s)"), B[6][:, 0:256]).then_inc(Q["xt_ready"], 1)
                    if tail:
                        act.wait_ge(Q["combined"], e)
                    nc.scalar.copy(sgt[1 - u].rearrange("p m t -> p (m t)"), B[6][:, 256:]).then_inc(Q["sgt_ready"], 1)

            def step(e, u, tail=True, follow=True):
                act.wait_ge(Q["gate_done"], e + 1)
                nc.scalar.activation(th, B[4][:, 0:P], ACT.Tanh, scale=0.5).then_inc(Q["gate_tanh"], 1)
                copies(e, u, tail, follow)

            act.wait_ge(S["passes_ready"], 1)
            act.wait_ge(S["acc_ready"], 2)
            n = act.value_load(passes[0:1, 0:1], min_val=1, max_val=T // BLK)
            with act.Fori(0, n):
                copies(-1, 1, False, True)
                step(0, 0, tail=False)
                with act.Fori(0, NE // 2 - 1) as k:
                    step(k * 2 + 1, 1)
                    step(k * 2 + 2, 0)
                step(NE - 1, 1, follow=False)
                copies(NE, 0, True, False)
                arrive(act, "act")

        @block.tensor
        def _(pe):
            for m in range(MT):
                pe.wait_ge(S["xn_ready"], m + 1)
                for c in range(KC):
                    t = nc.tensor.transpose(B[2 * m + c // 4][:, c % 4 * P:(c % 4 + 1) * P], xn[:, m, :, c], ident)
                    if c % 4 == 3:
                        t.then_inc(S["h_transposed"], 1)
            for m in range(MT):
                pe.wait_ge(S["ht_ready"], 2 * m + 2)
                for c in range(KC):
                    mm = nc.tensor.matmul(B[4][:, m * 72:(m + 1) * 72], ht[:, c, m * P:(m + 1) * P], w_route[:, c], start=c == 0, stop=c == KC - 1)
            mm.then_inc(S["scored"], 1)
            pe.wait_ge(S["member_ready"], 1)
            nc.tensor.matmul(B[5][:, 0:NE], const("before"), member[:, 0], start=True, stop=True)
            nc.tensor.matmul(B[5][:, NE:2 * NE], const("before"), member[:, 1], start=True, stop=False)
            nc.tensor.matmul(B[5][:, NE:2 * NE], const("ones"), member[:, 0], start=False, stop=True)
            nc.tensor.matmul(B[5][:, 2 * NE:3 * NE], const("ones"), member[:, 0], start=True, stop=False)
            nc.tensor.matmul(B[5][:, 2 * NE:3 * NE], const("ones"), member[:, 1], start=False, stop=True).then_inc(S["ranked"], 1)

            def gather(e, u, first):
                pe.wait_ge(Q["sel_ready"], e + 1)
                if not first:
                    pe.wait_ge(Q["sgt_ready"], e)
                for c in range(KC):
                    for m in range(MT):
                        nc.tensor.matmul(B[6][:, c * BLK:(c + 1) * BLK], xn[:, m, :, c], sel[u][:, m], start=m == 0, stop=m == MT - 1)
                for m in range(MT):
                    t = nc.tensor.transpose(B[6][:, 256 + m * P:256 + (m + 1) * P], sel_gate[:, m], ident)
                t.then_inc(Q["gathered"], 1)

            def into_hidden(u, bank, w, done):
                for c in range(KC):
                    for j in range(4):
                        mm = nc.tensor.matmul(B[bank][BLK * j:BLK * (j + 1), 0:P], xt[u][:, c], w[u][:, c, j * P:(j + 1) * P],
                                              start=c == 0, stop=c == KC - 1, tile_position=(0, BLK * j))
                mm.then_inc(done, 1)

            def turn(e):
                pe.wait_ge(Q["hid_ready"], e + 1)
                nc.tensor.transpose(B[7][:, 256:256 + P], hid, ident).then_inc(Q["hid_transposed"], 1)

            def down(e, u, use):
                pe.wait_ge(Q["hidt_ready"], e + 1)
                pe.wait_ge(down_in[u], use * 16)
                for k in range(4):
                    for j in range(4):
                        mm = nc.tensor.matmul(B[7][BLK * j:BLK * (j + 1), 0:256], hidt[:, BLK * k:BLK * (k + 1)], w_down[u][:, k, j * 256:(j + 1) * 256],
                                              start=k == 0, stop=k == 3, tile_position=(0, BLK * j))
                mm.then_inc(Q["down_done"], 1)

            def combine(e, u):
                for j in range(4):
                    pe.wait_ge(Q["y_ready"], e * 4 + j + 1)
                    for m in range(MT):
                        mm = nc.tensor.matmul(B[j][:, m * 256:(m + 1) * 256], sgt[u][:, m], y[:, j], start=False, stop=True,
                                              skip_group_check=True)
                mm.then_inc(Q["combined"], 1)

            def step(e, u, use, last_use, tail=True, follow=True):
                pe.wait_ge(gate_in[u], use * 16)
                pe.wait_ge(Q["xt_ready"], e + 1)
                if tail:
                    pe.wait_ge(Q["hid_ready"], e)
                into_hidden(u, 4, w_gate, Q["gate_done"])
                if tail:
                    turn(e - 1)
                pe.wait_ge(up_in[u], use * 16)
                into_hidden(u, 5, w_up, Q["up_done"])
                if tail:
                    down(e - 1, 1 - u, last_use)
                if follow:
                    gather(e + 1, 1 - u, False)
                if tail:
                    combine(e - 1, 1 - u)

            pe.wait_ge(S["passes_ready"], 1)
            n = pe.value_load(passes[0:1, 0:1], min_val=1, max_val=T // BLK)
            pe.wait_ge(S["acc_ready"], 2)
            with pe.Fori(0, n):
                gather(0, 0, True)
                step(0, 0, 1, 0, tail=False)
                with pe.Fori(0, NE // 2 - 1) as k:
                    step(k * 2 + 1, 1, k + 1, k + 1)
                    step(k * 2 + 2, 0, k + 2, k + 1)
                step(NE - 1, 1, NE // 2, NE // 2, follow=False)
                turn(NE - 1)
                down(NE - 1, 1, NE // 2)
                combine(NE - 1, 1)
                arrive(pe, "pe")

        @block.vector
        def _(dve):
            V = nc.vector
            after = Chain(dve, S["dve_step"])
            dve.wait_ge(S["params_in"], 16 * 6)
            dve.wait_ge(S["rstd_ready"], 1)
            for m in range(MT):
                tile = slice(m * D, (m + 1) * D)
                V.scalar_tensor_tensor(XN[:, tile], X[:, tile], rstd[:, m:m + 1], gain, ALU.mult, ALU.mult).then_inc(S["xn_ready"], 1)
            dve.wait_ge(S["scored"], 1)
            after(V.tensor_tensor(logit, view(B[4][:, 0:MT * 72], MT, 72), shape(b_route.unsqueeze(1), P, MT, 72), ALU.add))
            for m in range(MT):
                ins = V.max(top[:, m], logit[:, m, 0:NGROUP])
            after(ins)
            for m in range(MT):
                ins = V.max_index(index[:, m * 8:m * 8 + 8], top[:, m], logit[:, m, 0:NGROUP])
            after(ins)
            V.tensor_scalar(neg_top, top[:, :, 0], -1.0, None, ALU.mult).then_inc(S["gap_ready"], 1)
            after(V.tensor_copy(top_f.rearrange("p m k -> p (m k)"), index[:, 0:MT * 8]))
            iota = const("iota")
            for m in range(MT):
                ins = V.tensor_scalar(eq_group[:, m], iota[:, 0:NGROUP], top_f[:, m, 0:1], None, ALU.is_equal)
            after(ins)
            for m in range(MT):
                ins = V.tensor_tensor(of_group[:, m], logit[:, m, NGROUP:].rearrange("p (g j) -> p j g", g=NGROUP),
                                      shape(eq_group[:, m:m + 1], P, EPG, NGROUP), ALU.mult)
            after(ins)
            after(V.tensor_reduce(chosen, of_group, AX.X, ALU.add))
            for m in range(MT):
                ins = V.max(best[:, m], chosen[:, m])
            after(ins)
            for m in range(MT):
                ins = V.max_index(index[:, (MT + m) * 8:(MT + m) * 8 + 8], best[:, m], chosen[:, m])
            after(ins)
            V.tensor_tensor(gap, best[:, :, 1], best[:, :, 0], ALU.subtract).then_inc(S["gap_ready"], 1)
            after(V.tensor_copy(best_f.rearrange("p m k -> p (m k)"), index[:, MT * 8:]))
            after(V.scalar_tensor_tensor(ids, shape(top_f[:, :, 0:1], P, MT, 2), float(EPG), best_f[:, :, 0:2], ALU.mult, ALU.add))
            for m in range(MT):
                for k in range(2):
                    ins = V.tensor_scalar(pick[:, m, k], iota[:, 0:NE], ids[:, m, k:k + 1], None, ALU.is_equal)
            after(ins)
            V.tensor_tensor(member, pick[:, :, 0], pick[:, :, 1], ALU.add).then_inc(S["member_ready"], 1)
            dve.wait_ge(S["group_ready"], MT)
            dve.wait_ge(S["gates_exp"], 1)
            after(V.tensor_scalar(first_gate, second_gate, 1.0, None, ALU.add))
            after(V.tensor_tensor(first_gate, first_gate, group_sum, ALU.mult))
            after(V.reciprocal(first_gate, first_gate))
            after(V.tensor_scalar(first_gate, first_gate, 0.5, None, ALU.mult))
            after(V.tensor_tensor(second_gate, second_gate, first_gate, ALU.mult))
            for m in range(MT):
                ins = V.tensor_scalar(gate_of[:, m], pick[:, m, 0], first_gate[:, m:m + 1], None, ALU.mult)
            after(ins)
            for m in range(MT):
                ins = V.scalar_tensor_tensor(gate_of[:, m], pick[:, m, 1], second_gate[:, m:m + 1], gate_of[:, m], ALU.mult, ALU.add)
            after(ins)
            dve.wait_ge(S["ranked"], 1)
            ranks = view(B[5][:, 0:MT * NE], MT, NE)
            V.tensor_reduce(fullest, B[5][:, 2 * NE:3 * NE], AX.X, ALU.max)
            after(V.scalar_tensor_tensor(place, ranks, 1.0, member, ALU.add, ALU.mult))
            after(V.tensor_scalar(place, place, -1.0, None, ALU.add))
            after(V.tensor_scalar(over, const("blocks"), fullest, None, ALU.is_lt))
            after(V.tensor_reduce(fullest, over, AX.X, ALU.add))
            after(V.tensor_scalar(passes[:, 0:1], fullest[0:1], 1.0, None, ALU.mult))
            V.tensor_scalar(passes[:, 1:2], fullest[0:1], -1.0, None, ALU.add).then_inc(S["passes_ready"], 1)
            dve.wait_ge(S["ht_ready"], 4)
            for j in range(4):
                ins = V.memset(B[j][:, :], 0.0)
            ins.then_inc(S["acc_ready"], 1)
            V.memset(y, 0.0).then_inc(S["acc_ready"], 1)

            def select(e, u, first=False):
                if not first:
                    dve.wait_ge(Q["gathered"], e)
                for m in range(MT):
                    p = place[:, m, e:e + 1] if isinstance(e, int) else place[:, m, bass.ds(e, 1)]
                    g = gate_of[:, m, e:e + 1] if isinstance(e, int) else gate_of[:, m, bass.ds(e, 1)]
                    V.tensor_scalar(sel[u][:, m], const("slot_of")[:, 0:BLK], p, None, ALU.is_equal)
                    ins = V.tensor_scalar(sel_gate[:, m], const("slot_of"), p, g, ALU.is_equal, ALU.mult)
                ins.then_inc(Q["sel_ready"], 1)

            def step(e, u, follow=True):
                if follow:
                    select(e + 1, 1 - u)
                dve.wait_ge(Q["gate_tanh"], e + 1)
                V.scalar_tensor_tensor(th, th, 1.0, B[4][:, 0:P], ALU.add, ALU.mult).then_inc(Q["hid_half"], 1)
                dve.wait_ge(Q["hid_half"], e + 1)
                dve.wait_ge(Q["up_done"], e + 1)
                V.tensor_tensor(hid, th, B[5][:, 0:P], ALU.mult).then_inc(Q["hid_ready"], 1)

            dve.wait_ge(S["passes_ready"], 1)
            n = dve.value_load(passes[0:1, 0:1], min_val=1, max_val=T // BLK)
            with dve.Fori(0, n):
                select(0, 0, True)
                step(0, 0)
                with dve.Fori(0, NE // 2 - 1) as k:
                    step(k * 2 + 1, 1)
                    step(k * 2 + 2, 0)
                step(NE - 1, 1, follow=False)
                V.tensor_scalar(place, place, float(-BLK), None, ALU.add).then_inc(Q["pass_step"], 1)
                dve.wait_ge(Q["pass_step"], 1)
                dve.drain()
                dve.wait_ge(arrived, 3)
                dve.sem_clear(pass_sems)
                for weights in gate_in + up_in + down_in:
                    dve.sem_clear(weights)
                dve.sem_clear(arrived)
                for name in ("sp", "act", "pe"):
                    dve.sem_inc(release[name], 1)
            for m in range(MT):
                for j in range(4):
                    x = X[:, m * D + j * 256:m * D + (j + 1) * 256]
                    ins = V.tensor_tensor(x, x, B[j][:, m * 256:(m + 1) * 256], ALU.add)
                ins.then_inc(S["routed"], 1)


def program(nc, a, layout, ends, parts=("layers", "mixer", "experts")):
    first, second = ends
    ctx = ExitStack()
    with ctx:
        def sbuf(name, width):
            return ctx.enter_context(nc.sbuf_tensor(name, [P, width], F32))

        def sem(name):
            return ctx.enter_context(nc.semaphore(name))

        mem = {
            "slots": sbuf("weight_slots", NSLOT * SLOT)[:, :].rearrange("p (s n) -> p s n", s=NSLOT),
            "x": sbuf("tokens", MT * D),
            "xn": sbuf("normed_tokens", MT * D),
            "ht": sbuf("normed_features", KC * T),
            "const": sbuf("const_rows", first),
            "region": sbuf("work_region", REGION)[:, :],
            "loaded": [sem(f"slot{i}_loaded") for i in range(NSLOT)],
            "w1_loaded": [sem("w1_k_loaded"), sem("w1_v_loaded")],
            "gate_in": [sem(f"gate_in_{u}") for u in range(2)],
            "up_in": [sem(f"up_in_{u}") for u in range(2)],
            "down_in": [sem(f"down_in_{u}") for u in range(2)],
            "arrived": sem("engines_arrived"),
            "release": {n: sem(f"{n}_released") for n in ("sp", "pool", "act", "pe")},
        }
        for n in ("rows_in", "small_in", "br_loaded", "norm_in", "rows_transposed", "both_ready", "x_in", "const_in", "zeroed", "stored"):
            mem[n] = sem(n)

        def const(name):
            at, w = layout[name]
            return mem["const"][:, at:at + w]

        banks = [ctx.enter_context(nc.psum_tensor(f"bank{i}", [P, 512], F32)) for i in range(8)]
        if "layers" in parts:
            with ExitStack() as own:
                layers_part(nc, own, a, mem, banks, const)
        if "mixer" in parts:
            with ExitStack() as own:
                mixer_part(nc, own, a, mem, banks, layout, first, second)
        if "experts" in parts:
            with ExitStack() as own:
                experts_part(nc, own, a, mem, banks, layout, second)
        if "experts" not in parts:
            with nc.Block() as block:
                @block.sync
                def _(sp):
                    sp.dma_start(a["out"].rearrange("b (m p) n -> p (b m) n", p=P), mem["x"][:, :].rearrange("p (m n) -> p m n", m=MT)).then_inc(mem["stored"], 16)
                    sp.wait_ge(mem["stored"], 16)


_INS = """x norm_g w_in conv_w conv_b rg_wr rg_br rg_wi rg_bi rg_lambda q_norm_g k_norm_g cmp_pe_k cmp_w1_k cmp_w2_k
    cmp_pe_v cmp_w1_v cmp_w2_v w_out norm_mix_w_2 w_in_2 mu_shift_2 rw_w0_2 rw_w2_2 rw_a0_2 rw_a2_2 rw_g2_2 rw_k_k_2
    rw_k_a_2 rw_r_k_2 rw_ln_w_2 rw_ln_b_2 fox_b_f_2 fox_q_norm_w_2 fox_k_norm_w_2 w_out_2 norm_ffn_w_2
    router_group_w_2 router_group_b_2 router_expert_w_2 router_expert_b_2 exp_w_gate_2 exp_w_up_2 exp_w_down_2""".split()


def kernel(**inputs):
    import concourse.bacc as bacc
    from concourse.bass_utils import run_bass_kernel_spmd as run

    nc = bacc.Bacc("TRN2", target_bir_lowering=False, num_devices=1)
    table, layout, ends = constants()
    arrays, a = {}, {}
    for name in _INS + ["constants"]:
        value = table if name == "constants" else np.ascontiguousarray(inputs[name])
        arrays[f"in_{name}_dram"] = value
        a[name] = nc.dram_tensor(f"in_{name}_dram", value.shape, mybir.dt.from_np(value.dtype), kind="ExternalInput").ap()
    a["out"] = nc.dram_tensor("out_dram", (1, T, D), F32, kind="ExternalOutput").ap()
    program(nc, a, layout, ends)
    return run(nc, [arrays], core_ids=[0]).results[0]["out_dram"]
```

```python
from contextlib import ExitStack

import numpy as np

import concourse.bass as bass
from concourse import mybir

F32 = mybir.dt.float32
I32 = mybir.dt.int32
U32 = mybir.dt.uint32
ALU = mybir.AluOpType
ACT = mybir.ActivationFunctionType
AX = mybir.AxisListType

P = 128
T = 256
MT = T // P
D = 1024
KC = D // P
DEPTH = 2
HD = 64
EPS = 1e-6
NEG = -1e30
LOWEST = -3e38
SCALE = HD ** -0.5

RG = 512
CT = RG // P
CONV_W = 4
NH = 8
NG = 2
HPG = NH // NG
ROPE = 16
CMP_LEN, CMP_STRIDE = 32, 16
NB = (T - CMP_LEN) // CMP_STRIDE + 1
HID = 128
LP = CMP_LEN // 2
CHUNK = 32
SLOT = 4096
NSLOT = 6
NE = 64
NGROUP, EPG = 8, 8
DE = 512
BLK = 32
NRING = 6

COL_RGX, COL_RGG, COL_Q = 0, RG, 2 * RG
COL_KC = 3 * RG
COL_KW = COL_KC + 4 * NG * HD
COL_NG = COL_KW + 2 * NG * HD
COL_BR = COL_NG + NH * HD
N_IN = COL_BR + 3 * NH
NKW = 2 * NG * HD + 3 * NH

REGION = 20800
CONST3 = 4 * P
N_ROWS2, N_SMALL2 = 12, 8

ROW_CONV, ROW_CB, ROW_BR, ROW_BI, ROW_LAM, ROW_PEK, ROW_PEV = 0, 16, 20, 24, 28, 32, 48
NROWS = 64


def constants():
    cols, at = [], {}

    def add(name, a):
        a = np.asarray(a, np.float32).reshape(P, -1)
        at[name] = (sum(c.shape[1] for c in cols), a.shape[1])
        cols.append(a)

    p = np.arange(P)[:, None]
    f = np.arange(P)[None, :]
    add("ident", p == f)
    add("causal", np.concatenate([np.zeros((P, P)), np.where(f <= p, 0.0, NEG)], 1))
    end = np.arange(NB) * CMP_STRIDE + CMP_LEN - 1
    seen = np.stack([end[None, :] <= (m * P + p) for m in range(MT)], 1)
    add("cmp_neg", np.where(seen, 0.0, NEG))
    add("cmp_one", seen)
    inv = (np.float32(500000.0) ** (-np.arange(ROPE // 2, dtype=np.float32) / (ROPE // 2))).astype(np.float32)

    def rope(name, pos):
        ang = (pos.astype(np.float32)[..., None] * inv).astype(np.float32)
        c, s = np.cos(ang), np.sin(ang)
        add(name + "_cos", np.concatenate([c, c], -1))
        add(name + "_sin", np.concatenate([-s, s], -1))

    rope("pos", np.arange(MT)[None, :] * P + p)
    rope("end", np.concatenate([end, np.zeros(P - NB)])[:, None])
    add("minus_half", np.full((P, 32), -0.5))
    first = sum(c.shape[1] for c in cols)
    same = lambda n: p // n == f // n
    add("upto", np.concatenate([p <= f, np.ones((P, P))], 1))
    add("restart", np.tile((np.arange(T) % CHUNK != 0)[None], (P, 1)))
    add("below_half_t", (p < f) & same(CHUNK // 2))
    add("below_half", (f < p) & same(CHUNK // 2))
    add("across", (f < p) & same(CHUNK) & ~same(CHUNK // 2))
    add("below_t", (p < f) & same(CHUNK))
    add("upto_t", (p <= f) & same(CHUNK))
    add("head_ones", same(HD))
    add("head_pick", p // HD == np.arange(2)[None, :])
    second = sum(c.shape[1] for c in cols)
    add("before", p < f)
    add("ones", np.ones((P, P)))
    add("iota", np.tile(np.arange(P)[None], (P, 1)))
    add("slot_of", np.tile((np.arange(P) % BLK)[None], (P, 1)))
    return np.concatenate(cols, 1).astype(np.float32), at, (first, second)


def shape(ap, *dims):
    return ap.to_broadcast(list(dims))


def semaphores(nc, ctx, names, suffix=""):
    sems = {n: ctx.enter_context(nc.semaphore(n + suffix)) for n in names}
    nums = sorted(s.num for s in sems.values())
    assert nums == list(range(nums[0], nums[0] + len(nums)))
    return sems, range(nums[0], nums[-1] + 1)


class Chain:

    def __init__(self, eng, sem):
        self.eng, self.sem, self.n = eng, sem, 0

    def __call__(self, ins):
        self.n += 1
        ins.then_inc(self.sem, 1)
        self.eng.wait_ge(self.sem, self.n)
        return ins


def view(ap, *dims):
    names = "abcd"[:len(dims)]
    return ap.rearrange(f"p ({' '.join(names)}) -> p {' '.join(names)}", **dict(zip(names, dims)))


def carve(region):
    at = [0]

    def room(*dims):
        n = int(np.prod(dims))
        ap = region[:, at[0]:at[0] + n]
        at[0] += n
        assert at[0] <= region.shape[1], (at[0], region.shape)
        return view(ap, *dims)

    room.at = at
    return room


def layers_part(nc, ctx, a, mem, psum, const):
    slot, loaded = mem["slots"], mem["loaded"]
    X, XN, HT = mem["x"], mem["xn"], mem["ht"]
    arrived, release = mem["arrived"], mem["release"]
    ident, B = const("ident"), psum
    room = carve(mem["region"])

    rows, params_both, params = room(P), room(DEPTH, NROWS), room(NROWS)
    norm_g = room(DEPTH, KC)
    gain, gain12, gain_c = room(3, HD), room(12, HD), room(HD)
    ss, rstd = mem["square_sum"], mem["rstd"]
    ssq, rsq = room(MT * 12), room(MT * 12)
    ssk, rsk = room(NG), room(NG)
    wri = room(2, CT, P)
    w2 = room(2, HD)
    qk_flat = room(MT * 12 * HD)
    qk = view(qk_flat, MT, 12, HD)
    qt = room(MT, HPG, P)
    kt = room(2, T)
    vsw = room(MT, 2, NG, HD)
    tbr, coef, rden = room(MT, 3 * NH), room(MT, 3, NH), room(NH)
    tc, hc = room(2 * NG * NB), room(2 * NG * NB)
    kc, ka, kb = room(NG, HD), room(NG, HD), room(NG, ROPE)
    kct = room(16)
    xc = room(CT, T + CONV_W - 1)
    cv, tr, ti, aa, sgr = room(CT, T), room(CT, T), room(CT, T), room(CT, T), room(CT, T)
    lam, half_b = room(12, CT), room(2, CT)
    sgn_flat = room(MT * NH * HD)
    sgn = view(sgn_flat, MT, NH * HD)
    rot_a, rot_b = [view(sgn_flat[:, i * MT * 12 * ROPE:(i + 1) * MT * 12 * ROPE], MT, 12, ROPE) for i in range(2)]
    cs, cmax = room(MT, NH, NB), room(NH)
    pc, pct = room(MT, NG, HPG * 32), room(MT, NG, P)
    rowmax, negmax, den = room(2, NH), room(2, NH), room(MT, 3, NH)
    yb, tmp = room(MT, NH, HD), room(NH, HD)
    prob = [view(XN[:, :], NH, T), view(HT[:, :], NH, T)]
    ring = room(NRING * 4 * P)
    pt = view(ring, NRING, 4, P)
    vbd = room(NG, HPG * HD)
    ybt = view(qk_flat[:, 0:4 * T], 4, T)
    ht = view(HT[:, :], KC, T)
    junk = ring[:, 0:MT * D]
    sqk = view(ring[:, 0:MT * 12 * HD], MT * 12, HD)
    z = view(ring[:, MT * 12 * HD:MT * 12 * HD + 2 * LP * NG * NB], 2, LP, NG * NB)

    names = """params_ready ss_ready rstd_ready xn_ready params_transposed h_transposed ht_ready
        q_done kcvc_done ksvs_done kwvw_done rgx_done qk_copied qk_ss qk_rstd qk_ready qk_transposed qkt_ready
        z_ready comp1_done comp1_tanh hid_ready comp2_done kc_ss kc_rstd kc_ready kc_transposed kct_ready vbd_ready
        xc_ready cv_ready half_ready lam_in lam_exp c_ready lru_gates_done tr_ready ti_ready rgg_done rgg_tanh sgr_ready
        nsag_done nsag_tanh sgn_ready cmp_scores cmp_out cmp_shifted cmp_exp pc_ready pc_transposed pct_ready
        th_ready aa_ready uq_in uq_ready ya_ready scores masked exp_done p_transposed pt_ready weighed o_taken
        yb_ready yb_transposed ybt_ready out_done x_added dve_step pool_step""".split()
    S, layer_sems = semaphores(nc, ctx, names)

    Q_S, KV_S, KW_S, RGX_S, W1_S, RGG_S, NSAG_S, WO_S = 0, 1, 2, 3, 4, 5, 1, (2, 3)

    def chunk(s, width):
        return slot[:, s, 0:KC * width].rearrange("p (c n) -> p c n", c=KC)

    w_out_c = [chunk(s, 512) for s in WO_S]
    w1_c = slot[:, W1_S, :].rearrange("p (v l h) -> p v l h", v=2, l=LP)
    STEPS = [(0, 0), (1, 0), (0, 1), (1, 1)]
    GROUPS = [2 * (m + 1) for _, m in STEPS]

    def pairs(n, g):
        nk = STEPS[n][1] + 1
        return [((4 * g + b) // nk, (4 * g + b) % nk) for b in range(4)]

    def score_out(n, h):
        (br, m), (g, j) = STEPS[n], divmod(h, HPG)
        if m == 0:
            return B[4 + 2 * br + g][:, j * P:(j + 1) * P]
        return B[4 + 2 * g + j // 2][:, j % 2 * T:(j % 2 + 1) * T]

    def arrive(eng, name):
        eng.drain().then_inc(arrived, 1)
        eng.wait_ge(release[name], 1)
        eng.sem_clear(release[name])

    with nc.Block() as block:

        @block.sync
        def _(sp):
            win, wout = a["w_in"], a["w_out"]

            def load(s, src, width=512):
                sp.dma_start(chunk(s, width), src.rearrange("(p c) n -> p c n", c=KC)).then_inc(loaded[s], 16)

            def load_kw(l):
                kw = chunk(KW_S, NKW)
                sp.dma_start(kw[:, :, 0:256], win[l, :, COL_KW:COL_NG].rearrange("(p c) n -> p c n", c=KC))\
                    .then_inc(loaded[KW_S], 16)
                sp.dma_start(kw[:, :, 256:NKW], win[l, :, COL_BR:N_IN].rearrange("(p c) n -> p c n", c=KC))\
                    .then_inc(mem["br_loaded"], 16)

            def load_w1(l):
                for v, name in enumerate(("cmp_w1_k", "cmp_w1_v")):
                    sp.dma_start(w1_c[:, v], a[name][l].rearrange("(l p) h -> p l h", p=P)).then_inc(mem["w1_loaded"][v], 16)

            def load_small(l):
                sp.dma_start(gain[:, 0], shape(a["q_norm_g"][l:l + 1], P, HD)).then_inc(mem["small_in"], 16)
                sp.dma_start(gain[:, 1:3], shape(a["k_norm_g"][l:l + 1, 1:3], P, 2, HD)).then_inc(mem["small_in"], 16)
                sp.dma_start(gain_c, shape(a["k_norm_g"][l:l + 1, 0], P, HD)).then_inc(mem["small_in"], 16)
                for v, n in enumerate(("cmp_w2_k", "cmp_w2_v")):
                    sp.dma_start(w2[:, v], a[n][l]).then_inc(mem["small_in"], 16)
                for v, n in enumerate(("rg_wr", "rg_wi")):
                    for u in range(2):
                        r = slice(64 * u, 64 * u + 64)
                        sp.dma_start(wri[r, v, :, r], a[n][l].rearrange("(i u) c d -> u c i d", u=2)[u]).then_inc(mem["small_in"], 16)

            sp.dma_start(X[:, :].rearrange("p (m n) -> p m n", m=MT),
                         a["x"].rearrange("b (m p) n -> p (b m) n", p=P)).then_inc(mem["x_in"], 16)
            sp.wait_ge(mem["zeroed"], 4)
            sp.dma_start(mem["const"][:, :], a["constants"][:, 0:mem["const"].shape[1]]).then_inc(mem["const_in"], 16)
            for l in range(DEPTH):
                at = l * NROWS
                sp.dma_start(rows[at + ROW_CONV:at + ROW_CB], a["conv_w"][l].rearrange("k (i p) -> (k i) p", p=P)).then_inc(mem["rows_in"], 16)
                for r, n in ((ROW_CB, "conv_b"), (ROW_BR, "rg_br"), (ROW_BI, "rg_bi"), (ROW_LAM, "rg_lambda")):
                    sp.dma_start(rows[at + r:at + r + 4], a[n][l].rearrange("(i p) -> i p", p=P)).then_inc(mem["rows_in"], 16)
                for r, n in ((ROW_PEK, "cmp_pe_k"), (ROW_PEV, "cmp_pe_v")):
                    sp.dma_start(rows[at + r:at + r + LP], a[n][l].rearrange("(l t) d -> l (t d)", t=2)).then_inc(mem["rows_in"], 16)
            sp.dma_start(norm_g, a["norm_g"].rearrange("l (p c) -> p l c", c=KC)).then_inc(mem["norm_in"], 16)
            load(Q_S, win[0, :, COL_Q:COL_KC])
            load(KV_S, win[0, :, COL_KC:COL_KW])
            load_small(0)
            load_kw(0)
            load(RGX_S, win[0, :, COL_RGX:COL_RGG])
            load_w1(0)
            load(RGG_S, win[0, :, COL_RGG:COL_Q])
            for l in range(DEPTH):
                sp.wait_ge(S["ksvs_done"], MT)
                load(NSAG_S, win[l, :, COL_NG:COL_BR])
                for h, done, n in ((0, S["kwvw_done"], MT), (1, S["rgx_done"], 2)):
                    sp.wait_ge(done, n)
                    sp.dma_start(w_out_c[h], wout[l, :, h * 512:(h + 1) * 512].rearrange("(k p) n -> p k n", p=P))\
                        .then_inc(loaded[WO_S[h]], 16)
                if l + 1 < DEPTH:
                    sp.wait_ge(S["q_done"], MT)
                    load(Q_S, win[l + 1, :, COL_Q:COL_KC])
                    sp.wait_ge(S["comp1_done"], 1)
                    load_w1(l + 1)
                    sp.wait_ge(S["rgg_done"], 2)
                    load(RGG_S, win[l + 1, :, COL_RGG:COL_Q])
                    sp.wait_ge(S["nsag_done"], MT)
                    load(KV_S, win[l + 1, :, COL_KC:COL_KW])
                    sp.wait_ge(S["out_done"], 2 * MT)
                    load_small(l + 1)
                    load_kw(l + 1)
                    load(RGX_S, win[l + 1, :, COL_RGX:COL_RGG])
                else:
                    for done, n, names in ((S["q_done"], MT, ("fq",)), (S["comp1_done"], 1, ("fk",)), (S["rgg_done"], 2, ("fv",)),
                                           (S["nsag_done"], MT, ("lora",)), (S["out_done"], 2 * MT, ("r", "k"))):
                        sp.wait_ge(done, n)
                        for name in names:
                            load_mixer_weights(sp, a, slot, loaded, name)
                arrive(sp, "sp")

        @block.gpsimd
        def _(pool):
            nc.gpsimd.memset(wri, 0.0).then_inc(mem["zeroed"], 1)
            nc.gpsimd.memset(vbd, 0.0).then_inc(mem["zeroed"], 1)
            nc.gpsimd.memset(xc[:, :, 0:CONV_W - 1], 0.0).then_inc(mem["zeroed"], 1)
            nc.gpsimd.memset(pc, 0.0).then_inc(mem["zeroed"], 1)
            pool.wait_ge(mem["zeroed"], 4)
            pool.wait_ge(mem["const_in"], 16)
            pool.wait_ge(mem["first_ss"], MT)
            nc.gpsimd.tensor_scalar(rstd, ss, 1.0 / D, EPS, ALU.mult, ALU.add).then_inc(mem["first_step"], 1)
            pool.wait_ge(mem["first_step"], 1)
            nc.gpsimd.tensor_tensor(rstd, rstd, const("minus_half")[:, 0:MT], ALU.pow).then_inc(mem["first_rstd"], 1)
            with pool.Fori(0, DEPTH):
                steps = [0]

                def inv_root(out, src, scale, ready, n, done):
                    pool.wait_ge(ready, n)
                    nc.gpsimd.tensor_scalar(out, src, scale, EPS, ALU.mult, ALU.add).then_inc(S["pool_step"], 1)
                    steps[0] += 1
                    pool.wait_ge(S["pool_step"], steps[0])
                    nc.gpsimd.tensor_tensor(out, out, const("minus_half")[0:out.shape[0], 0:out.shape[1]], ALU.pow)\
                        .then_inc(done, 1)

                inv_root(rsq, ssq, 1.0 / HD, S["qk_ss"], 1, S["qk_rstd"])
                inv_root(rsk[0:NB], ssk[0:NB], 1.0 / HD, S["kc_ss"], 1, S["kc_rstd"])
                for m in range(MT):
                    inv_root(rstd[:, m:m + 1], ss[:, m:m + 1], 1.0 / D, S["ss_ready"], m + 1, S["rstd_ready"])
                arrive(pool, "pool")

        @block.scalar
        def _(act):
            act.wait_ge(mem["x_in"], 16)

            def square(m, done):
                nc.scalar.activation(junk[:, m * D:(m + 1) * D], X[:, m * D:(m + 1) * D], ACT.Square,
                                     accum_out=ss[:, m:m + 1]).then_inc(done, 1)

            for m in range(MT):
                square(m, mem["first_ss"])
            act.wait_ge(mem["rows_transposed"], 1)
            nc.scalar.copy(params_both.rearrange("p l r -> p (l r)"), B[7][:, 0:P]).then_inc(mem["both_ready"], 1)
            def early(dst, src):
                act.dma_start(dst, src).then_inc(mem["rows2_in"], 16)

            rows, norm_g = mem["rows2"], mem["norm_g2"]
            mu = a["mu_shift_2"]
            for t, c in ((0, COL2_R), (4, COL2_K), (8, COL2_V)):
                early(rows[t:t + 4], mu[0, c:c + RW].rearrange("(i p) -> i p", p=P))
            early(rows[12:13, 0:LORA], mu[0:1, COL2_PW:COL2_PW + LORA])
            early(rows[12:13, LORA:P], mu[0:1, COL2_PA:COL2_PA + LORA])
            early(rows[13:14], mu[0:1, COL2_PA + LORA:COL2_FQ])
            for r, name in ((ROW_W0, "rw_w0_2"), (ROW_A0, "rw_a0_2"), (ROW_KK, "rw_k_k_2"), (ROW_KA, "rw_k_a_2")):
                early(rows[r:r + 4], a[name][0].rearrange("(i p) -> i p", p=P))
            early(rows[ROW_RK:ROW_RK + 4], a["rw_r_k_2"][0].rearrange("(i u) d -> i (u d)", u=2))
            early(norm_g, a["norm_mix_w_2"][0].rearrange("(p c) -> p c", c=KC))
            act.wait_ge(mem["both_ready"], 1)
            with act.Fori(0, DEPTH) as l:
                nc.scalar.copy(params.unsqueeze(1), params_both[:, bass.ds(l, 1)]).then_inc(S["params_ready"], 1)
                act.wait_ge(S["params_ready"], 1)
                nc.scalar.mul(half_b.rearrange("p a b -> p (a b)"), params[:, ROW_BR:ROW_LAM], 0.5).then_inc(S["half_ready"], 1)
                act.wait_ge(S["lam_in"], 1)
                nc.scalar.activation(lam[:, 1], lam[:, 0], ACT.Exp, scale=-1.0).then_inc(S["lam_exp"], 1)
                for m in range(MT):
                    act.wait_ge(S["q_done"], m + 1)
                    nc.scalar.copy(qk[:, m, 0:NH].rearrange("p (j g) d -> p g j d", g=NG),
                                   B[4 + m][:, :].rearrange("p (g j d) -> p g j d", g=NG, d=HD)).then_inc(S["qk_copied"], 1)
                act.wait_ge(S["ksvs_done"], MT)
                for m in range(MT):
                    v = B[7][:, m * 256:(m + 1) * 256].rearrange("p (k d) -> p k d", d=HD)
                    nc.scalar.copy(qk[:, m, 8:10], v[:, 0:2]).then_inc(S["qk_copied"], 1)
                    nc.scalar.copy(vsw[:, m, 0], v[:, 2:4]).then_inc(S["qk_copied"], 1)
                for m in range(MT):
                    act.wait_ge(S["kwvw_done"], m + 1)
                    v = B[m][:, 0:256].rearrange("p (k d) -> p k d", d=HD)
                    nc.scalar.copy(qk[:, m, 10:12], v[:, 0:2]).then_inc(S["qk_copied"], 1)
                    nc.scalar.copy(vsw[:, m, 1], v[:, 2:4]).then_inc(S["qk_copied"], 1)
                    nc.scalar.activation(tbr[:, m], B[m][:, 256:NKW], ACT.Tanh, scale=0.5).then_inc(S["qk_copied"], 1)
                for b in range(2):
                    act.wait_ge(S["rgx_done"], b + 1)
                    nc.scalar.copy(xc[:, 2 * b:2 * b + 2, CONV_W - 1:], B[2 + b][:, :].rearrange("p (i t) -> p i t", i=2))\
                        .then_inc(S["xc_ready"], 1)
                act.wait_ge(S["comp1_done"], 1)
                nc.scalar.activation(tc, B[6][:, 0:2 * NG * NB], ACT.Tanh, scale=0.5).then_inc(S["comp1_tanh"], 1)
                for m in range(MT):
                    act.wait_ge(S["qk_transposed"], m + 1)
                    b0, b1 = (B[4], B[5]) if m == 0 else (B[7], B[0])
                    nc.scalar.copy(qt[:, m], b0[:, :].rearrange("p (j t) -> p j t", j=HPG)).then_inc(S["qkt_ready"], 1)
                    nc.scalar.copy(kt[:, :, m * P:(m + 1) * P], b1[:, 0:256].rearrange("p (v t) -> p v t", v=2))\
                        .then_inc(S["qkt_ready"], 1)
                for b in range(2):
                    act.wait_ge(S["rgg_done"], b + 1)
                    nc.scalar.activation(sgr[:, 2 * b:2 * b + 2], B[2 + b][:, :].rearrange("p (i t) -> p i t", i=2),
                                         ACT.Tanh, scale=0.5).then_inc(S["rgg_tanh"], 1)
                act.wait_ge(S["half_ready"], 1)
                for g, (out, sem) in enumerate(((tr, S["tr_ready"]), (ti, S["ti_ready"]))):
                    for i in range(CT):
                        if i % 2 == 0:
                            act.wait_ge(S["lru_gates_done"], 2 * g + i // 2 + 1)
                        nc.scalar.activation(out[:, i], B[4 + 2 * g + i // 2][:, i % 2 * T:(i % 2 + 1) * T], ACT.Tanh,
                                             bias=half_b[:, g, i:i + 1], scale=0.5).then_inc(sem, 1)
                act.wait_ge(S["kc_transposed"], 1)
                nc.scalar.copy(kct[:, 0:NB], B[1][:, 256:256 + NB]).then_inc(S["kct_ready"], 1)
                act.wait_ge(S["c_ready"], 2)
                act.wait_ge(S["tr_ready"], CT)
                for i in range(CT):
                    nc.scalar.activation(aa[:, i], tr[:, i], ACT.Exp, bias=lam[:, 11, i:i + 1], scale=lam[:, 11, i:i + 1])\
                        .then_inc(S["aa_ready"], 1)
                act.wait_ge(S["aa_ready"], CT)
                for i in range(CT):
                    nc.scalar.activation(tr[:, i], tr[:, i], ACT.Tanh, bias=lam[:, 10, i:i + 1], scale=lam[:, 10, i:i + 1])\
                        .then_inc(S["th_ready"], 1)
                for m in range(MT):
                    act.wait_ge(S["nsag_done"], m + 1)
                    nc.scalar.activation(sgn[:, m], B[2 * m][:, :], ACT.Tanh, scale=0.5).then_inc(S["nsag_tanh"], 1)
                act.wait_ge(S["uq_in"], 1)
                nc.scalar.activation(tr, tr, ACT.Sqrt, scale=0.5).then_inc(S["uq_ready"], 1)
                for m in range(MT):
                    act.wait_ge(S["cmp_shifted"], m + 1)
                    nc.scalar.activation(cs[:, m], cs[:, m], ACT.Exp, scale=SCALE).then_inc(S["cmp_exp"], 1)

                def exps(n, heads=range(NH)):
                    br, m = STEPS[n]
                    act.wait_ge(S["masked"], n + 1)
                    for h in heads:
                        p = prob[n % 2][:, h, 0:(m + 1) * P]
                        nc.scalar.activation(p, p, ACT.Exp, bias=negmax[:, n % 2, h:h + 1], scale=SCALE,
                                             accum_out=den[:, m, 1 + br, h:h + 1]).then_inc(S["exp_done"], 1)

                def evacuate(n, groups=None):
                    for g in groups or range(GROUPS[n]):
                        k = sum(GROUPS[:n]) + g
                        if k >= NRING:
                            act.wait_ge(S["weighed"], k - NRING + 1)
                        act.wait_ge(S["p_transposed"], k + 1)
                        nc.scalar.copy(pt[:, k % NRING], B[k % 2][:, :].rearrange("p (b t) -> p b t", b=4)).then_inc(S["pt_ready"], 1)

                exps(0)
                for m in range(MT):
                    act.wait_ge(S["pc_transposed"], m + 1)
                    nc.scalar.copy(pct[:, m], B[m][:, 0:256].rearrange("p (g t) -> p g t", g=NG)).then_inc(S["pct_ready"], 1)
                exps(1)
                evacuate(0)
                evacuate(1)
                exps(2)
                for g in range(GROUPS[2]):
                    evacuate(2, [g])
                    exps(3, [2 * g, 2 * g + 1])
                evacuate(3)
                for m in range(MT):
                    act.wait_ge(S["yb_transposed"], m + 1)
                    nc.scalar.copy(ybt[:, :, m * P:(m + 1) * P], B[m][:, :].rearrange("p (k t) -> p k t", k=4)).then_inc(S["ybt_ready"], 1)
                for m in range(MT):
                    act.wait_ge(S["x_added"], 2 * (m + 1))
                    square(m, S["ss_ready"])
                arrive(act, "act")

        @block.tensor
        def _(pe):
            pe.wait_ge(mem["const_in"], 16)
            pe.wait_ge(mem["rows_in"], 16 * 7 * DEPTH)
            nc.tensor.transpose(B[7][:, 0:P], rows, ident).then_inc(mem["rows_transposed"], 1)
            with pe.Fori(0, DEPTH) as l:
                weights = (l + 1) * 16
                second = (l + 1) * 32
                first_of_two = l * 32 + 16

                for m in range(MT):
                    pe.wait_ge(S["xn_ready"], m + 1)
                    xn = XN[:, m * D:(m + 1) * D].rearrange("p (k c) -> p k c", c=KC)
                    for c in range(KC):
                        t = nc.tensor.transpose(B[2 * m + c // 4][:, c % 4 * P:(c % 4 + 1) * P], xn[:, :, c], ident)
                        if c % 4 == 3:
                            t.then_inc(S["h_transposed"], 1)

                def tokens(m, out, w, cols):
                    for c in range(KC):
                        mm = nc.tensor.matmul(out, ht[:, c, m * P:(m + 1) * P], w[:, c, cols], start=c == 0, stop=c == KC - 1)
                    return mm

                def features(out, w, cols):
                    for c in range(KC):
                        mm = nc.tensor.matmul(out, w[:, c, cols], ht[:, c, :], start=c == 0, stop=c == KC - 1)
                    return mm

                pe.wait_ge(loaded[Q_S], weights)
                for m in range(MT):
                    pe.wait_ge(S["ht_ready"], 2 * (m + 1))
                    tokens(m, B[4 + m][:, :], chunk(Q_S, 512), slice(0, 512)).then_inc(S["q_done"], 1)
                pe.wait_ge(loaded[KV_S], first_of_two)
                kv = chunk(KV_S, 512)
                for v in range(2):
                    features(B[6][:, v * T:(v + 1) * T], kv, slice(v * P, (v + 1) * P)).then_inc(S["kcvc_done"], 1)
                pe.wait_ge(S["params_ready"], 1)
                for m in range(MT):
                    tokens(m, B[7][:, m * 256:(m + 1) * 256], kv, slice(256, 512)).then_inc(S["ksvs_done"], 1)
                pe.wait_ge(loaded[KW_S], first_of_two)
                pe.wait_ge(mem["br_loaded"], weights)
                for m in range(MT):
                    tokens(m, B[m][:, 0:NKW], chunk(KW_S, NKW), slice(0, NKW)).then_inc(S["kwvw_done"], 1)
                pe.wait_ge(loaded[RGX_S], first_of_two)
                for i in range(CT):
                    mm = features(B[2 + i // 2][:, i % 2 * T:(i % 2 + 1) * T], chunk(RGX_S, 512), slice(i * P, (i + 1) * P))
                    if i % 2:
                        mm.then_inc(S["rgx_done"], 1)
                pe.wait_ge(S["z_ready"], 1)
                for v in range(2):
                    pe.wait_ge(mem["w1_loaded"][v], weights)
                    for i in range(LP):
                        mm = nc.tensor.matmul(B[6][:, v * NG * NB:(v + 1) * NG * NB], w1_c[:, v, i], z[:, v, i],
                                              start=i == 0, stop=i == LP - 1)
                mm.then_inc(S["comp1_done"], 1)
                pe.wait_ge(loaded[RGG_S], weights)
                pe.wait_ge(S["xc_ready"], 2)
                for i in range(CT):
                    mm = features(B[2 + i // 2][:, i % 2 * T:(i % 2 + 1) * T], chunk(RGG_S, 512), slice(i * P, (i + 1) * P))
                    if i % 2:
                        mm.then_inc(S["rgg_done"], 1)
                pe.wait_ge(S["qk_ready"], 1)
                for m in range(MT):
                    b0, b1 = (B[4], B[5]) if m == 0 else (B[7], B[0])
                    for j in range(HPG):
                        nc.tensor.transpose(b0[:, j * P:(j + 1) * P], qk[:, m, 2 * j:2 * j + 2].rearrange("p g d -> p (g d)"), ident)
                    for v in range(2):
                        t = nc.tensor.transpose(b1[:, v * P:(v + 1) * P], qk[:, m, 8 + 2 * v:10 + 2 * v].rearrange("p g d -> p (g d)"), ident)
                    t.then_inc(S["qk_transposed"], 1)
                pe.wait_ge(S["hid_ready"], 1)
                pe.wait_ge(mem["small_in"], weights * 9)
                for v in range(2):
                    for g in range(NG):
                        at = (v * NG + g) * NB
                        mm = nc.tensor.matmul(B[1][0:NB, (v * NG + g) * HD:(v * NG + g + 1) * HD], hc[:, at:at + NB], w2[:, v],
                                              start=True, stop=True)
                mm.then_inc(S["comp2_done"], 1)
                for g in range(2):
                    pe.wait_ge(S["qkt_ready"], 2 * (g + 1))
                    for i in range(CT):
                        pe.wait_ge(S["cv_ready"], i + 1)
                        mm = nc.tensor.matmul(B[4 + 2 * g + i // 2][:, i % 2 * T:(i % 2 + 1) * T], wri[:, g, i], cv[:, i],
                                              start=True, stop=True)
                        if i % 2:
                            mm.then_inc(S["lru_gates_done"], 1)
                pe.wait_ge(S["kc_ready"], 1)
                pe.wait_ge(S["vbd_ready"], 1)
                nc.tensor.transpose(B[1][:, 256:256 + NB], kc[0:NB].rearrange("p g d -> p (g d)"), ident[0:NB, 0:NB])\
                    .then_inc(S["kc_transposed"], 1)
                pe.wait_ge(loaded[NSAG_S], second)
                for m in range(MT):
                    if m:
                        pe.wait_ge(S["sgr_ready"], 1)
                    tokens(m, B[2 * m][:, :], chunk(NSAG_S, 512), slice(0, 512)).then_inc(S["nsag_done"], 1)
                pe.wait_ge(S["kct_ready"], 1)
                pe.wait_ge(S["sgr_ready"], 2)
                for m in range(MT):
                    for g in range(NG):
                        r = slice(64 * g, 64 * g + 64)
                        for j in range(HPG):
                            at = (m * HPG + j) * 16
                            mm = nc.tensor.matmul(B[(3, 1)[g]][:, at:at + NB], qt[r, m, j], kct[r, 0:NB], start=True, stop=True)
                        mm.then_inc(S["cmp_scores"], 1)

                def score(n):
                    br, m = STEPS[n]
                    for j in range(HPG):
                        for g in range(NG):
                            r = slice(64 * g, 64 * g + 64)
                            mm = nc.tensor.matmul(score_out(n, g * HPG + j), qt[r, m, j], kt[r, br, 0:(m + 1) * P],
                                                  start=True, stop=True)
                    mm.then_inc(S["scores"], 1)

                def transpose_group(n, g):
                    k = sum(GROUPS[:n]) + g
                    if k >= 2:
                        pe.wait_ge(S["pt_ready"], k - 1)
                    else:
                        pe.wait_ge(S["pct_ready"], k + 1)
                    for b, (h, key) in enumerate(pairs(n, g)):
                        t = nc.tensor.transpose(B[k % 2][:, b * P:(b + 1) * P], prob[n % 2][:, h, key * P:(key + 1) * P], ident)
                    t.then_inc(S["p_transposed"], 1)

                def weigh_group(n, g):
                    br, m = STEPS[n]
                    k = sum(GROUPS[:n]) + g
                    pe.wait_ge(S["pt_ready"], k + 1)
                    for b, (h, key) in enumerate(pairs(n, g)):
                        mm = nc.tensor.matmul(B[2 + n % 2][:, h * HD:(h + 1) * HD], pt[:, k % NRING, b], vsw[:, key, br, h // HPG],
                                              start=key == 0, stop=key == m)
                    mm.then_inc(S["weighed"], 1)

                def attend(n):
                    pe.wait_ge(S["exp_done"], NH * (n + 1))
                    pe.wait_ge(S["o_taken"], n + 1)
                    for g in range(GROUPS[n]):
                        transpose_group(n, g)
                        if g:
                            weigh_group(n, g - 1)
                    weigh_group(n, GROUPS[n] - 1)

                pe.wait_ge(S["tr_ready"], CT)
                score(0)
                pe.wait_ge(S["ti_ready"], CT)
                score(1)
                for m in range(MT):
                    pe.wait_ge(S["pc_ready"], m + 1)
                    if m == 0:
                        pe.wait_ge(S["sgn_ready"], 1)
                    for g in range(NG):
                        t = nc.tensor.transpose(B[m][:, g * P:(g + 1) * P], pc[:, m, g], ident)
                    t.then_inc(S["pc_transposed"], 1)
                pe.wait_ge(S["vbd_ready"], 1)
                for m in range(MT):
                    pe.wait_ge(S["pct_ready"], m + 1)
                    pe.wait_ge(S["sgn_ready"] if m == 0 else S["cmp_shifted"], 2)
                    for g in range(NG):
                        mm = nc.tensor.matmul(B[2 + m][:, g * 256:(g + 1) * 256], pct[:, m, g], vbd[:, g], start=True, stop=True)
                    mm.then_inc(S["cmp_out"], 1)
                attend(0)
                pe.wait_ge(S["masked"], 2)
                score(2)
                attend(1)
                pe.wait_ge(S["masked"], 3)
                score(3)
                attend(2)
                attend(3)
                for m in range(MT):
                    pe.wait_ge(S["yb_ready"], m + 1)
                    pe.wait_ge(S["pt_ready"], sum(GROUPS))
                    for k in range(4):
                        t = nc.tensor.transpose(B[m][:, k * P:(k + 1) * P],
                                                yb[:, m, 2 * k:2 * k + 2].rearrange("p h d -> p (h d)"), ident)
                    t.then_inc(S["yb_transposed"], 1)
                pe.wait_ge(S["masked"], 4)
                pe.wait_ge(S["ya_ready"], CT)
                for h in range(2):
                    pe.wait_ge(loaded[WO_S[h]], second)
                for m in range(MT):
                    pe.wait_ge(S["ybt_ready"], m + 1)
                    for h in range(2):
                        for k in range(KC):
                            y = cv[:, k, m * P:(m + 1) * P] if k < CT else ybt[:, k - CT, m * P:(m + 1) * P]
                            mm = nc.tensor.matmul(B[4 + 2 * m + h][:, :], y, w_out_c[h][:, k, :], start=k == 0, stop=k == KC - 1)
                        mm.then_inc(S["out_done"], 1)
                arrive(pe, "pe")

        @block.vector
        def _(dve):
            dve.wait_ge(mem["zeroed"], 4)
            dve.wait_ge(mem["x_in"], 16)
            with dve.Fori(0, DEPTH) as l:
                after = Chain(dve, S["dve_step"])
                V = nc.vector
                dve.wait_ge(mem["first_rstd"], 1)
                for m in range(MT):
                    V.tensor_scalar(XN[:, m * D:(m + 1) * D], X[:, m * D:(m + 1) * D], rstd[:, m:m + 1], None, ALU.mult)\
                        .then_inc(S["xn_ready"], 1)
                dve.wait_ge(mem["norm_in"], 16)
                for m in range(MT):
                    for b in range(2):
                        dve.wait_ge(S["h_transposed"], 2 * m + b + 1)
                        V.tensor_tensor(ht[:, 4 * b:4 * b + 4, m * P:(m + 1) * P], B[2 * m + b][:, :].rearrange("p (c t) -> p c t", c=4),
                                        shape(norm_g[:, bass.ds(l, 1), 4 * b:4 * b + 4].rearrange("p l c -> p c l"), P, 4, P), ALU.mult)\
                            .then_inc(S["ht_ready"], 1)
                dve.wait_ge(mem["small_in"], (l + 1) * 16 * 9)
                V.tensor_copy(gain12[:, 0:8], shape(gain[:, 0:1], P, 8, HD))
                after(V.tensor_copy(gain12[:, 8:12].rearrange("p (v g) d -> p v g d", v=2),
                                    shape(gain[:, 1:3].unsqueeze(2), P, 2, NG, HD)))
                dve.wait_ge(S["params_ready"], 1)
                pl = params[:, ROW_LAM:ROW_LAM + 4]
                after(V.tensor_scalar(lam[:, 7], pl, -1.0, 0.0, ALU.mult, ALU.max))
                V.scalar_tensor_tensor(lam[:, 0], lam[:, 7], 2.0, pl, ALU.mult, ALU.add).then_inc(S["lam_in"], 1)
                dve.wait_ge(S["lam_exp"], 1)
                log1p_of(V, after, lam)
                after(V.scalar_tensor_tensor(lam[:, 9], lam[:, 8], 2.0, lam[:, 7], ALU.mult, ALU.add))
                V.tensor_scalar(lam[:, 10], lam[:, 9], 4.0, None, ALU.mult).then_inc(S["c_ready"], 1)
                V.tensor_scalar(lam[:, 11], lam[:, 9], -4.0, None, ALU.mult).then_inc(S["c_ready"], 1)
                dve.wait_ge(S["kcvc_done"], 2)
                for v in range(2):
                    for g in range(NG):
                        src = B[6][64 * g:64 * g + 64, v * T:(v + 1) * T]
                        for t in range(2):
                            rws = slice(64 * t, 64 * t + 64)
                            tok = src.rearrange("p (b i t) -> p t i b", t=2, i=LP // 2)[:, t]
                            row = (ROW_PEK, ROW_PEV)[v]
                            for half in range(2):
                                i = slice(half * LP // 2, (half + 1) * LP // 2)
                                pe = shape(params[rws, row + i.start:row + i.stop].unsqueeze(2), 64, LP // 2, NB)
                                ins = V.tensor_tensor(z[rws, v, i, g * NB:(g + 1) * NB], tok[:, :, half:half + NB], pe, ALU.add)
                ins.then_inc(S["z_ready"], 1)
                dve.wait_ge(S["qk_copied"], 12)
                flat = qk.rearrange("p m k d -> p (m k) d")
                after(V.tensor_tensor(sqk, flat, flat, ALU.mult))
                V.tensor_reduce(ssq, sqk, AX.X, ALU.add).then_inc(S["qk_ss"], 1)
                for i in range(CT):
                    if i % 2 == 0:
                        dve.wait_ge(S["xc_ready"], i // 2 + 1)
                    w = lambda k: params[:, ROW_CONV + 4 * k + i:ROW_CONV + 4 * k + i + 1]
                    after(V.tensor_scalar(cv[:, i], xc[:, i, 0:T], w(0), params[:, ROW_CB + i:ROW_CB + i + 1], ALU.mult, ALU.add))
                    for k in range(1, CONV_W):
                        ins = V.scalar_tensor_tensor(cv[:, i], xc[:, i, k:k + T], w(k), cv[:, i], ALU.mult, ALU.add)
                        if k < CONV_W - 1:
                            after(ins)
                    ins.then_inc(S["cv_ready"], 1)
                dve.wait_ge(S["qk_rstd"], 1)
                after(V.tensor_tensor(flat, flat, shape(rsq.unsqueeze(2), P, MT * 12, HD), ALU.mult))
                after(V.tensor_tensor(qk, qk, shape(gain12.unsqueeze(1), P, MT, 12, HD), ALU.mult))
                cos, sin = [const("pos_" + n).rearrange("p (m r) -> p m r", m=MT) for n in ("cos", "sin")]
                wide = lambda t, lo, hi: shape(t[:, :, lo:hi].unsqueeze(2), P, MT, 12, hi - lo)
                V.tensor_tensor(rot_a, qk[:, :, :, 0:ROPE], wide(cos, 0, ROPE), ALU.mult)
                V.tensor_tensor(rot_b[:, :, :, 0:8], qk[:, :, :, 8:16], wide(sin, 0, 8), ALU.mult)
                after(V.tensor_tensor(rot_b[:, :, :, 8:16], qk[:, :, :, 0:8], wide(sin, 8, 16), ALU.mult))
                V.tensor_tensor(qk[:, :, :, 0:ROPE], rot_a, rot_b, ALU.add).then_inc(S["qk_ready"], 1)
                dve.wait_ge(S["comp1_tanh"], 1)
                V.scalar_tensor_tensor(hc, tc, 1.0, B[6][:, 0:2 * NG * NB], ALU.add, ALU.mult).then_inc(S["hid_ready"], 1)
                dve.wait_ge(S["comp2_done"], 1)
                kn, kan, kbn = kc[0:NB], ka[0:NB], kb[0:NB]
                after(V.tensor_scalar(kn, B[1][0:NB, 0:NG * HD].rearrange("p (g d) -> p g d", g=NG), 0.5, None, ALU.mult))
                after(V.tensor_tensor(kan, kn, kn, ALU.mult))
                V.tensor_reduce(ssk[0:NB], kan, AX.X, ALU.add).then_inc(S["kc_ss"], 1)
                for g in range(NG):
                    for j in range(HPG):
                        ins = V.tensor_scalar(vbd[32 * j:32 * j + NB, g, j * HD:(j + 1) * HD],
                                              B[1][0:NB, (NG + g) * HD:(NG + g + 1) * HD], 0.5, None, ALU.mult)
                ins.then_inc(S["vbd_ready"], 1)
                dve.wait_ge(S["kc_rstd"], 1)
                after(V.tensor_tensor(kn, kn, shape(rsk[0:NB].unsqueeze(2), NB, NG, HD), ALU.mult))
                after(V.tensor_tensor(kn, kn, shape(gain_c[0:NB].unsqueeze(1), NB, NG, HD), ALU.mult))
                ec, es = [shape(const("end_" + n)[0:NB].unsqueeze(1), NB, NG, ROPE) for n in ("cos", "sin")]
                V.tensor_tensor(kan[:, :, 0:ROPE], kn[:, :, 0:ROPE], ec, ALU.mult)
                V.tensor_tensor(kbn[:, :, 0:8], kn[:, :, 8:16], es[:, :, 0:8], ALU.mult)
                after(V.tensor_tensor(kbn[:, :, 8:16], kn[:, :, 0:8], es[:, :, 8:16], ALU.mult))
                V.tensor_tensor(kn[:, :, 0:ROPE], kan[:, :, 0:ROPE], kbn, ALU.add).then_inc(S["kc_ready"], 1)
                for b in range(2):
                    dve.wait_ge(S["rgg_tanh"], b + 1)
                    g2 = sgr[:, 2 * b:2 * b + 2]
                    V.scalar_tensor_tensor(g2, g2, 1.0, B[2 + b][:, :].rearrange("p (i t) -> p i t", i=2), ALU.add, ALU.mult)\
                        .then_inc(S["sgr_ready"], 1)
                dve.wait_ge(S["th_ready"], CT)
                xt = xc[:, :, CONV_W - 1:]
                after(V.tensor_scalar(xt, tr, 1.0, None, ALU.add))
                after(V.reciprocal(xt, xt))
                V.tensor_tensor(tr, tr, xt, ALU.mult).then_inc(S["uq_in"], 1)
                dve.wait_ge(S["ti_ready"], CT)
                dve.wait_ge(S["lru_gates_done"], 4)
                after(V.scalar_tensor_tensor(cv, ti, 1.0, cv, ALU.add, ALU.mult))
                for m in range(MT):
                    dve.wait_ge(S["nsag_tanh"], m + 1)
                    V.scalar_tensor_tensor(sgn[:, m], sgn[:, m], 1.0, B[2 * m][:, :], ALU.add, ALU.mult).then_inc(S["sgn_ready"], 1)
                dve.wait_ge(S["cmp_scores"], MT * NG)
                for m in range(MT):
                    neg = const("cmp_neg")[:, m * NB:(m + 1) * NB]
                    for g in range(NG):
                        sc = view(B[(3, 1)[g]][:, m * 64:(m + 1) * 64], HPG, 16)[:, :, 0:NB]
                        ins = V.tensor_tensor(cs[:, m, g * HPG:(g + 1) * HPG], sc, shape(neg.unsqueeze(1), P, HPG, NB), ALU.add)
                    after(ins)
                    after(V.tensor_reduce(cmax, cs[:, m], AX.X, ALU.max))
                    V.tensor_tensor(cs[:, m], cs[:, m], shape(cmax.unsqueeze(2), P, NH, NB), ALU.subtract).then_inc(S["cmp_shifted"], 1)
                    if m == 0:
                        dve.wait_ge(S["cmp_shifted"], 1)

                def mask(n):
                    br, m = STEPS[n]
                    dve.wait_ge(S["scores"], n + 1)
                    if n >= 2:
                        dve.wait_ge(S["p_transposed"], sum(GROUPS[:n - 1]))
                    for h in range(NH):
                        ins = V.tensor_tensor_reduce(out=prob[n % 2][:, h, 0:(m + 1) * P], in0=score_out(n, h),
                                                     in1=const("causal")[:, (1 - m) * P:], scale=1.0, scalar=LOWEST,
                                                     op0=ALU.add, op1=ALU.max, accum_out=rowmax[:, n % 2, h:h + 1])
                    after(ins)
                    if n >= 2:
                        dve.wait_ge(S["exp_done"], NH * (n - 1))
                    V.tensor_scalar(negmax[:, n % 2], rowmax[:, n % 2], -SCALE, None, ALU.mult).then_inc(S["masked"], 1)

                def take(n, br, m, bank, first):
                    after(V.reciprocal(rden, den[:, m, br]))
                    after(V.scalar_tensor_tensor(coef[:, m, br], tbr[:, m].rearrange("p (h b) -> p b h", b=3)[:, br], 1.0, rden,
                                                 ALU.add, ALU.mult))
                    o = bank[:, :].rearrange("p (h d) -> p h d", h=NH)
                    by = shape(coef[:, m, br].unsqueeze(2), P, NH, HD)
                    if first:
                        V.tensor_tensor(yb[:, m], o, by, ALU.mult).then_inc(S["o_taken"], 1)
                        dve.wait_ge(S["o_taken"], n)
                    else:
                        V.tensor_tensor(tmp, o, by, ALU.mult).then_inc(S["o_taken"], 1)
                        dve.wait_ge(S["o_taken"], n)
                        after(V.tensor_tensor(yb[:, m], yb[:, m], tmp, ALU.add))

                def finish(m):
                    yf = yb[:, m].rearrange("p h d -> p (h d)")
                    V.scalar_tensor_tensor(yf, yf, 0.25, sgn[:, m], ALU.mult, ALU.mult).then_inc(S["yb_ready"], 1)

                mask(0)
                for m in range(MT):
                    dve.wait_ge(S["cmp_exp"], m + 1)
                    V.tensor_reduce(den[:, m, 0], cs[:, m], AX.X, ALU.add)
                    one = const("cmp_one")[:, m * NB:(m + 1) * NB]
                    V.tensor_tensor(pc[:, m].rearrange("p g (j k) -> p (g j) k", k=32)[:, :, 0:NB], cs[:, m],
                                    shape(one.unsqueeze(1), P, NH, NB), ALU.mult).then_inc(S["pc_ready"], 1)
                dve.wait_ge(S["pc_ready"], 2)
                mask(1)
                for m in range(MT):
                    dve.wait_ge(S["cmp_out"], m + 1)
                    take(m + 1, 0, m, B[2 + m], True)
                dve.wait_ge(S["uq_ready"], 1)
                after(V.tensor_tensor(cv, cv, tr, ALU.mult))
                for i in range(CT):
                    ins = V.tensor_tensor_scan(ti[:, i], aa[:, i], cv[:, i], 0.0, ALU.mult, ALU.add)
                after(ins)
                for i in range(CT):
                    V.scalar_tensor_tensor(cv[:, i], ti[:, i], 0.5, sgr[:, i], ALU.mult, ALU.mult).then_inc(S["ya_ready"], 1)
                mask(2)
                dve.wait_ge(S["weighed"], sum(GROUPS[:1]))
                take(3, 1, 0, B[2], False)
                mask(3)
                dve.wait_ge(S["weighed"], sum(GROUPS[:2]))
                take(4, 2, 0, B[3], False)
                finish(0)
                dve.wait_ge(S["weighed"], sum(GROUPS[:3]))
                take(5, 1, 1, B[2], False)
                dve.wait_ge(S["weighed"], sum(GROUPS[:4]))
                take(6, 2, 1, B[3], False)
                finish(1)
                for m in range(MT):
                    for h in range(2):
                        dve.wait_ge(S["out_done"], 2 * m + h + 1)
                        x = X[:, m * D + h * 512:m * D + (h + 1) * 512]
                        V.tensor_tensor(x, x, B[4 + 2 * m + h][:, :], ALU.add).then_inc(S["x_added"], 1)
                dve.wait_ge(S["x_added"], 2 * MT)
                dve.drain()
                dve.wait_ge(arrived, 4)
                dve.sem_clear(layer_sems)
                dve.sem_clear(arrived)
                for r in release.values():
                    dve.sem_inc(r, 1)


def log1p_of(V, after, w):
    after(V.tensor_scalar(w[:, 2], w[:, 1], 2.0, None, ALU.add))
    after(V.reciprocal(w[:, 3], w[:, 2]))
    after(V.tensor_tensor(w[:, 4], w[:, 1], w[:, 3], ALU.mult))
    after(V.tensor_tensor(w[:, 5], w[:, 4], w[:, 4], ALU.mult))
    after(V.tensor_scalar(w[:, 6], w[:, 5], 1.0 / 17, None, ALU.mult))
    for k in range(15, 1, -2):
        after(V.scalar_tensor_tensor(w[:, 6], w[:, 6], 1.0 / k, w[:, 5], ALU.add, ALU.mult))
    after(V.scalar_tensor_tensor(w[:, 8], w[:, 6], 1.0, w[:, 4], ALU.add, ALU.mult))


ROW_MU, ROW_W0, ROW_A0, ROW_KK, ROW_KA, ROW_RK, NROWS2 = 0, 14, 18, 22, 26, 30, 34
LORA = 64
RW = 512
COL2_R, COL2_PW, COL2_K, COL2_V, COL2_PA = 0, RW, RW + LORA, 2 * RW + LORA, 3 * RW + LORA
COL2_FQ = COL2_PA + LORA + P
COL2_FK, COL2_FV, COL2_F = COL2_FQ + 512, COL2_FQ + 1024, COL2_FQ + 1536
N_IN2 = COL2_F + NH
LORA_W = 2 * LORA + P + NH
FQ_S, FK_S, FV_S, LORA_S, R_S, K_S, V_S, WO2_S = 0, 4, 5, 1, 2, 3, 0, (2, 3)
DECAY = float(np.exp(np.float32(-0.5)))
NTILE = 14


def load_mixer_weights(sp, a, slot, loaded, name):
    win = a["w_in_2"]

    def load(s, at, cols, width):
        dst = slot[:, s, 0:KC * width].rearrange("p (c n) -> p c n", c=KC)[:, :, at:at + cols[1] - cols[0]]
        sp.dma_start(dst, win[0, :, cols[0]:cols[1]].rearrange("(p c) n -> p c n", c=KC)).then_inc(loaded[s], 16)

    wide = {"fq": (FQ_S, COL2_FQ), "fk": (FK_S, COL2_FK), "fv": (FV_S, COL2_FV), "r": (R_S, COL2_R), "k": (K_S, COL2_K), "v": (V_S, COL2_V)}
    if name == "lora":
        load(LORA_S, 0, (COL2_PW, COL2_PW + LORA), LORA_W)
        load(LORA_S, LORA, (COL2_PA, COL2_FQ), LORA_W)
        load(LORA_S, 2 * LORA + P, (COL2_F, N_IN2), LORA_W)
    else:
        s, c = wide[name]
        load(s, 0, (c, c + 512), 512)


def mixer_part(nc, ctx, a, mem, psum, layout, first, second):
    slot, loaded = mem["slots"], mem["loaded"]
    X, XN, HT = mem["x"], mem["xn"], mem["ht"]
    B = psum
    room = carve(mem["region"][:, 0:REGION - D - CONST3])
    const2 = room(second - first)

    def const(name):
        at, w = layout[name]
        return const2[:, at - first:at - first + w] if at >= first else mem["const"][:, at:at + w]

    ident = const("ident")
    rows, norm_g, params = mem["rows2"], mem["norm_g2"], room(NROWS2)
    gain, b_f = room(2, HD), room(NH)
    lora_w, g2 = room(RW), room(RW)
    ln_w, ln_b = room(RW), room(RW)
    ss, rstd = mem["square_sum"], mem["rstd"]
    ssq, rsq = room(MT * 2 * NH), room(MT * 2 * NH)
    half_b = room(2, CT)
    f8, wk = room(MT * NH), room(9, MT * NH)
    rowmax, negmax, den = room(2, NH), room(2, NH), room(2, NH)
    rden = room(NH)
    bonus = room(MT, NH)
    last = room(CT, T // CHUNK)
    mean, var, rvar = room(MT * NH), room(MT * NH), room(MT * NH)
    raw_flat = room(NTILE * (T + 1))
    raw = view(raw_flat, NTILE, T + 1)
    ps = room(NTILE, T)
    r_, k_, v_ = ps[:, 0:4], ps[:, 4:8], ps[:, 8:12]
    aa, gt, ld, kk = room(CT, T), room(CT, T), room(CT, T), room(CT, T)
    qk_flat, v2 = room(MT * 2 * NH * HD), room(MT, NH * HD)
    qk = view(qk_flat, MT, 2 * NH, HD)
    yft = room(4, T)
    ht = view(HT[:, :], KC, T)
    lc, ex, ei = [view(raw_flat[:, i * CT * T:(i + 1) * CT * T], CT, T) for i in range(3)]
    room45 = carve(slot[:, 4:6].rearrange("p s n -> p (s n)"))
    qt, kt = room45(4, T), room45(4, T)
    pt = room45(4, 4, P)
    sqk = room45(MT * 2 * NH, HD)
    yf = view(pt.rearrange("p a b t -> p (a b t)")[:, 0:MT * RW], MT, RW)
    prob = [view(qk_flat[:, 0:NH * P], NH, P), view(XN[:, :], NH, T)]
    room45 = carve(slot[:, 4:6].rearrange("p s n -> p (s n)"))
    am, wu = room45(MT, NH, P), room45(MT, NH, P)
    rbt, rkt = room45(MT, NH, P), room45(MT, NH, P)
    room01 = carve(slot[:, 0:2].rearrange("p s n -> p (s n)"))
    btok, ktok, vtok = room01(MT, RW), room01(MT, RW), room01(MT, RW)
    wt = room01(MT, CT, P)
    rk = room01(CT, T)
    state = room01(T // CHUNK + 1, CT, HD)
    chunks = [view(XN[:, :], 4, 2, CT, HD), view(HT[:, :], 4, 2, CT, HD)]
    flats = [qk_flat, v2.rearrange("p m n -> p (m n)")] + [t.rearrange("p i t -> p (i t)") for t in (lc, kk, ex, ei)]
    units = [view(f[:, i:i + 512], 4, P) for f in flats for i in range(0, f.shape[1], 512)]
    W = []
    for u in range(2):
        w = dict(zip(("NT", "N", "NO", "F", "AKT", "P2", "P2T"), units[7 * u:7 * u + 7]))
        w.update(P4=w["NT"], P4T=w["N"], P8=w["P2"], XD=w["P2T"], Q=w["AKT"])
        W.append(w)
    yr, yrt = view(ex.rearrange("p i t -> p (i t)"), MT * NH, HD), ei
    ysq = lc.rearrange("p i t -> p (i t)")

    names = """small_in const2_in ss_ready rstd_ready xn_ready params_transposed params_ready h_transposed ht_ready
        fq_done fk_done fv_done f_done lora_done rkv_done raw_ready qkv_copied f_ready f_abs f_exp qk_ss qk_rstd qk_ready
        qk_transposed qkt_ready scores masked exp_done p_transposed pt_ready weighed yf_ready yf_transposed yft_ready
        shifted lora_in lora_mul lora_tanh gates_ready kk_sq kk_sum kk_bound kk_inverse kk_root lc_ready decays_ready
        scaled tok_transposed tok_ready bonus_done bonus_ready unit_made unit_taken chunk_made chunk_taken
        state_made state_ready sa_made sa_ready y_made y_taken y_var y_rstd y_ready y_transposed yrt_ready
        out_done x_added dve_step pool_step""".split()
    S, mixer_sems = semaphores(nc, ctx, names, "_2")
    GROUPS = [2, 4]
    of_tile = lambda t, m: t[:, m * NH:(m + 1) * NH]
    NCH = T // CHUNK
    STAGES = "NT N AKT RBT RKT P2 P2T MV P4 P4T F2 P8 F3 F4 XD Q F5 WU WT".split()

    def order(m, u, stage):
        return (m * len(STAGES) + STAGES.index(stage)) * 2 + u

    def y_bank(m, u):
        return B[(6, 7, 4, 5)[2 * m + u]]

    def score_out(m, h):
        i, u = divmod(h, 2)
        return B[2 + u][:, i * P:(i + 1) * P] if m == 0 else B[4 + 2 * u + i // 2][:, i % 2 * T:(i % 2 + 1) * T]

    def pairs(m, g):
        return [((4 * g + b) // (m + 1), (4 * g + b) % (m + 1)) for b in range(4)]

    with nc.Block() as block:

        @block.sync
        def _(sp):
            sp.wait_ge(S["fq_done"], MT)
            load_mixer_weights(sp, a, slot, loaded, "v")
            wout = a["w_out_2"]
            for h in range(2):
                sp.wait_ge(S["rkv_done"], 2 * (h + 1))
                dst = slot[:, WO2_S[h], :].rearrange("p (k n) -> p k n", k=KC)
                sp.dma_start(dst, wout[0, :, h * 512:(h + 1) * 512].rearrange("(k p) n -> p k n", p=P)).then_inc(loaded[WO2_S[h]], 16)
            sp.wait_ge(S["y_made"], 2 * MT)
            load_first_experts(sp, a, mem, EARLY[:3])
            sp.wait_ge(S["y_ready"], MT)
            load_first_experts(sp, a, mem, EARLY[3:])
            for i in range(2):
                sp.wait_ge(S["out_done"], 3 + i)
                load_first_experts(sp, a, mem, LATE[i:i + 1])

        @block.gpsimd
        def _(pool):
            nc.gpsimd.memset(raw[:, :, 0:1], 0.0).then_inc(S["pool_step"], 1)
            steps = [1]

            def inv_root(out, src, scale, eps, ready, n, done):
                pool.wait_ge(ready, n)
                nc.gpsimd.tensor_scalar(out, src, scale, eps, ALU.mult, ALU.add).then_inc(S["pool_step"], 1)
                steps[0] += 1
                pool.wait_ge(S["pool_step"], steps[0])
                nc.gpsimd.tensor_tensor(out, out, const("minus_half")[0:out.shape[0], 0:out.shape[1]], ALU.pow).then_inc(done, 1)

            inv_root(rsq, ssq, 1.0 / HD, EPS, S["qk_ss"], 1, S["qk_rstd"])
            for m in range(MT):
                inv_root(of_tile(rvar, m), of_tile(var, m), 1.0 / HD, 64e-5, S["y_var"], m + 1, S["y_rstd"])
            for m in range(MT):
                inv_root(rstd[:, m:m + 1], ss[:, m:m + 1], 1.0 / D, EPS, S["ss_ready"], m + 1, S["rstd_ready"])

        @block.scalar
        def _(act):
            n = [0]

            def small(dst, src):
                act.dma_start(dst, src).then_inc(S["small_in"], 16)
                n[0] += 1

            act.dma_start(const2, a["constants"][:, first:first + const2.shape[1]]).then_inc(S["const2_in"], 16)
            small(gain[:, 0], shape(a["fox_q_norm_w_2"], P, HD))
            small(gain[:, 1], shape(a["fox_k_norm_w_2"], P, HD))
            small(b_f, shape(a["fox_b_f_2"], P, NH))
            small(lora_w[0:LORA], a["rw_w2_2"][0])
            small(lora_w[LORA:P], a["rw_a2_2"][0])
            small(g2, a["rw_g2_2"][0])
            small(ln_w, shape(a["rw_ln_w_2"], P, RW))
            small(ln_b, shape(a["rw_ln_b_2"], P, RW))
            w_route, b_route, const3, gain3 = router_memory(mem)
            act.dma_start(gain3, shape(a["norm_ffn_w_2"], P, D)).then_inc(mem["router_in"], 16)
            act.dma_start(const3, a["constants"][:, second:second + const3.shape[1]]).then_inc(mem["router_in"], 16)
            act.dma_start(w_route[:, :, 0:NGROUP], a["router_group_w_2"][0].rearrange("(p c) n -> p c n", c=KC)).then_inc(mem["router_in"], 16)
            act.dma_start(w_route[:, :, NGROUP:], a["router_expert_w_2"][0].rearrange("(p c) n -> p c n", c=KC)).then_inc(mem["router_in"], 16)
            act.dma_start(b_route[:, 0:NGROUP], shape(a["router_group_b_2"], P, NGROUP)).then_inc(mem["router_in"], 16)
            act.dma_start(b_route[:, NGROUP:], shape(a["router_expert_b_2"], P, NE)).then_inc(mem["router_in"], 16)
            assert n[0] == N_SMALL2
            act.wait_ge(S["params_transposed"], 1)
            nc.scalar.copy(params, B[7][:, 0:NROWS2]).then_inc(S["params_ready"], 1)
            act.wait_ge(S["params_ready"], 1)
            nc.scalar.mul(half_b.rearrange("p a b -> p (a b)"), params[:, ROW_W0:ROW_KK], 0.5).then_inc(S["params_ready"], 1)
            for m in range(MT):
                act.wait_ge(S["fq_done"], m + 1)
                nc.scalar.copy(qk[:, m, 0:NH], view(B[4 + m][:, :], NH, HD)).then_inc(S["qkv_copied"], 1)
            for m in range(MT):
                act.wait_ge(S["fk_done"], m + 1)
                nc.scalar.copy(qk[:, m, NH:], view(B[6 + m][:, :], NH, HD)).then_inc(S["qkv_copied"], 1)
            for m in range(MT):
                act.wait_ge(S["fv_done"], m + 1)
                nc.scalar.copy(v2[:, m], B[m][:, :]).then_inc(S["qkv_copied"], 1)
            act.wait_ge(S["f_abs"], 1)
            nc.scalar.activation(wk[:, 1], wk[:, 0], ACT.Exp, scale=-1.0).then_inc(S["f_exp"], 1)
            act.wait_ge(S["pool_step"], 1)
            act.wait_ge(S["lora_done"], 1)
            nc.scalar.copy(raw[:, 12:14, 1:], view(B[3][:, :], 2, T)).then_inc(S["raw_ready"], 1)
            for b in range(4):
                act.wait_ge(S["rkv_done"], b + 1)
                nc.scalar.copy(raw[:, 2 * b:2 * b + 2, 1:], view(B[b][:, :], 2, T)).then_inc(S["raw_ready"], 1)
            for m in range(MT):
                act.wait_ge(S["qk_transposed"], m + 1)
                nc.scalar.copy(qt[:, :, m * P:(m + 1) * P], view(B[4 + 2 * m][:, :], 4, P)).then_inc(S["qkt_ready"], 1)
                nc.scalar.copy(kt[:, :, m * P:(m + 1) * P], view(B[5 + 2 * m][:, :], 4, P)).then_inc(S["qkt_ready"], 1)
            for b in range(2):
                act.wait_ge(S["rkv_done"], 5 + b)
                nc.scalar.copy(raw[:, 8 + 2 * b:10 + 2 * b, 1:], view(B[b][:, :], 2, T)).then_inc(S["raw_ready"], 1)
            act.wait_ge(S["shifted"], 2)
            nc.scalar.activation(ps[0:LORA, 12], ps[0:LORA, 12], ACT.Tanh).then_inc(S["lora_in"], 1)
            nc.scalar.activation(ps[:, 13], ps[:, 13], ACT.Tanh, scale=0.5).then_inc(S["lora_in"], 1)
            for m in range(MT):
                act.wait_ge(S["masked"], m + 1)
                for h in range(NH):
                    p = prob[m][:, h]
                    nc.scalar.activation(p, p, ACT.Exp, bias=negmax[:, m, h:h + 1], scale=SCALE,
                                         accum_out=den[:, m, h:h + 1]).then_inc(S["exp_done"], 1)
                for g in range(GROUPS[m]):
                    k = sum(GROUPS[:m]) + g
                    if k >= 4:
                        act.wait_ge(S["weighed"], k - 3)
                    act.wait_ge(S["p_transposed"], k + 1)
                    nc.scalar.copy(pt[:, k % 4], view(B[k % 2][:, :], 4, P)).then_inc(S["pt_ready"], 1)
            act.wait_ge(S["kk_inverse"], 1)
            nc.scalar.activation(lc, lc, ACT.Sqrt).then_inc(S["kk_root"], 1)
            for m in range(MT):
                act.wait_ge(S["yf_transposed"], m + 1)
                nc.scalar.copy(yft[:, :, m * P:(m + 1) * P], view(B[4 + m][:, :], 4, P)).then_inc(S["yft_ready"], 1)
            act.wait_ge(S["params_ready"], 2)
            for g, out in enumerate((ld, aa)):
                for i in range(CT):
                    if i % 2 == 0:
                        act.wait_ge(S["lora_mul"], 2 * g + i // 2 + 1)
                    bank = B[(6, 7, 0, 1)[2 * g + i // 2]]
                    nc.scalar.activation(out[:, i], bank[:, i % 2 * T:(i % 2 + 1) * T], ACT.Tanh, bias=half_b[:, g, i:i + 1],
                                         scale=0.5).then_inc(S["lora_tanh"], 1)
            for b in range(2):
                act.wait_ge(S["lora_mul"], 5 + b)
                nc.scalar.copy(gt[:, 2 * b:2 * b + 2], view(B[2 + b][:, :], 2, T)).then_inc(S["gates_ready"], 1)
            act.wait_ge(S["lc_ready"], 1)
            nc.scalar.activation(ex, lc, ACT.Exp).then_inc(S["decays_ready"], 1)
            nc.scalar.activation(ei, lc, ACT.Exp, scale=-1.0).then_inc(S["decays_ready"], 1)
            act.wait_ge(S["lc_ready"], 2)
            nc.scalar.activation(ld, ld, ACT.Exp).then_inc(S["decays_ready"], 1)
            for m in range(MT):
                act.wait_ge(S["tok_transposed"], m + 1)
                nc.scalar.copy(vtok[:, m], B[m][:, :]).then_inc(S["tok_ready"], 1)
            for m in range(MT):
                act.wait_ge(S["tok_transposed"], 2 + m + 1)
                nc.scalar.copy(am[:, m, :, 0:HD], view(B[2 + m][:, :], NH, HD)).then_inc(S["tok_ready"], 1)
            for j, dst in enumerate((btok, ktok)):
                for m in range(MT):
                    act.wait_ge(S["tok_transposed"], 4 + 2 * j + m + 1)
                    nc.scalar.copy(dst[:, m], B[4 + 2 * j + m][:, :]).then_inc(S["tok_ready"], 1)
            act.wait_ge(S["bonus_done"], 1)
            nc.scalar.copy(bonus.rearrange("p m h -> p (m h)"), B[0][:, 0:MT * NH]).then_inc(S["bonus_ready"], 1)
            for q in range(NCH):
                m, c = divmod(q, 4)
                act.wait_ge(S["chunk_made"], m + 1)
                nc.scalar.copy(chunks[m][:, c].rearrange("p x i k -> p (x i k)"), B[q % 8][:, :]).then_inc(S["chunk_taken"], 1)
            for m in range(MT):
                act.wait_ge(S["x_added"], 2 * (m + 1))
                nc.scalar.activation((ysq, kk.rearrange("p i t -> p (i t)"))[m], X[:, m * D:(m + 1) * D], ACT.Square, accum_out=ss[:, m:m + 1]).then_inc(S["ss_ready"], 1)

        @block.tensor
        def _(pe):
            pe.wait_ge(mem["rows2_in"], 16 * N_ROWS2)
            nc.tensor.transpose(B[7][:, 0:NROWS2], rows[0:NROWS2], ident[0:NROWS2, 0:NROWS2]).then_inc(S["params_transposed"], 1)
            for m in range(MT):
                pe.wait_ge(S["xn_ready"], m + 1)
                xn = XN[:, m * D:(m + 1) * D].rearrange("p (k c) -> p k c", c=KC)
                for c in range(KC):
                    t = nc.tensor.transpose(B[2 * m + c // 4][:, c % 4 * P:(c % 4 + 1) * P], xn[:, :, c], ident)
                    if c % 4 == 3:
                        t.then_inc(S["h_transposed"], 1)

            def chunk(s, width=512):
                return slot[:, s, 0:KC * width].rearrange("p (c n) -> p c n", c=KC)

            def tokens(m, out, w, cols):
                for c in range(KC):
                    mm = nc.tensor.matmul(out, ht[:, c, m * P:(m + 1) * P], w[:, c, cols], start=c == 0, stop=c == KC - 1)
                return mm

            def features(out, w, cols):
                for c in range(KC):
                    mm = nc.tensor.matmul(out, w[:, c, cols], ht[:, c, :], start=c == 0, stop=c == KC - 1)
                return mm

            for s, uses, bank, done in ((FQ_S, 1, 4, S["fq_done"]), (FK_S, 0, 6, S["fk_done"]), (FV_S, 1, 0, S["fv_done"])):
                pe.wait_ge(loaded[s], 16 * (DEPTH * uses + 1))
                for m in range(MT):
                    pe.wait_ge(S["ht_ready"], 2 * (m + 1) if s != FV_S else 4)
                    if bank + m == 7:
                        pe.wait_ge(S["params_ready"], 1)
                    tokens(m, B[bank + m][:, :], chunk(s), slice(0, 512)).then_inc(done, 1)
            pe.wait_ge(loaded[LORA_S], 16 * (DEPTH * 2 + 3))
            w = chunk(LORA_S, LORA_W)
            for m in range(MT):
                mm = tokens(m, B[2][:, m * NH:(m + 1) * NH], w, slice(2 * LORA + P, LORA_W))
            mm.then_inc(S["f_done"], 1)
            features(B[3][:, 0:T], w, slice(0, P))
            features(B[3][:, T:], w, slice(P, 2 * P)).then_inc(S["lora_done"], 1)
            pe.wait_ge(S["qkv_copied"], 6)
            for b in range(4):
                if b == 0:
                    pe.wait_ge(loaded[R_S], 16 * (DEPTH * 2 + 1))
                if b == 2:
                    pe.wait_ge(loaded[K_S], 16 * (DEPTH * 2 + 1))
                    pe.wait_ge(S["f_ready"], 1)
                    pe.wait_ge(S["raw_ready"], 1)
                for i in range(2):
                    mm = features(B[b][:, i * T:(i + 1) * T], chunk((R_S, K_S)[b // 2]), slice((2 * b % 4 + i) * P, (2 * b % 4 + i + 1) * P))
                mm.then_inc(S["rkv_done"], 1)
            pe.wait_ge(S["qk_ready"], 1)
            for m in range(MT):
                for j in range(2):
                    for i in range(4):
                        at = j * NH + 2 * i
                        t = nc.tensor.transpose(B[4 + 2 * m + j][:, i * P:(i + 1) * P], qk[:, m, at:at + 2].rearrange("p u d -> p (u d)"), ident)
                t.then_inc(S["qk_transposed"], 1)
            pe.wait_ge(loaded[V_S], 16 * (DEPTH + 2))
            pe.wait_ge(S["raw_ready"], 3)
            for b in range(2):
                for i in range(2):
                    mm = features(B[b][:, i * T:(i + 1) * T], chunk(V_S), slice((2 * b + i) * P, (2 * b + i + 1) * P))
                mm.then_inc(S["rkv_done"], 1)
            pe.wait_ge(S["kk_sq"], 1)
            pe.wait_ge(S["qkt_ready"], 4)
            pe.wait_ge(S["const2_in"], 16)
            for i in range(CT):
                mm = nc.tensor.matmul(B[6 + i // 2][:, i % 2 * T:(i % 2 + 1) * T], const("head_ones"), lc[:, i], start=True, stop=True)
                if i % 2:
                    mm.then_inc(S["kk_sum"], 1)
            pe.wait_ge(S["raw_ready"], 5)
            pe.wait_ge(S["f_ready"], 2)
            upto = const("upto")
            for m in range(MT):
                if m == 1:
                    pe.wait_ge(S["kk_bound"], 2)
                for i in range(4):
                    for u in range(2):
                        h = 2 * i + u
                        out = score_out(m, h)
                        lf = lambda s: shape(f8[:, s * NH + h:s * NH + h + 1], P, P)
                        nc.tensor.matmul(out, lf(0), upto[:, 0:(m + 1) * P], start=True, stop=False)
                        if m:
                            nc.tensor.matmul(out[:, P:T], lf(1), upto[:, 0:P], start=False, stop=False)
                        r = slice(64 * u, 64 * u + 64)
                        mm = nc.tensor.matmul(out, qt[r, i, m * P:(m + 1) * P], kt[r, i, 0:(m + 1) * P], start=False, stop=True)
                mm.then_inc(S["scores"], 1)
            for m in range(MT):
                pe.wait_ge(S["exp_done"], NH * (m + 1))
                if m == 0:
                    pe.wait_ge(S["raw_ready"], 7)
                    pe.wait_ge(S["masked"], 1)
                base = sum(GROUPS[:m])

                def weigh(g):
                    pe.wait_ge(S["pt_ready"], base + g + 1)
                    for b, (h, key) in enumerate(pairs(m, g)):
                        mm = nc.tensor.matmul(B[2 + m][:, h * HD:(h + 1) * HD], pt[:, (base + g) % 4, b], v2[:, key, h * HD:(h + 1) * HD],
                                              start=key == 0, stop=key == m)
                    mm.then_inc(S["weighed"], 1)

                for g in range(GROUPS[m]):
                    if base + g >= 2:
                        pe.wait_ge(S["pt_ready"], base + g - 1)
                    for b, (h, key) in enumerate(pairs(m, g)):
                        t = nc.tensor.transpose(B[(base + g) % 2][:, b * P:(b + 1) * P], prob[m][:, h, key * P:(key + 1) * P], ident)
                    t.then_inc(S["p_transposed"], 1)
                    if g:
                        weigh(g - 1)
                weigh(GROUPS[m] - 1)
            pe.wait_ge(S["masked"], 2)
            for m in range(MT):
                pe.wait_ge(S["yf_ready"], m + 1)
                for k in range(4):
                    t = nc.tensor.transpose(B[4 + m][:, k * P:(k + 1) * P], yf[:, m, k * P:(k + 1) * P], ident)
                t.then_inc(S["yf_transposed"], 1)
            pe.wait_ge(S["lora_in"], 3)
            pe.wait_ge(S["small_in"], 16 * N_SMALL2)
            for g in range(3):
                r = (slice(0, LORA), slice(LORA, P), slice(0, P))[g]
                w = (lora_w, lora_w, g2)[g]
                for i in range(CT):
                    bank = B[(6, 7, 0, 1, 2, 3)[2 * g + i // 2]]
                    mm = nc.tensor.matmul(bank[:, i % 2 * T:(i % 2 + 1) * T], w[r, i * P:(i + 1) * P], ps[r, 12 + (g == 2)], start=True, stop=True)
                    if i % 2:
                        mm.then_inc(S["lora_mul"], 1)
            for j, (src, n) in enumerate(((v_, 0), (ld, 1), (ex, 3), (ei, 4))):
                for m in range(MT):
                    if j == 0:
                        pe.wait_ge(S["lora_tanh"], 8)
                    if j == 1:
                        pe.wait_ge(S["gates_ready"], 2)
                    if j == 2:
                        pe.wait_ge(S["yft_ready"], 2)
                    if n:
                        pe.wait_ge(S["scaled"], n)
                    for i in range(CT):
                        t = nc.tensor.transpose(B[2 * j + m][:, i * P:(i + 1) * P], src[:, i, m * P:(m + 1) * P], ident)
                    t.then_inc(S["tok_transposed"], 1)
            pe.wait_ge(S["tok_ready"], 1)
            for m in range(MT):
                for i in range(CT):
                    at = m * NH + 2 * i
                    mm = nc.tensor.matmul(B[0][:, at:at + 2], rk[:, i, m * P:(m + 1) * P], const("head_pick"), start=True, stop=True)
            mm.then_inc(S["bonus_done"], 1)
            pe.wait_ge(S["tok_ready"], 8)
            pe.wait_ge(S["bonus_ready"], 1)

            def unit(m, u, stage, operands, width=P, rows_out=slice(0, P), transpose=False):
                k = order(m, u, stage)
                if k >= 8:
                    pe.wait_ge(S["unit_taken"], k - 7)
                for i in range(CT):
                    left, right = operands(i)
                    out = B[k % 8][rows_out, i * width:(i + 1) * width]
                    mm = nc.tensor.transpose(out, left, ident) if transpose else nc.tensor.matmul(out, left, right, start=True, stop=True)
                mm.then_inc(S["unit_made"], 1)

            for m in range(MT):
                tile = slice(m * P, (m + 1) * P)
                row = [slice(64 * u, 64 * u + 64) for u in range(2)]
                for u in range(2):
                    unit(m, u, "NT", lambda i: (aa[row[u], i, tile], ld[row[u], i, tile]))
                for u in range(2):
                    unit(m, u, "N", lambda i: (ld[row[u], i, tile], aa[row[u], i, tile]))
                for u in range(2):
                    unit(m, u, "AKT", lambda i: (k_[row[u], i, tile], ld[row[u], i, tile]))
                for u in range(2):
                    unit(m, u, "RBT", lambda i: (aa[row[u], i, tile], r_[row[u], i, tile]))
                for u in range(2):
                    unit(m, u, "RKT", lambda i: (k_[row[u], i, tile], r_[row[u], i, tile]))

                def step(stage, needs, operands, **kw):
                    for u in range(2):
                        pe.wait_ge(S["unit_taken"], max(order(m, u, n) for n in needs) + 1)
                        unit(m, u, stage, lambda i: operands(W[u], u, i), **kw)

                step("P2", ("NT", "N"), lambda w, u, i: (w["NT"][:, i], w["N"][:, i]))
                step("P2T", ("NT", "N"), lambda w, u, i: (w["N"][:, i], w["NT"][:, i]))
                step("MV", ("AKT",), lambda w, u, i: (w["AKT"][:, i], vtok[:, m, (2 * i + u) * HD:(2 * i + u + 1) * HD]), width=HD)
                step("P4", ("P2", "P2T"), lambda w, u, i: (w["P2T"][:, i], w["P2"][:, i]))
                step("P4T", ("P2", "P2T"), lambda w, u, i: (w["P2"][:, i], w["P2T"][:, i]))
                step("F2", ("P2", "NT"), lambda w, u, i: (w["P2"][:, i], w["F"][:, i]))
                step("P8", ("P4", "P4T"), lambda w, u, i: (w["P4T"][:, i], w["P4"][:, i]))
                step("F3", ("P4", "F2"), lambda w, u, i: (w["P4"][:, i], w["F"][:, i]))
                step("F4", ("P8", "F3"), lambda w, u, i: (w["P8"][:, i], w["F"][:, i]))
                step("XD", ("F4",), lambda w, u, i: (w["F"][:, i], None), transpose=True)
                step("Q", ("F4", "N"), lambda w, u, i: (w["NO"][:, i], w["F"][:, i]))
                step("F5", ("XD", "Q"), lambda w, u, i: (w["XD"][:, i], w["Q"][:, i]))
                step("WU", ("F5", "MV"), lambda w, u, i: (w["F"][:, i], am[:, m, 2 * i + u]))
                for u in range(2):
                    unit(m, u, "WT", lambda i: (am[:, m, 2 * i + u, 0:HD], W[u]["F"][:, i]), rows_out=row[u])
            pe.wait_ge(S["unit_taken"], order(MT - 1, 1, "WT") + 1)
            for m in range(MT):
                for i in range(CT):
                    for u in range(2):
                        h = 2 * i + u
                        cols = slice(h * HD, (h + 1) * HD)
                        for product in range(3):
                            for c in range(4):
                                s = slice(CHUNK * c, CHUNK * (c + 1))
                                out = B[4 * m + c][64 * u:64 * u + 64, :]
                                g_out, h_out = out[:, i * HD:(i + 1) * HD], out[:, 256 + i * HD:256 + (i + 1) * HD]
                                if product == 0:
                                    nc.tensor.matmul(g_out, wu[s, m, h, 0:HD], btok[s, m, cols], start=True, stop=True)
                                elif product == 1:
                                    nc.tensor.matmul(h_out, btok[s, m, cols], wu[s, m, h, HD:P], start=True, stop=False)
                                else:
                                    mm = nc.tensor.matmul(h_out, ktok[s, m, cols], vtok[s, m, cols], start=False, stop=True)
                mm.then_inc(S["chunk_made"], 1)
            for q in range(NCH):
                m, c = divmod(q, 4)
                pe.wait_ge(S["chunk_taken"], NCH)
                pe.wait_ge(S["state_ready"], 2 * q + 1)
                for i in range(CT):
                    for u in range(2):
                        r = slice(64 * u, 64 * u + 64)
                        mm = nc.tensor.matmul(B[u][r, i * HD:(i + 1) * HD], chunks[m][r, c, 0, i], state[r, q, i], start=True, stop=True)
                mm.then_inc(S["state_made"], 1)
                for j in range(2):
                    mh, i = divmod(2 * q + j, CT)
                    t, u = divmod(mh, 2)
                    h = 2 * i + u
                    nc.tensor.matmul(y_bank(t, u)[:, i * HD:(i + 1) * HD], rkt[:, t, h], vtok[:, t, h * HD:(h + 1) * HD],
                                     start=i == 0, stop=False, skip_group_check=True)
            pe.wait_ge(S["state_ready"], 2 * NCH - 1)
            for m in range(MT):
                if m == 1:
                    pe.wait_ge(S["state_ready"], 2 * NCH + 1)
                for u in range(2):
                    r = slice(64 * u, 64 * u + 64)
                    for i in range(CT):
                        for c in range(4):
                            mm = nc.tensor.matmul(B[(2, 3, 0, 1)[2 * m + u]][CHUNK * c:CHUNK * (c + 1), i * HD:(i + 1) * HD],
                                                  wt[r, m, i, CHUNK * c:CHUNK * (c + 1)], state[r, 4 * m + c, i], start=True, stop=True)
                    mm.then_inc(S["sa_made"], 1)
            for m in range(MT):
                for u in range(2):
                    bank = y_bank(m, u)
                    pe.wait_ge(S["sa_ready"], 2 * m + u + 1)
                    r = slice(64 * u, 64 * u + 64)
                    for i in range(CT):
                        h = 2 * i + u
                        nc.tensor.matmul(bank[:, i * HD:(i + 1) * HD], rbt[:, m, h], wu[:, m, h, HD:P], start=False, stop=False,
                                         skip_group_check=True)
                    for i in range(CT):
                        for c in range(4):
                            t = slice(m * P + CHUNK * c, m * P + CHUNK * (c + 1))
                            mm = nc.tensor.matmul(bank[CHUNK * c:CHUNK * (c + 1), i * HD:(i + 1) * HD], r_[r, i, t], state[r, 4 * m + c, i],
                                                  start=False, stop=True, skip_group_check=True)
                    mm.then_inc(S["y_made"], 1)
            for h in range(2):
                pe.wait_ge(loaded[WO2_S[h]], 16 * (DEPTH * 2 + 2))
            pe.wait_ge(S["sa_ready"], 4)
            for m in range(MT):
                pe.wait_ge(S["y_ready"], m + 1)
                for k in range(4):
                    at = m * NH + 2 * k
                    t = nc.tensor.transpose(B[2 + m][:, k * P:(k + 1) * P], yr[:, at:at + 2].rearrange("p h d -> p (h d)"), ident)
                t.then_inc(S["y_transposed"], 1)
                pe.wait_ge(S["yrt_ready"], m + 1)
                for h in range(2):
                    w = slot[:, WO2_S[h], :].rearrange("p (k n) -> p k n", k=KC)
                    for k in range(KC):
                        y = (yrt if k < 4 else yft)[:, k % 4, m * P:(m + 1) * P]
                        mm = nc.tensor.matmul(B[(0, 1, 6, 7)[2 * m + h]][:, :], y, w[:, k, :], start=k == 0, stop=k == KC - 1)
                    mm.then_inc(S["out_done"], 1)

        @block.vector
        def _(dve):
            V = nc.vector
            after = Chain(dve, S["dve_step"])
            for m in range(MT):
                V.tensor_scalar(XN[:, m * D:(m + 1) * D], X[:, m * D:(m + 1) * D], rstd[:, m:m + 1], None, ALU.mult).then_inc(S["xn_ready"], 1)
            dve.wait_ge(mem["rows2_in"], 16 * N_ROWS2)
            for m in range(MT):
                for b in range(2):
                    dve.wait_ge(S["h_transposed"], 2 * m + b + 1)
                    V.tensor_tensor(ht[:, 4 * b:4 * b + 4, m * P:(m + 1) * P], view(B[2 * m + b][:, :], 4, P),
                                    shape(norm_g[:, 4 * b:4 * b + 4].unsqueeze(2), P, 4, P), ALU.mult).then_inc(S["ht_ready"], 1)
            dve.wait_ge(S["qkv_copied"], 4)
            flat = qk.rearrange("p m k d -> p (m k) d")
            dve.wait_ge(S["fv_done"], MT)
            dve.wait_ge(S["fk_done"], MT)
            after(V.tensor_tensor(sqk, flat, flat, ALU.mult))
            V.tensor_reduce(ssq, sqk, AX.X, ALU.add).then_inc(S["qk_ss"], 1)
            dve.wait_ge(S["f_done"], 1)
            dve.wait_ge(S["small_in"], 16 * N_SMALL2)
            dve.wait_ge(S["const2_in"], 16)
            V.tensor_tensor(view(wk[:, 2], MT, NH), view(B[2][:, 0:MT * NH], MT, NH), shape(b_f.unsqueeze(1), P, MT, NH), ALU.add)\
                .then_inc(S["f_ready"], 1)
            dve.wait_ge(S["f_ready"], 1)
            after(V.tensor_scalar(wk[:, 7], wk[:, 2], -1.0, 0.0, ALU.mult, ALU.max))
            V.scalar_tensor_tensor(wk[:, 0], wk[:, 7], 2.0, wk[:, 2], ALU.mult, ALU.add).then_inc(S["f_abs"], 1)
            dve.wait_ge(S["f_exp"], 1)
            log1p_of(V, after, wk)
            after(V.scalar_tensor_tensor(wk[:, 6], wk[:, 8], 2.0, wk[:, 7], ALU.mult, ALU.add))
            V.tensor_scalar(f8, wk[:, 6], 8.0, None, ALU.mult).then_inc(S["f_ready"], 1)
            dve.wait_ge(S["qk_rstd"], 1)
            after(V.tensor_tensor(flat, flat, shape(rsq.unsqueeze(2), P, MT * 2 * NH, HD), ALU.mult))
            for m in range(MT):
                g4 = view(qk_flat[:, m * 1024:(m + 1) * 1024], 2, NH, HD)
                ins = V.tensor_tensor(g4, g4, shape(gain.unsqueeze(2), P, 2, NH, HD), ALU.mult)
            ins.then_inc(S["qk_ready"], 1)

            def mask(m):
                dve.wait_ge(S["scores"], m + 1)
                for h in range(NH):
                    ins = V.tensor_tensor_reduce(out=prob[m][:, h], in0=score_out(m, h), in1=const("causal")[:, (1 - m) * P:], scale=1.0,
                                                 scalar=LOWEST, op0=ALU.add, op1=ALU.max, accum_out=rowmax[:, m, h:h + 1])
                after(ins)
                V.tensor_scalar(negmax[:, m], rowmax[:, m], -SCALE, None, ALU.mult).then_inc(S["masked"], 1)

            def shift(tiles, ready):
                dve.wait_ge(S["raw_ready"], ready)
                dve.wait_ge(S["params_ready"], 1)
                after(V.tensor_tensor(ps[:, tiles], raw[:, tiles, 0:T], raw[:, tiles, 1:], ALU.subtract))
                for i in range(tiles.start, tiles.stop):
                    V.scalar_tensor_tensor(ps[:, i], ps[:, i], params[:, ROW_MU + i:ROW_MU + i + 1], raw[:, i, 1:], ALU.mult, ALU.add)\
                        .then_inc(S["shifted"], 1)

            prm = lambda row, i: params[:, row + i:row + i + 1]
            shift(slice(12, 14), 1)
            shift(slice(0, 8), 5)
            dve.wait_ge(S["shifted"], 10)
            for i in range(CT):
                ins = V.tensor_scalar(kk[:, i], k_[:, i], prm(ROW_KK, i), None, ALU.mult)
            after(ins)
            V.tensor_tensor(lc, kk, kk, ALU.mult).then_inc(S["kk_sq"], 1)
            for b in range(2):
                dve.wait_ge(S["kk_sum"], b + 1)
                V.tensor_scalar(lc[:, 2 * b:2 * b + 2], view(B[6 + b][:, :], 2, T), 1e-24, None, ALU.max).then_inc(S["kk_bound"], 1)
            dve.wait_ge(S["qk_transposed"], 2)
            mask(0)
            dve.wait_ge(S["kk_bound"], 2)
            V.reciprocal(lc, lc).then_inc(S["kk_inverse"], 1)
            mask(1)
            shift(slice(8, 12), 7)
            dve.wait_ge(S["lora_in"], 2)
            V.tensor_scalar(ps[:, 13], ps[:, 13], 0.5, 0.5, ALU.mult, ALU.add).then_inc(S["lora_in"], 1)
            for m in range(MT):
                dve.wait_ge(S["weighed"], sum(GROUPS[:m + 1]))
                if m == 0:
                    dve.wait_ge(S["weighed"], sum(GROUPS))
                after(V.reciprocal(rden, den[:, m]))
                V.tensor_tensor(view(yf[:, m], NH, HD), view(B[2 + m][:, :], NH, HD), shape(rden.unsqueeze(2), P, NH, HD), ALU.mult)\
                    .then_inc(S["yf_ready"], 1)
                dve.wait_ge(S["yf_ready"], m + 1)
            dve.wait_ge(S["kk_root"], 1)
            after(V.tensor_tensor(kk, kk, lc, ALU.mult))
            dve.wait_ge(S["lora_tanh"], 8)
            after(V.tensor_scalar(ld, ld, 1.0, -DECAY / 2, ALU.add, ALU.mult))
            after(V.tensor_scalar(aa, aa, 0.5, 0.5, ALU.mult, ALU.add))
            for i in range(CT):
                ins = V.tensor_tensor_scan(lc[:, i], const("restart"), ld[:, i], 0.0, ALU.mult, ALU.add)
            ins.then_inc(S["lc_ready"], 1)
            dve.wait_ge(S["lc_ready"], 1)
            V.tensor_tensor(ld, lc, ld, ALU.subtract).then_inc(S["lc_ready"], 1)
            for i in range(CT):
                ins = V.tensor_scalar(rk[:, i], aa[:, i], 1.0, prm(ROW_KA, i), ALU.subtract, ALU.mult)
            after(ins)
            after(V.scalar_tensor_tensor(k_, rk, 1.0, k_, ALU.add, ALU.mult))
            for i in range(CT):
                ins = V.scalar_tensor_tensor(rk[:, i], r_[:, i], prm(ROW_RK, i), k_[:, i], ALU.mult, ALU.mult)
            after(ins)
            dve.wait_ge(S["decays_ready"], 3)
            V.scalar_tensor_tensor(ld, kk, -1.0, ld, ALU.mult, ALU.mult).then_inc(S["scaled"], 1)
            ends = lambda t: t.rearrange("p i (q s) -> p (i q) s", s=CHUNK)
            V.tensor_copy(last.rearrange("p i q -> p (i q)"), ends(ex)[:, :, CHUNK - 1])
            V.tensor_tensor(aa, aa, kk, ALU.mult)
            V.tensor_tensor(r_, r_, ex, ALU.mult).then_inc(S["scaled"], 1)
            dve.wait_ge(S["scaled"], 2)
            after(V.tensor_tensor(aa, aa, ei, ALU.mult))
            by = shape(last.rearrange("p i q -> p (i q)").unsqueeze(2), P, CT * NCH, CHUNK)
            V.tensor_tensor(ends(ex), ends(aa), by, ALU.mult).then_inc(S["scaled"], 1)
            after(V.tensor_tensor(k_, k_, ei, ALU.mult))
            V.tensor_tensor(ends(ei), ends(k_), by, ALU.mult).then_inc(S["scaled"], 1)

            def take(m, u, stage):
                dve.wait_ge(S["unit_made"], order(m, u, stage) + 1)
                return view(B[order(m, u, stage) % 8][:, :], CT, P)

            def masked_copy(out, bank, name):
                return V.tensor_tensor(out, bank, shape(const(name).unsqueeze(1), P, CT, P), ALU.mult)

            taken = [0]

            def end(ins):
                ins.then_inc(S["unit_taken"], 1)
                taken[0] += 1

            def settle():
                dve.wait_ge(S["unit_taken"], taken[0])

            for m in range(MT):
                for u in range(2):
                    bank = take(m, u, "NT")
                    end(masked_copy(W[u]["NT"], bank, "below_half_t"))
                settle()
                for u in range(2):
                    after(V.tensor_tensor(W[u]["F"], W[u]["NT"], shape(ident.unsqueeze(1), P, CT, P), ALU.add))
                for u in range(2):
                    bank = take(m, u, "N")
                    masked_copy(W[u]["NO"], bank, "across")
                    end(masked_copy(W[u]["N"], bank, "below_half"))
                for u in range(2):
                    end(masked_copy(W[u]["AKT"], take(m, u, "AKT"), "below_t"))
                heads = lambda t, u: t[:, m].rearrange("p (i u) t -> p u i t", u=2)[:, u]
                for name, out in (("RBT", rbt), ("RKT", rkt)):
                    for u in range(2):
                        end(masked_copy(heads(out, u), take(m, u, name), "upto_t"))
                for name in ("P2", "P2T"):
                    for u in range(2):
                        end(V.tensor_copy(W[u][name], take(m, u, name)))
                for u in range(2):
                    bank = B[order(m, u, "MV") % 8]
                    dve.wait_ge(S["unit_made"], order(m, u, "MV") + 1)
                    end(V.tensor_copy(heads(am, u)[:, :, HD:P], view(bank[:, 0:CT * HD], CT, HD)))
                for name in ("P4", "P4T"):
                    for u in range(2):
                        end(V.tensor_copy(W[u][name], take(m, u, name)))

                def add_f(stage):
                    for u in range(2):
                        settle()
                        end(V.tensor_tensor(W[u]["F"], W[u]["F"], take(m, u, stage), ALU.add))

                add_f("F2")
                for u in range(2):
                    end(V.tensor_copy(W[u]["P8"], take(m, u, "P8")))
                add_f("F3")
                add_f("F4")
                for u in range(2):
                    end(V.tensor_copy(W[u]["XD"], take(m, u, "XD")))
                for u in range(2):
                    end(V.tensor_copy(W[u]["Q"], take(m, u, "Q")))
                add_f("F5")
                for u in range(2):
                    end(V.tensor_copy(heads(wu, u), take(m, u, "WU")))
                for u in range(2):
                    r = slice(64 * u, 64 * u + 64)
                    end(V.tensor_copy(wt[r, m], take(m, u, "WT")[r]))
            settle()
            V.memset(state[:, 0], 0.0).then_inc(S["state_ready"], 1)
            dve.wait_ge(S["chunk_taken"], NCH)
            dve.wait_ge(S["state_ready"], 1)
            for q in range(NCH):
                m, c = divmod(q, 4)
                nxt = state[:, q + 1]
                pcq = shape(last[:, :, q:q + 1], P, CT, HD)
                after(V.tensor_tensor(nxt, state[:, q], pcq, ALU.mult))
                after(V.tensor_tensor(nxt, nxt, chunks[m][:, c, 1], ALU.add))
                dve.wait_ge(S["state_made"], q + 1)
                for u in range(2):
                    r = slice(64 * u, 64 * u + 64)
                    V.tensor_tensor(nxt[r], nxt[r], view(B[u][r, 0:CT * HD], CT, HD), ALU.add).then_inc(S["state_ready"], 1)
                dve.wait_ge(S["state_ready"], 2 * q + 3)
            for m in range(MT):
                for u in range(2):
                    dve.wait_ge(S["sa_made"], 2 * m + u + 1)
                    su = wu[:, m].rearrange("p (i u) t -> p u i t", u=2)[:, u, :, HD:P]
                    V.tensor_tensor(su, su, view(B[(2, 3, 0, 1)[2 * m + u]][:, 0:CT * HD], CT, HD), ALU.add).then_inc(S["sa_ready"], 1)
            def take_y(m):
                for u in range(2):
                    dve.wait_ge(S["y_made"], 2 * m + u + 1)
                    V.tensor_copy(yr[:, m * NH:(m + 1) * NH].rearrange("p (i u) d -> p u i d", u=2)[:, u],
                                  view(y_bank(m, u)[:, 0:CT * HD], CT, HD)).then_inc(S["y_taken"], 1)
                dve.wait_ge(S["y_taken"], 2 * m + 2)

            def group_norm(m):
                y, sq, mu = yr[:, m * NH:(m + 1) * NH], view(ysq, MT * NH, HD)[:, m * NH:(m + 1) * NH], of_tile(mean, m)
                wide = lambda t: shape(t.unsqueeze(2), P, NH, HD)
                flat_y = y.rearrange("p h d -> p (h d)")
                after(V.tensor_reduce(mu, y, AX.X, ALU.add))
                after(V.tensor_scalar(mu, mu, 1.0 / HD, None, ALU.mult))
                after(V.tensor_tensor(y, y, wide(mu), ALU.subtract))
                after(V.tensor_tensor(sq, y, y, ALU.mult))
                V.tensor_reduce(of_tile(var, m), sq, AX.X, ALU.add).then_inc(S["y_var"], 1)
                dve.wait_ge(S["bonus_ready"], 1)
                dve.wait_ge(S["y_var"], m + 1)
                after(V.tensor_tensor(sq, view(vtok[:, m], NH, HD), wide(bonus[:, m]), ALU.mult))
                dve.wait_ge(S["y_rstd"], m + 1)
                after(V.tensor_tensor(y, y, wide(of_tile(rvar, m)), ALU.mult))
                after(V.tensor_tensor(flat_y, flat_y, ln_w, ALU.mult))
                after(V.tensor_tensor(flat_y, flat_y, ln_b, ALU.add))
                V.tensor_tensor(y, y, sq, ALU.add).then_inc(S["y_ready"], 1)

            def gate_y(m):
                dve.wait_ge(S["y_transposed"], m + 1)
                V.tensor_tensor(yrt[:, :, m * P:(m + 1) * P], view(B[2 + m][:, :], 4, P), gt[:, :, m * P:(m + 1) * P], ALU.mult)\
                    .then_inc(S["yrt_ready"], 1)

            take_y(0)
            group_norm(0)
            take_y(1)
            gate_y(0)
            group_norm(1)
            gate_y(1)
            for m in range(MT):
                for h in range(2):
                    dve.wait_ge(S["out_done"], 2 * m + h + 1)
                    x = X[:, m * D + h * 512:m * D + (h + 1) * 512]
                    V.tensor_tensor(x, x, B[(0, 1, 6, 7)[2 * m + h]][:, :], ALU.add).then_inc(S["x_added"], 1)

    nc.all_engine_barrier(sems_to_clear=mixer_sems)


def router_memory(mem):
    w = mem["router"]
    return (view(w[:, 0:KC * (NGROUP + NE)], KC, NGROUP + NE), w[:, KC * (NGROUP + NE):],
            mem["region"][:, REGION - D - CONST3:REGION - D], mem["region"][:, REGION - D:])


NBUF = 3


def expert_slots(mem):
    slot, spare = mem["slots"], mem["region"][:, 0:3 * SLOT].rearrange("p (s n) -> p s n", s=3)
    gate, up, down = ((slot[:, x], slot[:, y], spare[:, i]) for i, (x, y) in enumerate(((0, 5), (1, 2), (4, 3))))
    wide = lambda group: [w.rearrange("p (c n) -> p c n", c=KC) for w in group]
    return wide(gate), wide(up), [w.rearrange("p (j n) -> p j n", j=DE // P) for w in down]


def load_first_experts(sp, a, mem, parts):
    buffers = dict(zip(("gate", "up", "down"), expert_slots(mem)))
    for name, e in parts:
        src = a[f"exp_w_{name}_2"][0, e]
        src = src.rearrange("(j p) n -> p j n", p=P) if name == "down" else src.rearrange("(p c) n -> p c n", c=KC)
        sp.dma_start(buffers[name][e], src).then_inc(mem[name + "_in"][e], 16)


EARLY = [("up", 0), ("down", 0), ("gate", 1), ("gate", 0)]
LATE = [("up", 1), ("down", 1), ("gate", 2), ("up", 2), ("down", 2)]


def experts_part(nc, ctx, a, mem, psum, layout, second):
    X, XN, HT = mem["x"], mem["xn"], mem["ht"]
    arrived, release = mem["arrived"], mem["release"]
    slot, B = mem["slots"], psum
    room = carve(mem["region"][:, 3 * SLOT:REGION - D - CONST3])
    w_route, b_route, const3, gain = router_memory(mem)

    def const(name):
        at, w = layout[name]
        return const3[:, at - second:at - second + w] if at >= second else mem["const"][:, at:at + w]

    ident = const("ident")
    rstd = mem["rstd"]
    logit = room(MT, NGROUP + NE)
    top, top_f = room(MT, 8), room(MT, 8)
    best, best_f = room(MT, 8), room(MT, 8)
    neg_top, group_sum, eq_group = room(MT), room(MT), room(MT, NGROUP)
    exp_junk, of_group, chosen = room(MT, NGROUP), room(MT, EPG, NGROUP), room(MT, EPG)
    gap, first_gate, second_gate = room(MT), room(MT), room(MT)
    ids = room(MT, 2)
    pick, member, gate_of, place = room(MT, 2, NE), room(MT, NE), room(MT, NE), room(MT, NE)
    fullest, over = room(1), room(T // BLK)
    sel, sel_gate = [room(MT, BLK) for _ in range(NBUF)], room(MT, P)
    xt = [room(KC, BLK) for _ in range(NBUF)]
    sgt = [room(MT, P) for _ in range(NBUF)]
    th, hid, hidt = room(P), room(P), room(P)
    y = room(4, 256)
    ht = view(HT[:, :], KC, T)
    xn = view(XN[:, :], MT, P, KC)
    index = ctx.enter_context(nc.sbuf_tensor("router_index", [P, 2 * MT * 8], U32))
    passes = ctx.enter_context(nc.sbuf_tensor("pass_count", [1, 2], I32))

    S, _ = semaphores(nc, ctx, """xn_ready h_transposed ht_ready routed gap_ready group_ready
        gates_exp member_ready ranked passes_ready y_zero acc_ready dve_step scored stored""".split(), "_3")
    Q, pass_sems = semaphores(nc, ctx, """sel_ready gathered xt_ready
        sgt_ready gate_done gate_tanh up_done hid_half hid_ready hid_transposed hidt_ready down_done y_ready combined
        pass_step""".split(), "_e")
    gate_in, up_in, down_in = mem["gate_in"], mem["up_in"], mem["down_in"]
    w_gate, w_up, w_down = expert_slots(mem)
    ROUNDS = (NE - 1 - NBUF) // NBUF
    assert NE == 1 + NBUF * ROUNDS + 3

    def arrive(eng, name):
        eng.drain().then_inc(arrived, 1)
        eng.wait_ge(release[name], 1)
        eng.sem_clear(release[name])

    with nc.Block() as block:

        @block.sync
        def _(sp):
            def into(e, name):
                return a[name][0, e:e + 1] if isinstance(e, int) else a[name][0, bass.ds(e, 1)]

            def load_hidden(e, used, b):
                sp.wait_ge(Q["gate_done"], used)
                sp.dma_start(w_gate[b], into(e, "exp_w_gate_2").rearrange("a (p c) n -> p (a c) n", c=KC)).then_inc(gate_in[b], 16)
                sp.wait_ge(Q["up_done"], used)
                sp.dma_start(w_up[b], into(e, "exp_w_up_2").rearrange("a (p c) n -> p (a c) n", c=KC)).then_inc(up_in[b], 16)

            def load_down(e, used, b):
                sp.wait_ge(Q["down_done"], used)
                sp.dma_start(w_down[b], into(e, "exp_w_down_2").rearrange("a (j p) n -> p (a j) n", p=P)).then_inc(down_in[b], 16)

            def rest_of_pass():
                load_hidden(3, 1, 0)
                with sp.Fori(0, ROUNDS) as k:
                    for i in range(NBUF):
                        load_hidden(k * NBUF + 4 + i, k * NBUF + 2 + i, (4 + i) % NBUF)
                        load_down(k * NBUF + 3 + i, k * NBUF + 1 + i, (3 + i) % NBUF)
                load_down(NE - 1, NE - NBUF, (NE - 1) % NBUF)
                arrive(sp, "sp")

            load_first_experts(sp, a, mem, LATE[2:])
            rest_of_pass()
            sp.wait_ge(S["passes_ready"], 1)
            n = sp.value_load(passes[0:1, 0:1], min_val=1, max_val=T // BLK)
            with sp.If(n > 1):
                with sp.Fori(1, n):
                    load_first_experts(sp, a, mem, EARLY + LATE)
                    rest_of_pass()
            for m in range(MT):
                sp.wait_ge(S["routed"], m + 1)
                sp.dma_start(a["out"][0, m * P:(m + 1) * P], X[:, m * D:(m + 1) * D]).then_inc(S["stored"], 16)
            sp.wait_ge(S["stored"], 16 * MT)

        @block.scalar
        def _(act):
            for m in range(MT):
                for b in range(2):
                    act.wait_ge(S["h_transposed"], 2 * m + b + 1)
                    nc.scalar.copy(ht[:, 4 * b:4 * b + 4, m * P:(m + 1) * P], view(B[2 * m + b][:, :], 4, P)).then_inc(S["ht_ready"], 1)
            act.wait_ge(S["y_zero"], 1)
            act.wait_ge(S["ht_ready"], 2 * MT)
            for j in range(4):
                nc.scalar.copy(B[j][:, :], y.rearrange("p j n -> p (j n)")[:, 0:512]).then_inc(S["acc_ready"], 1)
            act.wait_ge(S["gap_ready"], 1)
            for m in range(MT):
                nc.scalar.activation(exp_junk[:, m], logit[:, m, 0:NGROUP], ACT.Exp, bias=neg_top[:, m:m + 1],
                                     accum_out=group_sum[:, m:m + 1]).then_inc(S["group_ready"], 1)
            act.wait_ge(S["gap_ready"], 2)
            nc.scalar.activation(second_gate, gap, ACT.Exp).then_inc(S["gates_exp"], 1)

            def copies(e, b, tail, follow):
                if tail:
                    act.wait_ge(Q["hid_transposed"], e)
                    nc.scalar.copy(hidt, B[7][:, 256:256 + P]).then_inc(Q["hidt_ready"], 1)
                    act.wait_ge(Q["down_done"], e)
                    for j in range(4):
                        r = slice(BLK * j, BLK * (j + 1))
                        nc.scalar.copy(y[r, j], B[7][r, 0:256]).then_inc(Q["y_ready"], 1)
                if follow:
                    act.wait_ge(Q["gathered"], e + 2)
                    nc.scalar.copy(xt[(b + 1) % NBUF].rearrange("p c s -> p (c s)"), B[6][:, 0:256]).then_inc(Q["xt_ready"], 1)
                    if tail:
                        act.wait_ge(Q["combined"], e)
                    nc.scalar.copy(sgt[(b + 1) % NBUF].rearrange("p m t -> p (m t)"), B[6][:, 256:]).then_inc(Q["sgt_ready"], 1)

            def step(e, b, tail=True, follow=True):
                act.wait_ge(Q["gate_done"], e + 1)
                nc.scalar.activation(th, B[4][:, 0:P], ACT.Tanh, scale=0.5).then_inc(Q["gate_tanh"], 1)
                copies(e, b, tail, follow)

            act.wait_ge(S["passes_ready"], 1)
            n = act.value_load(passes[0:1, 0:1], min_val=1, max_val=T // BLK)
            with act.Fori(0, n):
                copies(-1, NBUF - 1, False, True)
                step(0, 0, tail=False)
                with act.Fori(0, ROUNDS) as k:
                    for b in (1, 2, 0):
                        step(k * NBUF + (b or NBUF), b)
                for e in range(NE - 3, NE):
                    step(e, e % NBUF, follow=e < NE - 1)
                copies(NE, NE % NBUF, True, False)
                arrive(act, "act")

        @block.tensor
        def _(pe):
            for m in range(MT):
                pe.wait_ge(S["xn_ready"], m + 1)
                for c in range(KC):
                    t = nc.tensor.transpose(B[2 * m + c // 4][:, c % 4 * P:(c % 4 + 1) * P], xn[:, m, :, c], ident)
                    if c % 4 == 3:
                        t.then_inc(S["h_transposed"], 1)
            for m in range(MT):
                pe.wait_ge(S["ht_ready"], 2 * m + 2)
                pe.wait_ge(mem["router_in"], 16 * 6)
                for c in range(KC):
                    mm = nc.tensor.matmul(B[4][:, m * 72:(m + 1) * 72], ht[:, c, m * P:(m + 1) * P], w_route[:, c], start=c == 0, stop=c == KC - 1)
            mm.then_inc(S["scored"], 1)
            pe.wait_ge(S["member_ready"], 1)
            nc.tensor.matmul(B[5][:, 0:NE], const("before"), member[:, 0], start=True, stop=True)
            nc.tensor.matmul(B[5][:, NE:2 * NE], const("before"), member[:, 1], start=True, stop=False)
            nc.tensor.matmul(B[5][:, NE:2 * NE], const("ones"), member[:, 0], start=False, stop=True)
            nc.tensor.matmul(B[5][:, 2 * NE:3 * NE], const("ones"), member[:, 0], start=True, stop=False)
            nc.tensor.matmul(B[5][:, 2 * NE:3 * NE], const("ones"), member[:, 1], start=False, stop=True).then_inc(S["ranked"], 1)

            def gather(e, u, first):
                pe.wait_ge(Q["sel_ready"], e + 1)
                if not first:
                    pe.wait_ge(Q["sgt_ready"], e)
                for c in range(KC):
                    for m in range(MT):
                        nc.tensor.matmul(B[6][:, c * BLK:(c + 1) * BLK], xn[:, m, :, c], sel[u][:, m], start=m == 0, stop=m == MT - 1)
                for m in range(MT):
                    t = nc.tensor.transpose(B[6][:, 256 + m * P:256 + (m + 1) * P], sel_gate[:, m], ident)
                t.then_inc(Q["gathered"], 1)

            def into_hidden(u, bank, w, done):
                for c in range(KC):
                    for j in range(4):
                        mm = nc.tensor.matmul(B[bank][BLK * j:BLK * (j + 1), 0:P], xt[u][:, c], w[u][:, c, j * P:(j + 1) * P],
                                              start=c == 0, stop=c == KC - 1, tile_position=(0, BLK * j))
                mm.then_inc(done, 1)

            def turn(e):
                pe.wait_ge(Q["hid_ready"], e + 1)
                nc.tensor.transpose(B[7][:, 256:256 + P], hid, ident).then_inc(Q["hid_transposed"], 1)

            def down(e, u, use):
                pe.wait_ge(Q["hidt_ready"], e + 1)
                pe.wait_ge(down_in[u], use * 16)
                for k in range(4):
                    for j in range(4):
                        mm = nc.tensor.matmul(B[7][BLK * j:BLK * (j + 1), 0:256], hidt[:, BLK * k:BLK * (k + 1)], w_down[u][:, k, j * 256:(j + 1) * 256],
                                              start=k == 0, stop=k == 3, tile_position=(0, BLK * j))
                mm.then_inc(Q["down_done"], 1)

            def combine(e, u):
                for j in range(4):
                    pe.wait_ge(Q["y_ready"], e * 4 + j + 1)
                    for m in range(MT):
                        mm = nc.tensor.matmul(B[j][:, m * 256:(m + 1) * 256], sgt[u][:, m], y[:, j], start=False, stop=True,
                                              skip_group_check=True)
                mm.then_inc(Q["combined"], 1)

            def step(e, b, use, last_use, tail=True, follow=True):
                before, behind = (b + NBUF - 1) % NBUF, (b + 1) % NBUF
                pe.wait_ge(gate_in[b], use * 16)
                pe.wait_ge(Q["xt_ready"], e + 1)
                if tail:
                    pe.wait_ge(Q["hid_ready"], e)
                into_hidden(b, 4, w_gate, Q["gate_done"])
                if tail:
                    turn(e - 1)
                pe.wait_ge(up_in[b], use * 16)
                into_hidden(b, 5, w_up, Q["up_done"])
                if tail:
                    down(e - 1, before, last_use)
                if follow:
                    gather(e + 1, behind, False)
                if tail:
                    combine(e - 1, before)

            pe.wait_ge(S["passes_ready"], 1)
            n = pe.value_load(passes[0:1, 0:1], min_val=1, max_val=T // BLK)
            pe.wait_ge(S["acc_ready"], 4)
            with pe.Fori(0, n):
                gather(0, 0, True)
                step(0, 0, 1, 0, tail=False)
                with pe.Fori(0, ROUNDS) as k:
                    step(k * NBUF + 1, 1, k + 1, k + 1)
                    step(k * NBUF + 2, 2, k + 1, k + 1)
                    step(k * NBUF + 3, 0, k + 2, k + 1)
                for e in range(NE - 3, NE):
                    step(e, e % NBUF, e // NBUF + 1, (e - 1) // NBUF + 1, follow=e < NE - 1)
                turn(NE - 1)
                down(NE - 1, (NE - 1) % NBUF, (NE - 1) // NBUF + 1)
                combine(NE - 1, (NE - 1) % NBUF)
                arrive(pe, "pe")

        @block.vector
        def _(dve):
            V = nc.vector
            after = Chain(dve, S["dve_step"])
            V.memset(y, 0.0).then_inc(S["y_zero"], 1)
            dve.wait_ge(mem["router_in"], 16 * 6)
            for m in range(MT):
                tile = slice(m * D, (m + 1) * D)
                V.scalar_tensor_tensor(XN[:, tile], X[:, tile], rstd[:, m:m + 1], gain, ALU.mult, ALU.mult).then_inc(S["xn_ready"], 1)
            dve.wait_ge(S["scored"], 1)
            after(V.tensor_tensor(logit, view(B[4][:, 0:MT * 72], MT, 72), shape(b_route.unsqueeze(1), P, MT, 72), ALU.add))
            for m in range(MT):
                ins = V.max(top[:, m], logit[:, m, 0:NGROUP])
            after(ins)
            for m in range(MT):
                ins = V.max_index(index[:, m * 8:m * 8 + 8], top[:, m], logit[:, m, 0:NGROUP])
            after(ins)
            V.tensor_scalar(neg_top, top[:, :, 0], -1.0, None, ALU.mult).then_inc(S["gap_ready"], 1)
            after(V.tensor_copy(top_f.rearrange("p m k -> p (m k)"), index[:, 0:MT * 8]))
            iota = const("iota")
            for m in range(MT):
                ins = V.tensor_scalar(eq_group[:, m], iota[:, 0:NGROUP], top_f[:, m, 0:1], None, ALU.is_equal)
            after(ins)
            for m in range(MT):
                ins = V.tensor_tensor(of_group[:, m], logit[:, m, NGROUP:].rearrange("p (g j) -> p j g", g=NGROUP),
                                      shape(eq_group[:, m:m + 1], P, EPG, NGROUP), ALU.mult)
            after(ins)
            after(V.tensor_reduce(chosen, of_group, AX.X, ALU.add))
            for m in range(MT):
                ins = V.max(best[:, m], chosen[:, m])
            after(ins)
            for m in range(MT):
                ins = V.max_index(index[:, (MT + m) * 8:(MT + m) * 8 + 8], best[:, m], chosen[:, m])
            after(ins)
            V.tensor_tensor(gap, best[:, :, 1], best[:, :, 0], ALU.subtract).then_inc(S["gap_ready"], 1)
            after(V.tensor_copy(best_f.rearrange("p m k -> p (m k)"), index[:, MT * 8:]))
            after(V.scalar_tensor_tensor(ids, shape(top_f[:, :, 0:1], P, MT, 2), float(EPG), best_f[:, :, 0:2], ALU.mult, ALU.add))
            for m in range(MT):
                for k in range(2):
                    ins = V.tensor_scalar(pick[:, m, k], iota[:, 0:NE], ids[:, m, k:k + 1], None, ALU.is_equal)
            after(ins)
            V.tensor_tensor(member, pick[:, :, 0], pick[:, :, 1], ALU.add).then_inc(S["member_ready"], 1)
            dve.wait_ge(S["group_ready"], MT)
            dve.wait_ge(S["gates_exp"], 1)
            after(V.tensor_scalar(first_gate, second_gate, 1.0, None, ALU.add))
            after(V.tensor_tensor(first_gate, first_gate, group_sum, ALU.mult))
            after(V.reciprocal(first_gate, first_gate))
            after(V.tensor_scalar(first_gate, first_gate, 0.5, None, ALU.mult))
            after(V.tensor_tensor(second_gate, second_gate, first_gate, ALU.mult))
            for m in range(MT):
                ins = V.tensor_scalar(gate_of[:, m], pick[:, m, 0], first_gate[:, m:m + 1], None, ALU.mult)
            after(ins)
            for m in range(MT):
                ins = V.scalar_tensor_tensor(gate_of[:, m], pick[:, m, 1], second_gate[:, m:m + 1], gate_of[:, m], ALU.mult, ALU.add)
            after(ins)
            dve.wait_ge(S["ranked"], 1)
            ranks = view(B[5][:, 0:MT * NE], MT, NE)
            V.tensor_reduce(fullest, B[5][:, 2 * NE:3 * NE], AX.X, ALU.max)
            after(V.scalar_tensor_tensor(place, ranks, 1.0, member, ALU.add, ALU.mult))
            after(V.tensor_scalar(place, place, -1.0, None, ALU.add))
            after(V.tensor_scalar(over, iota[:, 0:T // BLK], float(BLK), fullest, ALU.mult, ALU.is_lt))
            after(V.tensor_reduce(fullest, over, AX.X, ALU.add))
            after(V.tensor_scalar(passes[:, 0:1], fullest[0:1], 1.0, None, ALU.mult))
            V.tensor_scalar(passes[:, 1:2], fullest[0:1], -1.0, None, ALU.add).then_inc(S["passes_ready"], 1)

            def select(e, u, first=False):
                if not first:
                    dve.wait_ge(Q["gathered"], e)
                for m in range(MT):
                    p = place[:, m, e:e + 1] if isinstance(e, int) else place[:, m, bass.ds(e, 1)]
                    g = gate_of[:, m, e:e + 1] if isinstance(e, int) else gate_of[:, m, bass.ds(e, 1)]
                    V.tensor_scalar(sel[u][:, m], const("slot_of")[:, 0:BLK], p, None, ALU.is_equal)
                    ins = V.tensor_scalar(sel_gate[:, m], const("slot_of"), p, g, ALU.is_equal, ALU.mult)
                ins.then_inc(Q["sel_ready"], 1)

            def step(e, b, follow=True):
                if follow:
                    select(e + 1, (b + 1) % NBUF)
                dve.wait_ge(Q["gate_tanh"], e + 1)
                V.scalar_tensor_tensor(th, th, 1.0, B[4][:, 0:P], ALU.add, ALU.mult).then_inc(Q["hid_half"], 1)
                dve.wait_ge(Q["hid_half"], e + 1)
                dve.wait_ge(Q["up_done"], e + 1)
                V.tensor_tensor(hid, th, B[5][:, 0:P], ALU.mult).then_inc(Q["hid_ready"], 1)

            dve.wait_ge(S["passes_ready"], 1)
            n = dve.value_load(passes[0:1, 0:1], min_val=1, max_val=T // BLK)
            with dve.Fori(0, n):
                select(0, 0, True)
                step(0, 0)
                with dve.Fori(0, ROUNDS) as k:
                    for b in (1, 2, 0):
                        step(k * NBUF + (b or NBUF), b)
                for e in range(NE - 3, NE):
                    step(e, e % NBUF, follow=e < NE - 1)
                V.tensor_scalar(place, place, float(-BLK), None, ALU.add).then_inc(Q["pass_step"], 1)
                dve.wait_ge(Q["pass_step"], 1)
                dve.drain()
                dve.wait_ge(arrived, 3)
                dve.sem_clear(pass_sems)
                for weights in gate_in + up_in + down_in:
                    dve.sem_clear(weights)
                dve.sem_clear(arrived)
                for name in ("sp", "act", "pe"):
                    dve.sem_inc(release[name], 1)
            for m in range(MT):
                for j in range(4):
                    x = X[:, m * D + j * 256:m * D + (j + 1) * 256]
                    ins = V.tensor_tensor(x, x, B[j][:, m * 256:(m + 1) * 256], ALU.add)
                ins.then_inc(S["routed"], 1)


def program(nc, a, layout, ends):
    first, second = ends
    ctx = ExitStack()
    with ctx:
        def sbuf(name, width):
            return ctx.enter_context(nc.sbuf_tensor(name, [P, width], F32))

        def sem(name):
            return ctx.enter_context(nc.semaphore(name))

        mem = {
            "slots": sbuf("weight_slots", NSLOT * SLOT)[:, :].rearrange("p (s n) -> p s n", s=NSLOT),
            "x": sbuf("tokens", MT * D),
            "xn": sbuf("normed_tokens", MT * D),
            "ht": sbuf("normed_features", KC * T),
            "const": sbuf("const_rows", first),
            "region": sbuf("work_region", REGION)[:, :],
            "router": sbuf("router_weights", (KC + 1) * (NGROUP + NE))[:, :],
            "rows2": sbuf("mixer_param_rows", P)[:, :],
            "norm_g2": sbuf("mixer_norm_gain", KC)[:, :],
            "square_sum": sbuf("token_square_sums", MT)[:, :],
            "rstd": sbuf("token_rstd", MT)[:, :],
            "loaded": [sem(f"slot{i}_loaded") for i in range(NSLOT)],
            "w1_loaded": [sem("w1_k_loaded"), sem("w1_v_loaded")],
            "gate_in": [sem(f"gate_in_{b}") for b in range(NBUF)],
            "up_in": [sem(f"up_in_{b}") for b in range(NBUF)],
            "down_in": [sem(f"down_in_{b}") for b in range(NBUF)],
            "arrived": sem("engines_arrived"),
            "release": {n: sem(f"{n}_released") for n in ("sp", "pool", "act", "pe")},
        }
        for n in ("x_in", "const_in", "rows_in", "norm_in", "small_in", "br_loaded", "rows2_in", "router_in", "zeroed",
                  "rows_transposed", "both_ready", "first_ss", "first_step", "first_rstd"):
            mem[n] = sem(n)

        def const(name):
            at, w = layout[name]
            return mem["const"][:, at:at + w]

        banks = [ctx.enter_context(nc.psum_tensor(f"bank{i}", [P, 512], F32)) for i in range(8)]
        with ExitStack() as own:
            layers_part(nc, own, a, mem, banks, const)
        with ExitStack() as own:
            mixer_part(nc, own, a, mem, banks, layout, first, second)
        with ExitStack() as own:
            experts_part(nc, own, a, mem, banks, layout, second)


_INS = """x norm_g w_in conv_w conv_b rg_wr rg_br rg_wi rg_bi rg_lambda q_norm_g k_norm_g cmp_pe_k cmp_w1_k cmp_w2_k
    cmp_pe_v cmp_w1_v cmp_w2_v w_out norm_mix_w_2 w_in_2 mu_shift_2 rw_w0_2 rw_w2_2 rw_a0_2 rw_a2_2 rw_g2_2 rw_k_k_2
    rw_k_a_2 rw_r_k_2 rw_ln_w_2 rw_ln_b_2 fox_b_f_2 fox_q_norm_w_2 fox_k_norm_w_2 w_out_2 norm_ffn_w_2
    router_group_w_2 router_group_b_2 router_expert_w_2 router_expert_b_2 exp_w_gate_2 exp_w_up_2 exp_w_down_2""".split()


def kernel(**inputs):
    import concourse.bacc as bacc
    from concourse.bass_utils import run_bass_kernel_spmd as run

    nc = bacc.Bacc("TRN2", target_bir_lowering=False, num_devices=1)
    table, layout, ends = constants()
    arrays, a = {}, {}
    for name in _INS + ["constants"]:
        value = table if name == "constants" else np.ascontiguousarray(inputs[name])
        arrays[f"in_{name}_dram"] = value
        a[name] = nc.dram_tensor(f"in_{name}_dram", value.shape, mybir.dt.from_np(value.dtype), kind="ExternalInput").ap()
    a["out"] = nc.dram_tensor("out_dram", (1, T, D), F32, kind="ExternalOutput").ap()
    program(nc, a, layout, ends)
    return run(nc, [arrays], core_ids=[0]).results[0]["out_dram"]
```
